# Optimizing a Trainium2 kernel written in Bass

```python
import jax, jax.numpy as jnp
from jax import lax
import numpy as np

D_MODEL = 1024
BATCH = 1
SEQ = 1024
DEPTH = 1
DEC_BATCH = 1
DEC_SEQ = 64
PAST_LEN = 1024

CHUNK = 64
QUERY_BLOCK = 128
MIX_WIDTH = D_MODEL
RET_HEADS = 4
RET_HEAD_DIM = MIX_WIDTH // 2 // RET_HEADS
RET_WIDTH = RET_HEADS * RET_HEAD_DIM
RET_ROPE_THETA = 10000.0
ATT_HEADS = 8
ATT_HEAD_DIM = (MIX_WIDTH - RET_WIDTH) // ATT_HEADS
ATT_WIDTH = ATT_HEADS * ATT_HEAD_DIM
ATT_KV_HEADS = 2
ATT_ROT_DIM = ATT_HEAD_DIM // 4
ATT_ROPE_THETA = 500000.0
IDX_HEADS = 8
IDX_DIM = 64
IDX_ROT_DIM = IDX_DIM // 4
MAX_TOPK = 256
NORM_EPS = 1e-6
SPLIT_SIZES = (RET_WIDTH, RET_WIDTH, RET_WIDTH, RET_WIDTH,
               ATT_WIDTH, ATT_KV_HEADS * ATT_HEAD_DIM, ATT_KV_HEADS * ATT_HEAD_DIM, ATT_WIDTH,
               IDX_HEADS * IDX_DIM, IDX_DIM, IDX_HEADS)
D_IN = sum(SPLIT_SIZES)
SPLIT_POINTS = tuple(sum(SPLIT_SIZES[:i + 1]) for i in range(len(SPLIT_SIZES) - 1))

kernel_name = "hybrid_retention_dsa_stream_step"

def rmsnorm(x, g):
    xf = x.astype(jnp.float32)
    r = lax.rsqrt(jnp.mean(xf * xf, axis=-1, keepdims=True) + NORM_EPS)
    return (xf * r).astype(x.dtype) * g

def rope(x, pos, rot_dim, theta):
    half = rot_dim // 2
    inv = jnp.power(theta, -jnp.arange(half, dtype=jnp.float32) / half)
    ang = pos.astype(jnp.float32)[:, None] * inv[None, :]
    cos = jnp.cos(ang)[None, :, None, :].astype(x.dtype)
    sin = jnp.sin(ang)[None, :, None, :].astype(x.dtype)
    x1 = x[..., :half]
    x2 = x[..., half:rot_dim]
    return jnp.concatenate([x1 * cos - x2 * sin, x2 * cos + x1 * sin, x[..., rot_dim:]], axis=-1)

def retention(q, k, v, s0):
    b, t, h, dk = q.shape
    dv = v.shape[-1]
    c = min(t, CHUNK)
    nc = t // c
    log_gamma = jnp.log1p(-jnp.exp2(-5.0 - jnp.arange(h, dtype=jnp.float32)))
    n = jnp.arange(c, dtype=jnp.float32)
    intra = jnp.exp(log_gamma[:, None, None] * jnp.abs(n[:, None] - n[None, :])).astype(q.dtype)
    to_end = jnp.exp(log_gamma[None, :] * (c - 1.0 - n)[:, None]).astype(q.dtype)
    from_start = jnp.exp(log_gamma[None, :] * (n + 1.0)[:, None]).astype(q.dtype)
    chunk_decay = jnp.exp(log_gamma * c)
    qc = q.reshape(b, nc, c, h, dk)
    kc = k.reshape(b, nc, c, h, dk)
    vc = v.reshape(b, nc, c, h, dv)
    scores = jnp.einsum('bcnhd,bcmhd->bchnm', qc, kc) * intra
    out = jnp.einsum('bchnm,bcmhe->bcnhe', scores, vc)
    kv = jnp.einsum('bcmhd,bcmhe->cbhde', kc * to_end[:, :, None], vc).astype(jnp.float32)

    def step(s, kv_c):
        return s * chunk_decay[None, :, None, None] + kv_c, s

    s_final, s_prev = lax.scan(step, s0.astype(jnp.float32), kv)
    out = out + jnp.einsum('bcnhd,cbhde->bcnhe', qc * from_start[:, :, None], s_prev.astype(q.dtype))
    return out.reshape(b, t, h, dv), s_final.astype(q.dtype)

def dsa_attend(q, qi, wi, qpos, k, v, ki, kpos, topk):
    b, nq, _, hd = q.shape
    logits = jax.nn.relu(jnp.einsum('bqhd,bld->bqhl', qi, ki))
    index = jnp.einsum('bqhl,bqh->bql', logits, wi).astype(jnp.float32)
    admissible = (kpos // CHUNK)[None, :] <= (qpos // CHUNK)[:, None]
    index = jnp.where(admissible[None], index, -jnp.inf)
    top_val, sel = lax.top_k(index, topk)
    valid = jnp.isfinite(top_val)
    gather = jax.vmap(lambda rows, idx: rows[idx])
    kg = gather(k, sel)
    vg = gather(v, sel)
    qg = q.reshape(b, nq, ATT_KV_HEADS, ATT_HEADS // ATT_KV_HEADS, hd)
    s = jnp.einsum('bqkgd,bqnkd->bqkgn', qg, kg).astype(jnp.float32) * (hd ** -0.5)
    s = jnp.where(valid[:, :, None, None, :], s, -jnp.inf)
    p = jax.nn.softmax(s, axis=-1).astype(v.dtype)
    o = jnp.einsum('bqkgn,bqnkd->bqkgd', p, vg)
    return o.reshape(b, nq, ATT_WIDTH)

def mixer_layer(x, pos, ret_state, past_k, past_v, past_ki, norm_g, w_in, ret_gn_g, w_out):
    b, t, _ = x.shape
    h = rmsnorm(x, norm_g)
    proj = jnp.einsum('btd,de->bte', h, w_in)
    rq, rk, rv, rg, aq, ak, av, ag, iq, ik, iw = jnp.split(proj, SPLIT_POINTS, axis=-1)

    rq = rope(rq.reshape(b, t, RET_HEADS, RET_HEAD_DIM), pos, RET_HEAD_DIM, RET_ROPE_THETA)
    rk = rope(rk.reshape(b, t, RET_HEADS, RET_HEAD_DIM), pos, RET_HEAD_DIM, RET_ROPE_THETA) * (RET_HEAD_DIM ** -0.5)
    rv = rv.reshape(b, t, RET_HEADS, RET_HEAD_DIM)
    ro, new_ret = retention(rq, rk, rv, ret_state)
    ro = rmsnorm(ro, ret_gn_g.reshape(RET_HEADS, RET_HEAD_DIM)).reshape(b, t, RET_WIDTH) * jax.nn.silu(rg)

    aq = rope(aq.reshape(b, t, ATT_HEADS, ATT_HEAD_DIM), pos, ATT_ROT_DIM, ATT_ROPE_THETA)
    ak = rope(ak.reshape(b, t, ATT_KV_HEADS, ATT_HEAD_DIM), pos, ATT_ROT_DIM, ATT_ROPE_THETA)
    av = av.reshape(b, t, ATT_KV_HEADS, ATT_HEAD_DIM)
    iq = rope(iq.reshape(b, t, IDX_HEADS, IDX_DIM), pos, IDX_ROT_DIM, ATT_ROPE_THETA)
    ik = rope(ik.reshape(b, t, 1, IDX_DIM), pos, IDX_ROT_DIM, ATT_ROPE_THETA)[:, :, 0]
    iw = iw * (IDX_HEADS ** -0.5 * IDX_DIM ** -0.5)

    if past_k is None:
        n_keys = t
        topk = min(MAX_TOPK, n_keys // 4)
        nb = t // QUERY_BLOCK

        def blocks(a):
            return a.reshape((b, nb, QUERY_BLOCK) + a.shape[2:]).swapaxes(0, 1)

        def attend_block(args):
            qb, qib, wib, posb = args
            return dsa_attend(qb, qib, wib, posb, ak, av, ik, pos, topk)

        ao = lax.map(attend_block, (blocks(aq), blocks(iq), blocks(iw), pos.reshape(nb, QUERY_BLOCK)))
        ao = ao.swapaxes(0, 1).reshape(b, t, ATT_WIDTH)
    else:
        n_keys = past_k.shape[1] + t
        topk = min(MAX_TOPK, n_keys // 4)
        k_all = jnp.concatenate([past_k, ak], axis=1)
        v_all = jnp.concatenate([past_v, av], axis=1)
        ki_all = jnp.concatenate([past_ki, ik], axis=1)
        kpos = jnp.arange(n_keys, dtype=jnp.int32)
        ao = dsa_attend(aq, iq, iw, pos, k_all, v_all, ki_all, kpos, topk)
    ao = ao * jax.nn.silu(ag)

    mix = jnp.einsum('bte,ed->btd', jnp.concatenate([ro, ao], axis=-1), w_out)
    return x + mix, new_ret, ak, av, ik

def setup_inputs(seed: int = 0) -> dict:
    key = jax.random.key(seed)
    ks = jax.random.split(key, 11)
    f32 = jnp.float32
    return {
        'x_prompt': jax.random.normal(ks[0], (BATCH, SEQ, D_MODEL), f32),
        'x_sample': jax.random.normal(ks[1], (DEC_BATCH, DEC_SEQ, D_MODEL), f32),
        'state_ret': 0.05 * jax.random.normal(ks[2], (DEPTH, DEC_BATCH, RET_HEADS, RET_HEAD_DIM, RET_HEAD_DIM), f32),
        'cache_k': jax.random.normal(ks[3], (DEPTH, DEC_BATCH, PAST_LEN, ATT_KV_HEADS, ATT_HEAD_DIM), f32),
        'cache_v': jax.random.normal(ks[4], (DEPTH, DEC_BATCH, PAST_LEN, ATT_KV_HEADS, ATT_HEAD_DIM), f32),
        'cache_kidx': jax.random.normal(ks[5], (DEPTH, DEC_BATCH, PAST_LEN, IDX_DIM), f32),
        'norm_g': 1.0 + 0.05 * jax.random.normal(ks[6], (DEPTH, D_MODEL), f32),
        'w_in': jax.random.normal(ks[7], (DEPTH, D_MODEL, D_IN), f32) * (D_MODEL ** -0.5),
        'ret_gn_g': 1.0 + 0.05 * jax.random.normal(ks[8], (DEPTH, RET_WIDTH), f32),
        'w_out': jax.random.normal(ks[9], (DEPTH, MIX_WIDTH, D_MODEL), f32) * (MIX_WIDTH ** -0.5),
        'final_g': 1.0 + 0.05 * jax.random.normal(ks[10], (D_MODEL,), f32),
    }

def reference(x_prompt, x_sample, state_ret, cache_k, cache_v, cache_kidx, norm_g, w_in, ret_gn_g, w_out, final_g):
    pos_p = jnp.arange(x_prompt.shape[1], dtype=jnp.int32)
    pos_s = PAST_LEN + jnp.arange(x_sample.shape[1], dtype=jnp.int32)
    xp = x_prompt
    xs = x_sample
    ret_p, k_p, v_p, ki_p = [], [], [], []
    ret_s, k_s, v_s, ki_s = [], [], [], []
    for l in range(DEPTH):
        zero_state = jnp.zeros((xp.shape[0], RET_HEADS, RET_HEAD_DIM, RET_HEAD_DIM), xp.dtype)
        xp, sp, kp, vp, ip = mixer_layer(xp, pos_p, zero_state, None, None, None,
                                         norm_g[l], w_in[l], ret_gn_g[l], w_out[l])
        xs, ss, kss, vss, iss = mixer_layer(xs, pos_s, state_ret[l], cache_k[l], cache_v[l], cache_kidx[l],
                                            norm_g[l], w_in[l], ret_gn_g[l], w_out[l])
        ret_p.append(sp); k_p.append(kp); v_p.append(vp); ki_p.append(ip)
        ret_s.append(ss); k_s.append(kss); v_s.append(vss); ki_s.append(iss)
    y_prompt = rmsnorm(xp, final_g)
    y_sample = rmsnorm(xs, final_g)
    return (y_prompt, y_sample,
            jnp.stack(ret_p), jnp.stack(k_p), jnp.stack(v_p), jnp.stack(ki_p),
            jnp.stack(ret_s), jnp.stack(k_s), jnp.stack(v_s), jnp.stack(ki_s))


_drawn_inputs = setup_inputs


def setup_inputs(seed=0):
    import zlib

    import numpy as np

    out = dict(_drawn_inputs(seed))
    spreads = {}
    factors = {'ret_gn_g': 3.006, 'cache_k': 2.672}
    for name, (base, spread) in spreads.items():
        noise = np.random.default_rng([zlib.crc32(name.encode()), seed]).standard_normal(out[name].shape)
        drawn = base * np.exp(spread * noise) if base else spread * noise
        out[name] = __import__('jax').numpy.asarray(drawn.astype(out[name].dtype))
    for name, factor in factors.items():
        out[name] = (out[name] * factor).astype(out[name].dtype)
    return out
```

```python
from contextlib import ExitStack
from math import erf, sqrt

import numpy as np

import concourse.bass as bass
from concourse import mybir

F32 = mybir.dt.float32
F32R = mybir.dt.float32r
BF16 = mybir.dt.bfloat16
ALU = mybir.AluOpType
ACT = mybir.ActivationFunctionType
AX_X = mybir.AxisListType.X

P = 128
D = 1024
KD = D // P
SEQ, DEC, PAST = 1024, 64, 1024
CHUNK = 64
NT = SEQ // P
TILES = NT + 1
SAMPLE = NT
RH, RD = 4, 128
AH, HD, KVH = 8, 64, 2
IH = 8
ROT = HD // 4
TOPK = 256
EPS = 1e-6
NB = 8
BW = 512
MASKED = -3.0e38
TAKEN = -3.4e38
BETWEEN = -3.3e38
COUNTS = 5
WINDOW = 16
AIM = TOPK - (WINDOW + 1) / 2
C_RQ, C_RK, C_RV, C_RG = 0, 512, 1024, 1536
C_AQ, C_AK, C_AG, C_IQ, C_IK, C_IW = 2048, 2560, 2816, 3328, 3840, 3904
KVW = 328

LOG_GAMMA = [float(np.log1p(-np.exp2(-5.0 - h))) for h in range(RH)]


def keys_of(t):
    return PAST + DEC if t == SAMPLE else P * (t + 1)


def chunks_of(t):
    n = keys_of(t)
    return [(c, min(c + BW, n)) for c in range(0, n, BW)]


def groups_of(t):
    blocks = [(b, min(P, keys_of(t) - b * P)) for b in range(-(-keys_of(t) // P))]
    return [blocks[i:i + 4] for i in range(0, len(blocks), 4)]


def attention_order(t):
    scores = lambda h: [("score", h, c) for c in range(len(chunks_of(t)))]
    groups = range(len(groups_of(t)))
    order, last = scores(0) + scores(1), None
    for h in range(AH):
        for g in groups:
            order.append(("turn", h, g))
            if last:
                order.append(("value", *last))
            last = (h, g)
        if h + 2 < AH:
            order += scores(h + 2)
    return order + [("value", *last)]


def index_order(t):
    return [(h, c) for h in range(IH) for c in range(len(chunks_of(t)))]


SMALL = 28 + 2 * TILES


def searched(t):
    return keys_of(t) > TOPK


def normal_quantile(share):
    low, high = -8.0, 8.0
    for _ in range(60):
        mid = (low + high) / 2
        low, high = (mid, high) if (1 + erf(mid / sqrt(2))) / 2 < share else (low, mid)
    return low


def constants():
    pos = np.concatenate([np.arange(SEQ), PAST + np.arange(DEC), PAST + np.arange(DEC)]).astype(np.float32)

    def angles(half, theta):
        inv = np.power(np.float32(theta), -np.arange(half, dtype=np.float32) / np.float32(half)).astype(np.float32)
        a = (pos[:, None] * inv[None, :]).astype(np.float32)
        return np.cos(a).astype(np.float32), np.sin(a).astype(np.float32)

    c, s = angles(ROT // 2, 500000.0)
    rope_a = np.concatenate([c, c, -s, s], axis=1)
    rope_a = rope_a.reshape(TILES, P, 2 * ROT).transpose(1, 0, 2).reshape(P, -1)
    c, s = angles(RD // 2, 10000.0)
    ks = np.float32(RD ** -0.5)
    rope_r = np.concatenate([c, s, c * ks, s * ks], axis=1)
    lg = np.array(LOG_GAMMA)
    m, n = np.arange(P)[:, None], np.arange(P)[None, :]
    seen = (m // CHUNK) <= (n // CHUNK)
    decay = np.stack([np.where(seen, np.exp(g * np.abs(n - m)), 0.0) for g in lg], 1)
    first = (m < DEC) & (n < 2 * DEC)
    decay_s = np.stack([np.where(first, np.exp(g * np.abs(n % DEC - m)), 0.0) for g in lg], 1)
    from_start = np.stack([np.broadcast_to(np.exp(g * (np.arange(P) + 1)), (P, P)) for g in lg], 1)
    to_end = np.exp(lg[None, :] * (P - 1 - np.arange(P))[:, None])
    to_end_s = np.where(np.arange(P)[:, None] < DEC, np.exp(lg[None, :] * (DEC - 1 - np.arange(P))[:, None]), 0.0)
    small = np.zeros((P, SMALL))
    small[:, 0:4], small[:, 4:8] = to_end, to_end_s
    small[:, 8], small[:, 9], small[:, 10] = -0.5, 0.5, ((WINDOW - 1) / 2) ** 2
    small[:, 12:12 + WINDOW] = np.arange(WINDOW)
    for t in range(TILES):
        if searched(t):
            for rows, n in ((slice(0, CHUNK), keys_of(t) - (CHUNK if t < SAMPLE else 0)), (slice(CHUNK, P), keys_of(t))):
                z = normal_quantile(1 - AIM / n)
                small[rows, 28 + 2 * t] = z
                small[rows, 29 + 2 * t] = np.sqrt(2 * np.pi) * np.exp(z * z / 2) / n
    return {
        "identity": np.eye(P, dtype=np.float32),
        "rope_att": np.ascontiguousarray(rope_a, np.float32),
        "rope_ret": np.ascontiguousarray(rope_r, np.float32),
        "decay": decay.reshape(P, -1).astype(np.float32),
        "decay_sample": decay_s.reshape(P, -1).astype(np.float32),
        "from_start": from_start.reshape(P, -1).astype(np.float32),
        "small": small.astype(np.float32),
    }


def hybrid_stream_step(nc, x_prompt, x_sample, state_ret, cache_k, cache_v, cache_kidx, norm_g, w_in,
                       ret_gn_g, w_out, final_g, identity, rope_att, rope_ret, decay, decay_sample,
                       from_start, small,
                       y_prompt, y_sample, ret_p, k_p, v_p, kidx_p, ret_s, k_s, v_s, kidx_s):
    xp, xs = x_prompt[0], x_sample[0]
    w_rows = w_in[0].rearrange("(k p) n -> p k n", p=P)
    wo_rows = w_out[0].rearrange("(k p) n -> p k n", p=P)
    gn_row = ret_gn_g
    fg_row = final_g.rearrange("(a d) -> a d", a=1)
    kc = cache_k[0, 0].rearrange("(b p) h d -> p b (h d)", p=P)
    vc = cache_v[0, 0].rearrange("(b p) h d -> p b (h d)", p=P)
    ic = cache_kidx[0, 0].rearrange("(b p) d -> p b d", p=P)
    k_out, v_out, i_out = (a[0, 0] for a in (k_p, v_p, kidx_p))
    k_out, v_out = (a.rearrange("t h d -> t (h d)") for a in (k_out, v_out))
    ks_out, vs_out, is_out = (a[0, 0] for a in (k_s, v_s, kidx_s))
    ks_out, vs_out = (a.rearrange("t h d -> t (h d)") for a in (ks_out, vs_out))
    att_mem = nc.dram_tensor("attended", (TILES * P, BW), F32).ap()
    ret_mem = nc.dram_tensor("retained", (TILES * P, BW), F32).ap()

    with ExitStack() as ctx:
        place = [(nc.sbuf_base + 63) // 32 * 32]

        def sb(name, shape, dt=F32, at=None):
            size = int(np.prod(shape[1:])) * (2 if dt == BF16 else 4)
            where = place if at is None else at
            t = nc.alloc_sbuf_tensor_at(name, shape, dt, offset=where[0])
            where[0] += (size + 31) // 32 * 32
            return t

        SLOTS = 4
        w_hi = [sb(f"w_hi{s}", [P, KD, BW], F32R) for s in range(SLOTS)]
        w_lo = [sb(f"w_lo{s}", [P, KD, BW], F32R) for s in range(SLOTS)]
        stage = [sb(f"stage{s}", [P, 2, BW]) for s in range(2)]
        ident = sb("ident", [P, P])
        g_in = sb("g_in", [P, KD])
        cst = sb("cst", [P, SMALL])
        ones8 = sb("ones8", [P, KD])
        rope_t = sb("rope_t", [P, TILES, 2 * ROT])
        stats = sb("stats", [P, 2, 6])
        mean2 = sb("mean2", [P, 4])
        mean_sq = sb("mean_sq", [P, 2])
        group_sq = sb("group_sq", [P, 4])
        rstd = sb("rstd", [P, 4])
        xin = sb("xin", [P, D])
        xT_hi = sb("xT_hi", [P, KD, P], F32R)
        xT_lo = sb("xT_lo", [P, KD, P], F32R)
        phase_start = place[0]
        NK = PAST + DEC
        kT_hi, kT_lo = (sb(f"kT_{x}", [P, NK], F32R) for x in ("hi", "lo"))
        kiT_hi, kiT_lo = (sb(f"kiT_{x}", [P, NK], F32R) for x in ("hi", "lo"))
        v_sb = sb("v_sb", [P, TILES, KVH * HD])
        q_row = sb("q_row", [P, BW])
        kv_row = sb("kv_row", [P, 392])
        rope_a, rope_b = (sb(f"rope_{x}", [P, AH, ROT]) for x in "ab")
        iw_s = sb("iw_s", [P, IH])
        iqT_hi, iqT_lo = (sb(f"iqT_{x}", [P, 4, P], F32R) for x in ("hi", "lo"))
        aqT_hi, aqT_lo = (sb(f"aqT_{x}", [P, 4, P], F32R) for x in ("hi", "lo"))
        idx = sb("idx", [P, NK])
        work = sb("work", [P, NK + 8])
        top8 = sb("top8", [P, 8])
        drop8 = sb("drop8", [P, 8])
        found = sb("found", [P, 16])
        total, squares, mean, var, dev, above, slope, seen, over, over_was, far, move, gap, open_, any_far, left = (
            found[:, i:i + 1] for i in range(16))
        bias = sb("bias", [P, NK], BF16)
        probs = [sb(f"probs{i}", [P, NK]) for i in range(2)]
        pT = [sb(f"pT{i}", [P, 4, P]) for i in range(2)]
        low = sb("low", [P, AH, 3])
        den = sb("den", [P, AH])
        rden = sb("rden", [P, AH])
        ao = probs[0][:, 0:BW]
        assert place[0] <= nc.sbuf_usable_end, place[0]
        at = [phase_start]
        rq_row, rk_row, rv_row = (sb(f"{x}_row", [P, RH, RD], at=at) for x in ("rq", "rk", "rv"))
        rtmp = sb("rtmp", [P, RH, RD], at=at)
        kd_row = sb("kd_row", [P, RH, RD], at=at)
        rqT, rkT, rqdT = (sb(f"{x}T", [P, RH, P], at=at) for x in ("rq", "rk", "rqd"))
        rsT = sb("rsT", [P, RH, P], at=at)
        state = sb("state", [P, RH, RD], at=at)
        state_s = sb("state_s", [P, RH, RD], at=at)
        ro = sb("ro", [P, RH, RD], at=at)
        dec_t, dec_s, start_t = (sb(n, [P, RH, P], at=at) for n in ("dec_t", "dec_s", "start_t"))
        gn_t = sb("gn_t", [P, BW], at=at)
        rot_r = sb("rot_r", [P, 4, RD // 2], at=at)
        gate = sb("gate", [P, D], at=at)
        mixed = sb("mixed", [P, D], at=at)
        mT_hi, mT_lo = (sb(f"mT_{x}", [P, KD, P], F32R, at=at) for x in ("hi", "lo"))
        y_row = sb("y_row", [P, D], at=at)
        fg_t = sb("fg_t", [P, D], at=at)
        assert at[0] <= nc.sbuf_usable_end, at[0]

        bank = [ctx.enter_context(nc.psum_tensor(f"bank{b}", [P, BW], F32)) for b in range(NB)]
        filled = [ctx.enter_context(nc.semaphore(f"filled{b}")) for b in range(NB)]
        drained = [ctx.enter_context(nc.semaphore(f"drained{b}")) for b in range(NB)]

        def sem(name):
            return ctx.enter_context(nc.semaphore(name))

        const_in = sem("const_in")
        x_in = sem("x_in")
        stage_in = [sem(f"stage_in{i}") for i in range(2)]
        vcache_in = sem("vcache_in")
        w_rounded = sem("w_rounded")
        w_split = sem("w_split")
        stat_done = sem("stat_done")
        ms_ready = sem("ms_ready")
        rstd_ready = sem("rstd_ready")
        xn_ready = sem("xn_ready")
        hi_ready = sem("hi_ready")
        rowed = sem("rowed")
        rope_step = sem("rope_step")
        q_roped = sem("q_roped")
        kv_roped = sem("kv_roped")
        kv_stored = sem("kv_stored")
        relued = sem("relued")
        index_summed = sem("index_summed")
        guess_step = sem("guess_step")
        guessed = sem("guessed")
        far_ready = sem("far_ready")
        any_ready = sem("any_ready")
        whole_step = sem("whole_step")
        ones_ready = sem("ones_ready")
        value_done = sem("value_done")
        topk_step = sem("topk_step")
        exped = sem("exped")
        ao_step = sem("ao_step")
        ao_stored = sem("ao_stored")
        r_const_in = sem("r_const_in")
        rot_in = sem("rot_in")
        rq_ready, rk_ready = sem("rq_ready"), sem("rk_ready")
        kd_ready = sem("kd_ready")
        rqd_ready = sem("rqd_ready")
        squared = sem("squared")
        ro_stored = sem("ro_stored")
        state_zero = sem("state_zero")
        state_stored = sem("state_stored")
        mix_in = sem("mix_in")
        y_in = sem("y_in")
        gated = sem("gated")
        mixed_ready = sem("mixed_ready")
        summed = sem("summed")
        y_ready = sem("y_ready")
        y_stored = sem("y_stored")
        fg_in = sem("fg_in")

        uses = [0] * NB
        use = {}
        turn = [0]

        def take(key, b=None):
            if b is None:
                b = turn[0] % (NB - 1)
                turn[0] += 1
            use[key] = (b, uses[b])
            uses[b] += 1

        def take_attention(t):
            for step in attention_order(t):
                if step[0] != "value":
                    take((*step, t))
            take(("attended", t), NB - 1)

        for t in range(TILES):
            for s in ("x0", "x1", "iq", "kv", "turn_iq", "turn_kv"):
                take((s, "A", t))
            if t == SAMPLE:
                take(("turn_ci", 0))
                take(("turn_ci", 1))
            for h, c in index_order(t):
                take(("index", h, c, t))
            if t:
                take_attention(t - 1)
            if t == SAMPLE:
                take(("turn_ck", 0))
                take(("turn_ck", 1))
            take(("aq", "A", t))
            take(("turn_aq", "A", t))
        take_attention(SAMPLE)
        base_r = list(uses)
        R_BANK = {"q": (0, 0), "k": (1, 0), "v": (2, 0), "x0": (3, 0), "x1": (4, 0), "turn_q": (5, 0),
                  "turn_k": (6, 0), "scores": (7, 0), "out": (0, 1), "kv": (1, 1)}
        R_USES = [2, 2, 1, 1, 1, 1, 1, 1]
        base_o = [b + TILES * u for b, u in zip(base_r, R_USES)]
        O_BANK = {"rg": 0, "ag": 1, "x0": 2, "x1": 3, "turn0": 4, "turn1": 5, "y0": 6, "y1": 7}

        def bank_use(key):
            if key[-2:-1] == ("R",):
                b, k = R_BANK[key[0]]
                return b, base_r[b] + key[-1] * R_USES[b] + k
            if key[-2:-1] == ("O",):
                return O_BANK[key[0]], base_o[O_BANK[key[0]]] + key[-1]
            return use[key]

        def of(key):
            return bank[bank_use(key)[0]]

        def wait_filled(eng, key):
            b, n = bank_use(key)
            eng.wait_ge(filled[b], n + 1)

        def wait_drained(eng, key):
            b, n = bank_use(key)
            eng.wait_ge(drained[b], n + 1)

        def wait_free(eng, key):
            b, n = bank_use(key)
            if not (isinstance(n, int) and n == 0):
                eng.wait_ge(drained[b], n)

        def fills(key):
            return filled[bank_use(key)[0]], 1

        def drains(key):
            return drained[bank_use(key)[0]], 1

        A_HI, R_HI, O_HI = 6, 2, 4
        hi_at = {}
        n = 0
        for t in range(TILES):
            for s in ["x0", "x1", "turn_iq", "turn_kv"] + ["ci0", "ci1", "ck0", "ck1"] * (t == SAMPLE) + ["turn_aq"]:
                n += 1
                hi_at[s, "A", t] = n
        hi_r = n
        hi_o = hi_r + R_HI * TILES

        def hi_no(s, phase, t):
            if phase == "A":
                return hi_at[s, "A", t]
            if phase == "R":
                return hi_r + t * R_HI + {"x0": 1, "x1": 2}[s]
            return hi_o + t * O_HI + {"x0": 1, "x1": 2, "turn0": 3, "turn1": 4}[s]

        index_no, group_no, value_no, n, v = {}, {}, {}, 0, 0
        for t in range(TILES):
            for h, c in index_order(t):
                n += 1
                index_no[t, h, c] = n
        for t in range(TILES):
            for kind, h, g in attention_order(t):
                if kind == "value":
                    group_no[t, h, g] = len(group_no)
                    if (h, g) != (AH - 1, len(groups_of(t)) - 1):
                        v += 1
                        value_no[group_no[t, h, g]] = v
                    else:
                        value_no[group_no[t, h, g]] = ("attended", t)

        def wait_value(eng, no):
            if no >= 0:
                if isinstance(value_no[no], int):
                    eng.wait_ge(value_done, value_no[no])
                else:
                    wait_filled(eng, value_no[no])

        def last_score(t, h):
            return ("score", h, len(chunks_of(t)) - 1, t)

        def stat_no(what, t):
            if what == "y":
                return 35 if isinstance(t, int) and t == SAMPLE else 20 + 2 * t
            if what == "O":
                return 18 if isinstance(t, int) and t == 0 else 17 + 2 * t
            return NORM[what] + t

        def power_no(what, t):
            if what == "y":
                return 44 if isinstance(t, int) and t == SAMPLE else 29 + 2 * t
            if what == "O":
                return 26 + 2 * t
            if what == "retained":
                return 11 + 2 * t
            if what == "R":
                return TILES if isinstance(t, int) and t == 0 else 8 + 2 * t
            return t

        R_CONSTS = 16 * 5
        NORM = {"A": 0, "R": TILES, "O": 2 * TILES}

        def slot_items(slot, what):
            return [(slot, what, kp) for kp in range(KD // 2)]

        items = (slot_items(0, "iq") + slot_items(1, "kv") + slot_items(2, "aq") + slot_items(3, "rq")
                 + [(None, "ci", 0), (None, "ck", 0)] + slot_items(0, "rk") + slot_items(1, "rv")
                 + slot_items(2, "rg") + slot_items(3, "ag") + slot_items(0, "wo0") + slot_items(1, "wo1"))
        COLS = {"iq": [(C_IQ, 0, BW)], "kv": [(C_IK, 0, HD), (C_AK, HD, 2 * KVH * HD), (C_IW, HD + 2 * KVH * HD, IH)],
                "aq": [(C_AQ, 0, BW)], "rq": [(C_RQ, 0, BW)], "rk": [(C_RK, 0, BW)], "rv": [(C_RV, 0, BW)],
                "rg": [(C_RG, 0, BW)], "ag": [(C_AG, 0, BW)], "wo0": [(0, 0, BW)], "wo1": [(BW, 0, BW)]}
        item_no = {(w, kp): i for i, (_, w, kp) in enumerate(items)}
        staged, count = [], [0, 0]
        for i, (slot, w, kp) in enumerate(items):
            count[i % 2] += 16 * (len(COLS[w]) if slot is not None else 2 if w == "ci" else 1)
            staged.append(count[i % 2])
        split_no, n = {}, 0
        for slot, w, kp in items:
            if slot is not None:
                n += 1
                split_no[w, kp] = n
        slot_free = {"rk": ("iq", "A", SAMPLE), "rv": ("kv", "A", SAMPLE), "rg": ("aq", "A", SAMPLE),
                     "ag": ("q", "R", SAMPLE), "wo0": ("k", "R", SAMPLE), "wo1": ("v", "R", SAMPLE)}
        SLOT = {w: slot for slot, w, _ in items}
        WIDTH = {w: sum(c[2] for c in COLS[w]) for w in COLS}

        block = ctx.enter_context(nc.Block())

        @block.sync
        def _(sp):
            def load(i):
                slot, w, kp = items[i]
                buf = stage[i % 2]
                if i >= 2:
                    _, w2, kp2 = items[i - 2]
                    if w2 == "ci":
                        wait_filled(sp, ("turn_ci", 1))
                    elif w2 == "ck":
                        wait_filled(sp, ("turn_ck", 1))
                    else:
                        sp.wait_ge(w_split, split_no[w2, kp2])
                if w == "ci":
                    dst = buf[:].rearrange("p a (b h d) -> p (a b) h d", h=2, d=HD)
                    for half in range(2):
                        sp.dma_start(dst[:, :, half, :], ic).then_inc(stage_in[i % 2], 16)
                elif w == "ck":
                    sp.dma_start(buf[:].rearrange("p a (b n) -> p (a b) n", n=P), kc).then_inc(stage_in[i % 2], 16)
                else:
                    rows = wo_rows if w.startswith("wo") else w_rows
                    for src, dst, n in COLS[w]:
                        sp.dma_start(buf[:, :, dst:dst + n], rows[:, 2 * kp:2 * kp + 2, src:src + n])\
                          .then_inc(stage_in[i % 2], 16)

            def load_x(phase, t, wait=True):
                if wait:
                    prev = {"A": None, "R": ("x1", "A", SAMPLE), "O": ("x1", "R", SAMPLE)}[phase]
                    if not (isinstance(t, int) and t == 0):
                        prev = ("x1", phase, t - 1)
                    if prev:
                        wait_filled(sp, prev)
                for half in range(2):
                    src = xs if isinstance(t, int) and t == SAMPLE else xp[bass.ds(t * P + half * DEC, DEC), :]
                    sp.dma_start(xin[half * DEC:(half + 1) * DEC, :], src).then_inc(x_in, 16)

            sp.dma_start(ident[:], identity).then_inc(const_in, 16)
            sp.dma_start(g_in[:], norm_g).then_inc(const_in, 16)
            sp.dma_start(cst[:], small).then_inc(const_in, 16)
            sp.dma_start(rope_t[:], rope_att.rearrange("p (t n) -> p t n", n=2 * ROT)).then_inc(const_in, 16)
            load_x("A", 0)
            for i in range(12):
                load(i)
            for t in range(1, TILES):
                load_x("A", t)
                if 2 <= t <= 5:
                    load(10 + t)
                if t == 7:
                    load(item_no["ci", 0])
                    load(item_no["ck", 0])
            load_x("R", 0)
            for w in ("rk", "rv", "rg"):
                for kp in range(4):
                    load(item_no[w, kp])
            with sp.Fori(1, NT) as t:
                load_x("R", t)
            load_x("R", SAMPLE)
            load_x("O", 0)
            for w in ("ag", "wo0", "wo1"):
                for kp in range(4):
                    load(item_no[w, kp])
            with sp.Fori(1, NT) as t:
                load_x("O", t)
            load_x("O", SAMPLE)

        @block.tensor
        def _(pe):
            def turn_x(phase, t):
                pe.wait_ge(xn_ready, NORM[phase] + t + 1)
                for half in range(2):
                    key = (f"x{half}", phase, t)
                    wait_free(pe, key)
                    for j in range(4):
                        k = 4 * half + j
                        mm = pe.transpose(of(key)[:, j * P:(j + 1) * P], xin[:, k * P:(k + 1) * P], ident[:])
                    mm.then_inc(*fills(key))

            def product(key, slot, width, hi, lo):
                wait_free(pe, key)
                out = of(key)[:, 0:width]
                for k in range(KD):
                    wh, wl = w_hi[slot][:, k, 0:width], w_lo[slot][:, k, 0:width]
                    pe.matmul(out, hi[:, k, :], wh, start=(k == 0), stop=False)
                    pe.matmul(out, hi[:, k, :], wl, start=False, stop=False)
                    mm = pe.matmul(out, lo[:, k, :], wh, start=False, stop=(k == KD - 1))
                mm.then_inc(*fills(key))

            def project(name, w, phase, t, first):
                if first:
                    pe.wait_ge(w_split, split_no[w, 3])
                product((name, phase, t), SLOT[w], WIDTH[w], xT_hi, xT_lo)

            def turn_rows(key, rows, n):
                wait_free(pe, key)
                for j in range(n):
                    mm = pe.transpose(of(key)[:, j * P:(j + 1) * P], rows[:, j * P:(j + 1) * P], ident[:])
                mm.then_inc(*fills(key))

            def turn_cached(name, item):
                i = item_no[item, 0]
                pe.wait_ge(stage_in[i % 2], staged[i])
                for half in range(2):
                    key = (name, half)
                    wait_free(pe, key)
                    for j in range(4):
                        mm = pe.transpose(of(key)[:, j * P:(j + 1) * P], stage[i % 2][:, half, j * P:(j + 1) * P],
                                          ident[:])
                    mm.then_inc(*fills(key))

            def three(out, a_hi, a_lo, b_hi, b_lo):
                pe.matmul(out, a_hi, b_hi, start=True, stop=False)
                pe.matmul(out, a_hi, b_lo, start=False, stop=False)
                return pe.matmul(out, a_lo, b_hi, start=False, stop=True)

            def index(t):
                wait_drained(pe, ("turn_iq", "A", t))
                wait_drained(pe, ("turn_kv", "A", t))
                if t == SAMPLE:
                    for half in range(2):
                        wait_drained(pe, ("turn_ci", half))
                for h, c in index_order(t):
                    a, b = chunks_of(t)[c]
                    r = slice(HD * (h % 2), HD * (h % 2) + HD)
                    key = ("index", h, c, t)
                    wait_free(pe, key)
                    three(of(key)[:, 0:b - a], iqT_hi[r, h // 2, :], iqT_lo[r, h // 2, :],
                          kiT_hi[r, a:b], kiT_lo[r, a:b]).then_inc(*fills(key))

            def attend(t):
                wait_drained(pe, ("turn_aq", "A", t))
                if t == SAMPLE:
                    for half in range(2):
                        wait_drained(pe, ("turn_ck", half))
                    pe.wait_ge(vcache_in, 16)
                for kind, h, n in attention_order(t):
                    kv = h // (AH // KVH)
                    key = (kind, h, n, t)
                    if kind == "score":
                        a, b = chunks_of(t)[n]
                        r = slice(HD * kv, HD * kv + HD)
                        wait_free(pe, key)
                        three(of(key)[:, 0:b - a], aqT_hi[r, h % 4, :], aqT_lo[r, h % 4, :],
                              kT_hi[r, a:b], kT_lo[r, a:b]).then_inc(*fills(key))
                    elif kind == "turn":
                        pe.wait_ge(exped, AH * t + h + 1)
                        wait_free(pe, key)
                        for j, (blk, rows) in enumerate(groups_of(t)[n]):
                            mm = pe.transpose(of(key)[0:rows, j * P:(j + 1) * P],
                                              probs[h % 2][:, blk * P:blk * P + rows], ident[:])
                        mm.then_inc(*fills(key))
                    else:
                        wait_drained(pe, ("turn", h, n, t))
                        if h == 0 and n == 0:
                            wait_free(pe, ("attended", t))
                        for j, (blk, rows) in enumerate(groups_of(t)[n]):
                            last = blk == len([1 for g in groups_of(t) for _ in g]) - 1
                            mm = pe.matmul(of(("attended", t))[:, h * HD:(h + 1) * HD],
                                           pT[group_no[t, h, n] % 2][0:rows, j, :],
                                           v_sb[0:rows, blk, kv * HD:(kv + 1) * HD],
                                           start=(blk == 0), stop=last)
                        if last:
                            if h == AH - 1:
                                mm.then_inc(*fills(("attended", t)))
                            else:
                                mm.then_inc(value_done, 1)
                        else:
                            mm.then_inc(value_done, 1)

            pe.wait_ge(const_in, 64)
            for t in range(TILES):
                turn_x("A", t)
                for half in range(2):
                    wait_drained(pe, (f"x{half}", "A", t))
                project("iq", "iq", "A", t, t == 0)
                project("kv", "kv", "A", t, t == 0)
                pe.wait_ge(q_roped, 2 * t + 1)
                turn_rows(("turn_iq", "A", t), q_row, 4)
                pe.wait_ge(kv_roped, t + 1)
                turn_rows(("turn_kv", "A", t), kv_row, 2)
                if t == SAMPLE:
                    turn_cached("turn_ci", "ci")
                index(t)
                if t:
                    attend(t - 1)
                if t == SAMPLE:
                    turn_cached("turn_ck", "ck")
                project("aq", "aq", "A", t, t == 0)
                pe.wait_ge(q_roped, 2 * t + 2)
                turn_rows(("turn_aq", "A", t), q_row, 4)
            attend(SAMPLE)

            def retain(t, st):
                pe.wait_ge(rq_ready, t + 1)
                turn_rows(("turn_q", "R", t), rq_row[:].rearrange("p h d -> p (h d)"), 4)
                pe.wait_ge(rk_ready, t + 1)
                turn_rows(("turn_k", "R", t), rk_row[:].rearrange("p h d -> p (h d)"), 4)
                wait_drained(pe, ("turn_q", "R", t))
                wait_drained(pe, ("turn_k", "R", t))
                key = ("scores", "R", t)
                wait_free(pe, key)
                for h in range(RH):
                    mm = pe.matmul(of(key)[:, h * P:(h + 1) * P], rkT[:, h, :], rqT[:, h, :], start=True, stop=True)
                mm.then_inc(*fills(key))
                pe.wait_ge(kd_ready, t + 1)
                wait_drained(pe, ("v", "R", t))
                key = ("kv", "R", t)
                wait_free(pe, key)
                for h in range(RH):
                    mm = pe.matmul(of(key)[:, h * RD:(h + 1) * RD], kd_row[:, h, :], rv_row[:, h, :],
                                   start=True, stop=True)
                mm.then_inc(*fills(key))
                pe.wait_ge(rqd_ready, t + 1)
                if isinstance(t, int) and t == SAMPLE:
                    pe.wait_ge(r_const_in, R_CONSTS)
                elif isinstance(t, int) and t == 0:
                    pe.wait_ge(state_zero, 1)
                else:
                    wait_drained(pe, ("kv", "R", t - 1))
                wait_drained(pe, ("scores", "R", t))
                key = ("out", "R", t)
                wait_free(pe, key)
                for h in range(RH):
                    out = of(key)[:, h * RD:(h + 1) * RD]
                    pe.matmul(out, rqdT[:, h, :], st[:, h, :], start=True, stop=False)
                    mm = pe.matmul(out, rsT[:, h, :], rv_row[:, h, :], start=False, stop=True)
                mm.then_inc(*fills(key))

            def project_r(t, first=False):
                for half in range(2):
                    wait_drained(pe, (f"x{half}", "R", t))
                project("q", "rq", "R", t, first)
                project("k", "rk", "R", t, first)
                project("v", "rv", "R", t, first)

            turn_x("R", 0)
            project_r(0, True)
            turn_x("R", 1)
            retain(0, state)
            with pe.Fori(1, NT) as t:
                project_r(t)
                turn_x("R", t + 1)
                retain(t, state)
            project_r(SAMPLE)
            turn_x("O", 0)
            retain(SAMPLE, state_s)

            def out_tile(t, first=False, more=True):
                for half in range(2):
                    wait_drained(pe, (f"x{half}", "O", t))
                project("rg", "rg", "O", t, first)
                project("ag", "ag", "O", t, first)
                if more:
                    turn_x("O", t + 1)
                for half in range(2):
                    pe.wait_ge(mixed_ready, 2 * t + half + 1)
                    turn_rows((f"turn{half}", "O", t), mixed[:, half * BW:(half + 1) * BW], 4)
                for half in range(2):
                    wait_drained(pe, (f"turn{half}", "O", t))
                for half in range(2):
                    if first:
                        pe.wait_ge(w_split, split_no[f"wo{half}", 3])
                    product((f"y{half}", "O", t), SLOT[f"wo{half}"], BW, mT_hi, mT_lo)

            out_tile(0, first=True)
            with pe.Fori(1, NT) as t:
                out_tile(t)
            out_tile(SAMPLE, more=False)

        @block.scalar
        def _(act):
            def round_w(w, kp):
                i = item_no[w, kp]
                act.wait_ge(stage_in[i % 2], staged[i])
                if w in slot_free:
                    wait_filled(act, slot_free[w])
                g = ones8 if w.startswith("wo") else g_in
                for j in range(2):
                    k = 2 * kp + j
                    ins = act.activation(w_hi[SLOT[w]][:, k, 0:WIDTH[w]], stage[i % 2][:, j, 0:WIDTH[w]],
                                         ACT.Identity, scale=g[:, k:k + 1])
                ins.then_inc(w_rounded, 1)

            def hi(key, dst, src=None):
                wait_filled(act, key)
                act.copy(dst, of(key)[:] if src is None else src).then_inc(hi_ready, 1)

            def hi_x(phase, t):
                for half in range(2):
                    hi((f"x{half}", phase, t), xT_hi[:, 4 * half:4 * half + 4, :].rearrange("p k n -> p (k n)"))

            def attend(t):
                def exp(h):
                    nc_ = len(chunks_of(t))
                    wait_drained(act, last_score(t, h))
                    act.activation(probs[h % 2][:, 0:keys_of(t)], probs[h % 2][:, 0:keys_of(t)], ACT.Exp,
                                   bias=low[:, h, nc_ - 1:nc_], scale=-1.0,
                                   accum_out=den[:, h:h + 1]).then_inc(exped, 1)

                exp(0)
                exp(1)
                for h in range(AH):
                    for g in range(len(groups_of(t))):
                        key = ("turn", h, g, t)
                        n = group_no[t, h, g]
                        wait_filled(act, key)
                        wait_value(act, n - 2)
                        grp = groups_of(t)[g]
                        full = [x for x in grp if x[1] == P]
                        if full:
                            ins = act.copy(pT[n % 2][:, 0:len(full), :],
                                           of(key)[:, 0:len(full) * P].rearrange("p (j n) -> p j n", n=P))
                        if len(full) < len(grp):
                            ins = act.copy(pT[n % 2][0:grp[-1][1], len(full), :],
                                           of(key)[0:grp[-1][1], len(full) * P:(len(full) + 1) * P])
                        ins.then_inc(*drains(key))
                    if h + 2 < AH:
                        exp(h + 2)

            act.wait_ge(const_in, 64)
            act.wait_ge(ones_ready, 1)
            for kp in range(4):
                round_w("iq", kp)
            for t in range(TILES):
                hi_x("A", t)
                if t == 0:
                    for kp in range(4):
                        round_w("kv", kp)
                key = ("iq", "A", t)
                wait_filled(act, key)
                if t:
                    wait_filled(act, ("turn_aq", "A", t - 1))
                act.copy(q_row[:], of(key)[:]).then_inc(*drains(key))
                key = ("kv", "A", t)
                wait_filled(act, key)
                if t:
                    wait_filled(act, ("turn_kv", "A", t - 1))
                    act.wait_ge(kv_stored, 48 * t)
                act.copy(kv_row[:, HD:HD + KVW], of(key)[:, 0:KVW]).then_inc(rowed, 1)
                if t == SAMPLE:
                    act.copy(v_sb[0:DEC, SAMPLE, :], of(key)[0:DEC, 3 * HD:5 * HD]).then_inc(*drains(key))
                else:
                    act.copy(v_sb[:, t, :], of(key)[:, 3 * HD:5 * HD]).then_inc(*drains(key))
                hi(("turn_iq", "A", t), iqT_hi[:].rearrange("p k n -> p (k n)"))
                key = ("turn_kv", "A", t)
                n = DEC if t == SAMPLE else P
                wait_filled(act, key)
                act.copy(kiT_hi[:, t * P:t * P + n], of(key)[:, 0:n])
                act.copy(kT_hi[:, t * P:t * P + n], of(key)[:, P:P + n]).then_inc(hi_ready, 1)
                if t == SAMPLE:
                    for half in range(2):
                        hi(("turn_ci", half), kiT_hi[:, half * BW:(half + 1) * BW])
                for h, c in index_order(t):
                    a, b = chunks_of(t)[c]
                    key = ("index", h, c, t)
                    wait_filled(act, key)
                    act.activation(of(key)[:, 0:b - a], of(key)[:, 0:b - a], ACT.Relu).then_inc(relued, 1)
                if searched(t):
                    n = keys_of(t)
                    wait_drained(act, ("index", IH - 1, len(chunks_of(t)) - 1, t))
                    no = len([x for x in range(t) if searched(x)])
                    act.activation(work[:, 0:n], idx[:, 0:n], ACT.Identity, accum_out=total).then_inc(index_summed, 1)
                    act.wait_ge(index_summed, 2 * no + 1)
                    act.activation(work[:, 0:n], idx[:, 0:n], ACT.Square, accum_out=squares)\
                       .then_inc(index_summed, 1)
                if t:
                    attend(t - 1)
                if t == SAMPLE:
                    for half in range(2):
                        hi(("turn_ck", half), kT_hi[:, half * BW:(half + 1) * BW])
                    for kp in range(4):
                        round_w("rk", kp)
                if t == 0:
                    for kp in range(4):
                        round_w("aq", kp)
                key = ("aq", "A", t)
                wait_filled(act, key)
                wait_filled(act, ("turn_iq", "A", t))
                act.copy(q_row[:].rearrange("p (j a d) -> p a j d", a=2, d=HD),
                         of(key)[:].rearrange("p (a j d) -> p a j d", a=2, d=HD)).then_inc(*drains(key))
                hi(("turn_aq", "A", t), aqT_hi[:].rearrange("p k n -> p (k n)"))
                if 2 <= t <= 5:
                    round_w("rq", t - 2)
            for w in ("rv", "rg"):
                for kp in range(4):
                    round_w(w, kp)
            attend(SAMPLE)

            def retained(t):
                key = ("v", "R", t)
                wait_filled(act, key)
                if isinstance(t, int) and t == 0:
                    act.wait_ge(ao_stored, 16 * TILES)
                else:
                    wait_filled(act, ("out", "R", t - 1))
                act.copy(rv_row[:].rearrange("p h d -> p (h d)"), of(key)[:]).then_inc(*drains(key))

            def turned(t):
                key = ("turn_q", "R", t)
                wait_filled(act, key)
                act.copy(rqT[:].rearrange("p h d -> p (h d)"), of(key)[:]).then_inc(*drains(key))
                key = ("turn_k", "R", t)
                wait_filled(act, key)
                act.copy(rkT[:].rearrange("p h d -> p (h d)"), of(key)[:]).then_inc(*drains(key))

            def square(t):
                key = ("out", "R", t)
                wait_filled(act, key)
                if not (isinstance(t, int) and t == 0):
                    act.wait_ge(ro_stored, 16 * t)
                for h in range(RH):
                    ins = act.activation(ro[:, h, :], of(key)[:, h * RD:(h + 1) * RD], ACT.Square,
                                         accum_out=group_sq[:, h:h + 1])
                ins.then_inc(squared, 1)

            hi_x("R", 0)
            retained(0)
            hi_x("R", 1)
            turned(0)
            square(0)
            with act.Fori(1, NT) as t:
                retained(t)
                hi_x("R", t + 1)
                turned(t)
                square(t)
            retained(SAMPLE)
            hi_x("O", 0)
            turned(SAMPLE)
            for w in ("ag", "wo0", "wo1"):
                for kp in range(4):
                    round_w(w, kp)
            square(SAMPLE)

            def out_tile(t, more=True):
                for half, name in enumerate(("rg", "ag")):
                    key = (name, "O", t)
                    wait_filled(act, key)
                    if not (isinstance(t, int) and t == 0):
                        act.wait_ge(mixed_ready, 2 * t - 1 + half)
                    act.activation(gate[:, half * BW:(half + 1) * BW], of(key)[:], ACT.Silu)\
                       .then_inc(*drains(key))
                if more:
                    hi_x("O", t + 1)
                for half in range(2):
                    hi((f"turn{half}", "O", t), mT_hi[:, 4 * half:4 * half + 4, :].rearrange("p k n -> p (k n)"))

            out_tile(0)
            with act.Fori(1, NT) as t:
                out_tile(t)
            out_tile(SAMPLE, more=False)

        @block.vector
        def _(dve):
            def split_w(w, kp):
                i = item_no[w, kp]
                dve.wait_ge(w_rounded, split_no[w, kp])
                g = ones8 if w.startswith("wo") else g_in
                for j in range(2):
                    k = 2 * kp + j
                    ins = dve.scalar_tensor_tensor(
                        out=w_lo[SLOT[w]][:, k, 0:WIDTH[w]], in0=stage[i % 2][:, j, 0:WIDTH[w]],
                        scalar=g[:, k:k + 1], in1=w_hi[SLOT[w]][:, k, 0:WIDTH[w]].bitcast(F32),
                        op0=ALU.mult, op1=ALU.subtract)
                ins.then_inc(w_split, 1)

            STAT = 4

            def mean_square(rows, no):
                for half in range(2):
                    ins = dve.bn_stats(stats[:, half, :], rows[:, half * BW:(half + 1) * BW])
                ins.then_inc(stat_done, 1)
                parts = stats[:].rearrange("p a (b c) -> p (a b) c", c=3)
                dve.wait_ge(stat_done, STAT * no + 1)
                dve.tensor_tensor(mean2[:], parts[:, :, 1], parts[:, :, 1], ALU.mult).then_inc(stat_done, 1)
                dve.wait_ge(stat_done, STAT * no + 2)
                dve.scalar_tensor_tensor(out=mean2[:], in0=parts[:, :, 2], scalar=4.0 / D, in1=mean2[:],
                                         op0=ALU.mult, op1=ALU.add).then_inc(stat_done, 1)
                dve.wait_ge(stat_done, STAT * no + 3)
                dve.tensor_reduce(mean_sq[:, 0:1], mean2[:], AX_X, ALU.add).then_inc(stat_done, 1)
                dve.wait_ge(stat_done, STAT * no + 4)
                dve.tensor_scalar(mean_sq[:, 1:2], mean_sq[:, 0:1], 0.25, EPS, ALU.mult, ALU.add)\
                   .then_inc(ms_ready, 1)

            def normalise(phase, t):
                n = NORM[phase] + t
                dve.wait_ge(x_in, 32 * (n + 1))
                mean_square(xin, stat_no(phase, t))
                dve.wait_ge(rstd_ready, power_no(phase, t) + 1)
                dve.tensor_scalar(xin[:], xin[:], rstd[:, 0:1], None, ALU.mult).then_inc(xn_ready, 1)

            def lo(key, hi_index, dst, hi, src=None):
                dve.wait_ge(hi_ready, hi_index)
                dve.tensor_tensor(dst, of(key)[:] if src is None else src, hi.bitcast(F32), ALU.subtract)\
                   .then_inc(*drains(key))

            def lo_x(phase, t):
                for half in range(2):
                    s = slice(4 * half, 4 * half + 4)
                    lo((f"x{half}", phase, t), hi_no(f"x{half}", phase, t),
                       xT_lo[:, s, :].rearrange("p k n -> p (k n)"), xT_hi[:, s, :].rearrange("p k n -> p (k n)"))

            steps = [0]

            def step(ins):
                steps[0] += 1
                ins.then_inc(topk_step, 1)
                dve.wait_ge(topk_step, steps[0])

            def add_index(t):
                dve.wait_ge(kv_roped, t + 1)
                for h, c in index_order(t):
                    a, b = chunks_of(t)[c]
                    key = ("index", h, c, t)
                    dve.wait_ge(relued, index_no[t, h, c])
                    if h == 0:
                        ins = dve.tensor_scalar(idx[:, a:b], of(key)[:, 0:b - a], iw_s[:, 0:1], None, ALU.mult)
                    else:
                        wait_drained(dve, ("index", h - 1, c, t))
                        ins = dve.scalar_tensor_tensor(out=idx[:, a:b], in0=of(key)[:, 0:b - a],
                                                       scalar=iw_s[:, h:h + 1], in1=idx[:, a:b],
                                                       op0=ALU.mult, op1=ALU.add)
                    ins.then_inc(*drains(key))
                wait_drained(dve, ("index", IH - 1, len(chunks_of(t)) - 1, t))

            def choose(t):
                n = keys_of(t)
                if not searched(t):
                    step(dve.memset(bias[:, 0:n], 0.0))
                    step(dve.memset(bias[0:CHUNK, n - CHUNK:n], MASKED))
                    return
                no = len([x for x in range(t) if searched(x)])
                dve.wait_ge(guessed, no + 1)
                if t != SAMPLE:
                    step(dve.memset(idx[0:CHUNK, n - CHUNK:n], MASKED))
                now, was = over, over_was
                for i in range(COUNTS):
                    step(dve.tensor_scalar(work[:, 0:n], idx[:, 0:n], above, None, ALU.is_gt, ALU.add,
                                           accum_out=seen))
                    step(dve.tensor_scalar(now, seen, -AIM, None, ALU.add))
                    if i < COUNTS - 1:
                        step(dve.scalar_tensor_tensor(out=far, in0=now, scalar=now, in1=cst[:, 10:11],
                                                      op0=ALU.mult, op1=ALU.is_gt))
                        if i:
                            step(dve.tensor_tensor(gap, was, now, ALU.subtract))
                            step(dve.scalar_tensor_tensor(out=gap, in0=gap, scalar=0.0, in1=gap,
                                                          op0=ALU.is_equal, op1=ALU.add))
                            step(dve.reciprocal(gap, gap))
                            step(dve.tensor_tensor(gap, gap, move, ALU.mult))
                            step(dve.scalar_tensor_tensor(out=gap, in0=slope, scalar=0.25, in1=gap,
                                                          op0=ALU.mult, op1=ALU.max))
                            step(dve.scalar_tensor_tensor(out=slope, in0=slope, scalar=4.0, in1=gap,
                                                          op0=ALU.mult, op1=ALU.min))
                        step(dve.scalar_tensor_tensor(out=move, in0=now, scalar=slope, in1=far,
                                                      op0=ALU.mult, op1=ALU.mult))
                        step(dve.tensor_tensor(above, above, move, ALU.add))
                        now, was = was, now
                dve.scalar_tensor_tensor(out=far, in0=now, scalar=now, in1=cst[:, 10:11],
                                         op0=ALU.mult, op1=ALU.is_gt).then_inc(far_ready, 1)
                step(dve.memset(work[:, n:n + 8], TAKEN))
                step(dve.tensor_scalar(work[:, 0:n], idx[:, 0:n], above, TAKEN, ALU.is_gt, ALU.mult))
                step(dve.tensor_tensor(work[:, 0:n], work[:, 0:n], idx[:, 0:n], ALU.add))
                step(dve.tensor_scalar(left, seen, -1.0, float(TOPK), ALU.mult, ALU.add))
                for i in range(0, WINDOW, 8):
                    step(dve.tensor_scalar(drop8[:], cst[:, 12 + i:20 + i], left, TAKEN, ALU.is_ge, ALU.mult))
                    step(dve.max(top8[:], work[:, 0:n]))
                    step(dve.tensor_tensor(top8[:], top8[:], drop8[:], ALU.add))
                    step(dve.match_replace(work[:, 0:n + 8], top8[:], work[:, 0:n + 8], TAKEN))
                dve.wait_ge(any_ready, no + 1)
                off = dve.value_load(any_far[0:1, :].bitcast(mybir.dt.int32))
                with dve.If(off > 0):
                    dve.sem_clear(whole_step)
                    dve.tensor_copy(work[:, 0:n], idx[:, 0:n]).then_inc(whole_step, 1)
                    dve.wait_ge(whole_step, 1)
                    with dve.Fori(0, TOPK // 8):
                        dve.sem_clear(whole_step)
                        dve.max(top8[:], work[:, 0:n]).then_inc(whole_step, 1)
                        dve.wait_ge(whole_step, 1)
                        dve.match_replace(work[:, 0:n], top8[:], work[:, 0:n], TAKEN).then_inc(whole_step, 1)
                        dve.wait_ge(whole_step, 2)
                step(dve.tensor_scalar(bias[:, 0:n], work[:, 0:n], BETWEEN, MASKED, ALU.is_gt, ALU.mult))

            def attend(t):
                if t:
                    dve.wait_ge(ao_stored, 16 * t)
                for kind, h, c in attention_order(t):
                    if kind != "score":
                        continue
                    a, b = chunks_of(t)[c]
                    key = ("score", h, c, t)
                    wait_filled(dve, key)
                    if h >= 2:
                        wait_filled(dve, ("turn", h - 2, len(groups_of(t)) - 1, t))
                    if c:
                        wait_drained(dve, ("score", h, c - 1, t))
                    dve.tensor_tensor_reduce(out=probs[h % 2][:, a:b], in0=of(key)[:, 0:b - a], in1=bias[:, a:b],
                                             scale=-float(HD) ** -0.5, scalar=low[:, h, c - 1:c] if c else 3.0e38,
                                             op0=ALU.add, op1=ALU.min, accum_out=low[:, h, c:c + 1])\
                       .then_inc(*drains(key))
                dve.wait_ge(exped, AH * (t + 1))
                dve.reciprocal(rden[:], den[:]).then_inc(ao_step, 1)
                dve.wait_ge(ao_step, t + 1)
                key = ("attended", t)
                wait_filled(dve, key)
                dve.tensor_tensor(ao.rearrange("p (h d) -> p h d", d=HD),
                                  of(key)[:].rearrange("p (h d) -> p h d", d=HD),
                                  rden[:].unsqueeze(2).broadcast_to([P, AH, HD]), ALU.mult)\
                   .then_inc(*drains(key))

            dve.memset(ones8[:], 1.0).then_inc(ones_ready, 1)
            dve.wait_ge(const_in, 64)
            dve.wait_ge(ones_ready, 1)
            normalise("A", 0)
            for kp in range(4):
                split_w("iq", kp)
            for t in range(TILES):
                if t:
                    normalise("A", t)
                lo_x("A", t)
                if t == 0:
                    for kp in range(4):
                        split_w("kv", kp)
                lo(("turn_iq", "A", t), hi_no("turn_iq", "A", t), iqT_lo[:].rearrange("p k n -> p (k n)"),
                   iqT_hi[:].rearrange("p k n -> p (k n)"))
                key = ("turn_kv", "A", t)
                n = DEC if t == SAMPLE else P
                dve.wait_ge(hi_ready, hi_no("turn_kv", "A", t))
                dve.tensor_tensor(kiT_lo[:, t * P:t * P + n], of(key)[:, 0:n],
                                  kiT_hi[:, t * P:t * P + n].bitcast(F32), ALU.subtract)
                dve.tensor_tensor(kT_lo[:, t * P:t * P + n], of(key)[:, P:P + n],
                                  kT_hi[:, t * P:t * P + n].bitcast(F32), ALU.subtract).then_inc(*drains(key))
                if t == SAMPLE:
                    for half in range(2):
                        s = slice(half * BW, (half + 1) * BW)
                        lo(("turn_ci", half), hi_no(f"ci{half}", "A", t), kiT_lo[:, s], kiT_hi[:, s])
                add_index(t)
                if t:
                    attend(t - 1)
                if t == SAMPLE:
                    for half in range(2):
                        s = slice(half * BW, (half + 1) * BW)
                        lo(("turn_ck", half), hi_no(f"ck{half}", "A", t), kT_lo[:, s], kT_hi[:, s])
                    for kp in range(4):
                        split_w("rk", kp)
                if t == 0:
                    for kp in range(4):
                        split_w("aq", kp)
                lo(("turn_aq", "A", t), hi_no("turn_aq", "A", t), aqT_lo[:].rearrange("p k n -> p (k n)"),
                   aqT_hi[:].rearrange("p k n -> p (k n)"))
                if 2 <= t <= 5:
                    split_w("rq", t - 2)
                choose(t)
            for w in ("rv", "rg"):
                for kp in range(4):
                    split_w(w, kp)
            attend(SAMPLE)

            half = RD // 2

            def rotate(t, name, row, table, ready):
                key = (name, "R", t)
                wait_filled(dve, key)
                sin = rot_r[:, table + 1, :].unsqueeze(1)
                x = of(key)[:].rearrange("p (h a d) -> p h a d", a=2, d=half)
                both = rot_r[:, table, :].unsqueeze(1).broadcast_to([P, 2 * RH, half])
                dve.tensor_tensor(row[:].rearrange("p h (a d) -> p (h a) d", a=2),
                                  of(key)[:].rearrange("p (g d) -> p g d", d=half), both, ALU.mult)
                tm = rtmp[:].rearrange("p h (a d) -> p h a d", a=2)
                ro_ = row[:].rearrange("p h (a d) -> p h a d", a=2)
                for a in range(2):
                    ins = dve.tensor_tensor(tm[:, :, a, :], x[:, :, 1 - a, :], sin.broadcast_to([P, RH, half]), ALU.mult)
                ins.then_inc(*drains(key))
                wait_drained(dve, key)
                dve.tensor_tensor(ro_[:, :, 0, :], ro_[:, :, 0, :], tm[:, :, 0, :], ALU.subtract)
                dve.tensor_tensor(ro_[:, :, 1, :], ro_[:, :, 1, :], tm[:, :, 1, :], ALU.add).then_inc(ready, 1)

            def retain_rows(t):
                dve.wait_ge(rot_in, 16 * (t + 1))
                if isinstance(t, int) and t == 0:
                    dve.wait_ge(ao_stored, 16 * TILES)
                else:
                    wait_filled(dve, ("turn_k", "R", t - 1))
                    dve.wait_ge(kd_ready, t)
                rotate(t, "q", rq_row, 0, rq_ready)
                dve.wait_ge(rq_ready, t + 1)
                rotate(t, "k", rk_row, 2, rk_ready)

            def retain(t, st, table, length):
                key = ("scores", "R", t)
                wait_filled(dve, key)
                if not (isinstance(t, int) and t == 0):
                    wait_filled(dve, ("out", "R", t - 1))
                dve.tensor_tensor(rsT[:].rearrange("p h d -> p (h d)"), of(key)[:],
                                  table[:].rearrange("p h d -> p (h d)"), ALU.mult).then_inc(*drains(key))
                key = ("kv", "R", t)
                wait_filled(dve, key)
                wait_filled(dve, ("out", "R", t))
                for h in range(RH):
                    ins = dve.scalar_tensor_tensor(out=st[:, h, :], in0=st[:, h, :],
                                                   scalar=float(np.exp(LOG_GAMMA[h] * length)),
                                                   in1=of(key)[:, h * RD:(h + 1) * RD], op0=ALU.mult, op1=ALU.add)
                ins.then_inc(*drains(key))
                key = ("out", "R", t)
                dve.wait_ge(squared, t + 1)
                dve.tensor_scalar(group_sq[:], group_sq[:], 1.0 / RD, EPS, ALU.mult, ALU.add).then_inc(ms_ready, 1)
                dve.wait_ge(rstd_ready, power_no("retained", t) + 1)
                for h in range(RH):
                    ins = dve.scalar_tensor_tensor(out=ro[:, h, :], in0=of(key)[:, h * RD:(h + 1) * RD],
                                                   scalar=rstd[:, h:h + 1], in1=gn_t[:, h * RD:(h + 1) * RD],
                                                   op0=ALU.mult, op1=ALU.mult)
                ins.then_inc(*drains(key))

            normalise("R", 0)
            lo_x("R", 0)
            dve.wait_ge(ao_stored, 16 * TILES)
            dve.memset(state[:], 0.0).then_inc(state_zero, 1)
            dve.wait_ge(state_zero, 1)
            dve.wait_ge(r_const_in, R_CONSTS)
            retain_rows(0)
            normalise("R", 1)
            lo_x("R", 1)
            retain(0, state, dec_t, P)
            with dve.Fori(1, NT) as t:
                retain_rows(t)
                normalise("R", t + 1)
                lo_x("R", t + 1)
                retain(t, state, dec_t, P)
            retain_rows(SAMPLE)
            normalise("O", 0)
            lo_x("O", 0)
            for w in ("ag", "wo0", "wo1"):
                for kp in range(4):
                    split_w(w, kp)
            retain(SAMPLE, state_s, dec_s, DEC)

            def out_tile(t, more=True):
                dve.wait_ge(mix_in, 32 * (t + 1))
                for half_, name in enumerate(("rg", "ag")):
                    s = slice(half_ * BW, (half_ + 1) * BW)
                    wait_drained(dve, (name, "O", t))
                    dve.tensor_tensor(mixed[:, s], mixed[:, s], gate[:, s], ALU.mult).then_inc(mixed_ready, 1)
                if more:
                    normalise("O", t + 1)
                    lo_x("O", t + 1)
                for half_ in range(2):
                    s = slice(4 * half_, 4 * half_ + 4)
                    lo((f"turn{half_}", "O", t), hi_no(f"turn{half_}", "O", t),
                       mT_lo[:, s, :].rearrange("p k n -> p (k n)"), mT_hi[:, s, :].rearrange("p k n -> p (k n)"))
                dve.wait_ge(y_in, 32 * (t + 1))
                for half_ in range(2):
                    s = slice(half_ * BW, (half_ + 1) * BW)
                    key = (f"y{half_}", "O", t)
                    wait_filled(dve, key)
                    dve.tensor_tensor(y_row[:, s], of(key)[:], y_row[:, s], ALU.add).then_inc(*drains(key))
                for half_ in range(2):
                    wait_drained(dve, (f"y{half_}", "O", t))
                mean_square(y_row, stat_no("y", t))
                dve.wait_ge(rstd_ready, power_no("y", t) + 1)
                dve.scalar_tensor_tensor(out=y_row[:], in0=y_row[:], scalar=rstd[:, 0:1], in1=fg_t[:],
                                         op0=ALU.mult, op1=ALU.mult).then_inc(y_ready, 1)

            dve.wait_ge(fg_in, 16)
            out_tile(0)
            with dve.Fori(1, NT) as t:
                out_tile(t)
            out_tile(SAMPLE, more=False)

        @block.gpsimd
        def _(pool):
            def power(no, width):
                pool.wait_ge(ms_ready, no + 1)
                src = mean_sq[:, 1:2] if width == 1 else group_sq[:]
                pool.tensor_tensor(rstd[:, 0:width], src, cst[:, 8:9].broadcast_to([P, width]), ALU.pow)\
                    .then_inc(rstd_ready, 1)

            steps = [0]
            guesses = [0]

            def step(ins):
                steps[0] += 1
                ins.then_inc(rope_step, 1)
                pool.wait_ge(rope_step, steps[0])

            def rotate(rows, heads, t):
                x = rows.rearrange("p (h d) -> p h d", d=HD)
                cos = rope_t[:, t, 0:ROT].unsqueeze(1).broadcast_to([P, heads, ROT])
                a, b = rope_a[:, 0:heads, :], rope_b[:, 0:heads, :]
                h2 = ROT // 2
                pool.tensor_tensor(a, x[:, :, 0:ROT], cos, ALU.mult)
                for s in range(2):
                    sin = rope_t[:, t, ROT + s * h2:ROT + (s + 1) * h2].unsqueeze(1).broadcast_to([P, heads, h2])
                    ins = pool.tensor_tensor(b[:, :, s * h2:(s + 1) * h2], x[:, :, (1 - s) * h2:(2 - s) * h2], sin,
                                             ALU.mult)
                step(ins)
                return pool.tensor_tensor(x[:, :, 0:ROT], a, b, ALU.add)

            pool.wait_ge(const_in, 64)
            power(power_no("A", 0), 1)
            for t in range(TILES):
                wait_drained(pool, ("iq", "A", t))
                rotate(q_row[:], AH, t).then_inc(q_roped, 1)
                pool.wait_ge(q_roped, 2 * t + 1)
                pool.wait_ge(rowed, t + 1)
                step(rotate(kv_row[:, HD:4 * HD], 3, t))
                if t:
                    wait_drained(pool, ("index", IH - 1, len(chunks_of(t - 1)) - 1, t - 1))
                pool.tensor_scalar(iw_s[:], kv_row[:, 6 * HD:6 * HD + IH], IH ** -0.5 * HD ** -0.5, None, ALU.mult)
                pool.tensor_copy(kv_row[:, 0:HD], kv_row[:, HD:2 * HD]).then_inc(kv_roped, 1)
                pool.wait_ge(kv_roped, t + 1)
                outs = (k_out, v_out, i_out) if t != SAMPLE else (ks_out, vs_out, is_out)
                n = P if t != SAMPLE else DEC
                for dst, a, b in ((outs[0], 2, 4), (outs[1], 4, 6), (outs[2], 1, 2)):
                    rows = slice(t * P, t * P + n) if t != SAMPLE else slice(0, DEC)
                    pool.dma_start(dst[rows, :], kv_row[0:n, a * HD:b * HD]).then_inc(kv_stored, 16)
                if searched(t):
                    no = len([x for x in range(t) if searched(x)])
                    pool.wait_ge(index_summed, 2 * (no + 1))
                    n = keys_of(t)

                    def guess(ins):
                        guesses[0] += 1
                        ins.then_inc(guess_step, 1)
                        pool.wait_ge(guess_step, guesses[0])

                    guess(pool.tensor_scalar(mean, total, 1.0 / n, None, ALU.mult))
                    guess(pool.tensor_scalar(var, squares, 1.0 / n, None, ALU.mult))
                    guess(pool.tensor_tensor(dev, mean, mean, ALU.mult))
                    guess(pool.tensor_tensor(var, var, dev, ALU.subtract))
                    guess(pool.tensor_scalar(var, var, 1e-30, None, ALU.max))
                    guess(pool.tensor_tensor(dev, var, cst[:, 9:10], ALU.pow))
                    guess(pool.tensor_tensor(slope, dev, cst[:, 29 + 2 * t:30 + 2 * t], ALU.mult))
                    guess(pool.tensor_tensor(above, dev, cst[:, 28 + 2 * t:29 + 2 * t], ALU.mult))
                    pool.tensor_tensor(above, above, mean, ALU.add).then_inc(guessed, 1)
                if t:
                    wait_drained(pool, ("attended", t - 1))
                    pool.dma_start(att_mem[(t - 1) * P:t * P, :], ao).then_inc(ao_stored, 16)
                if t == SAMPLE:
                    pool.dma_start(v_sb[:, 0:NT, :], vc).then_inc(vcache_in, 16)
                wait_drained(pool, ("aq", "A", t))
                rotate(q_row[:], AH, t).then_inc(q_roped, 1)
                pool.wait_ge(q_roped, 2 * t + 2)
                if searched(t):
                    pool.wait_ge(far_ready, no + 1)
                    pool.partition_all_reduce(any_far, far, P, bass.bass_isa.ReduceOp.max).then_inc(any_ready, 1)
                if t + 1 < TILES:
                    power(power_no("A", t + 1), 1)
            wait_drained(pool, ("attended", SAMPLE))
            pool.dma_start(att_mem[SAMPLE * P:TILES * P, :], ao).then_inc(ao_stored, 16)
            power(power_no("R", 0), 1)

            pool.wait_ge(ao_stored, 16 * TILES)
            for dst, src in ((dec_t, decay), (dec_s, decay_sample), (start_t, from_start)):
                pool.dma_start(dst[:].rearrange("p h n -> p (h n)"), src).then_inc(r_const_in, 16)
            pool.dma_start(gn_t[:], gn_row.broadcast_to([P, BW]))\
                .then_inc(r_const_in, 16)
            pool.dma_start(state_s[:], state_ret[0, 0].rearrange("h d e -> d h e")).then_inc(r_const_in, 16)
            pool.dma_start(fg_t[:], fg_row.broadcast_to([P, D])).then_inc(fg_in, 16)

            def load_angles(t):
                pool.dma_start(rot_r[:].rearrange("p a d -> p (a d)"), rope_ret[bass.ds(t * P, P), :])\
                    .then_inc(rot_in, 16)

            def decay_rows(t, col):
                pool.wait_ge(rk_ready, t + 1)
                if not (isinstance(t, int) and t == 0):
                    wait_filled(pool, ("kv", "R", t - 1))
                pool.tensor_tensor(kd_row[:], rk_row[:], cst[:, col:col + RH].unsqueeze(2).broadcast_to([P, RH, RD]),
                                   ALU.mult).then_inc(kd_ready, 1)

            def decay_queries(t):
                wait_drained(pool, ("turn_q", "R", t))
                if not (isinstance(t, int) and t == 0):
                    wait_filled(pool, ("out", "R", t - 1))
                pool.tensor_tensor(rqdT[:], rqT[:], start_t[:], ALU.mult).then_inc(rqd_ready, 1)

            def store_ro(t):
                wait_drained(pool, ("out", "R", t))
                pool.dma_start(ret_mem[bass.ds(t * P, P), :], ro[:].rearrange("p h d -> p (h d)"))\
                    .then_inc(ro_stored, 16)

            load_angles(0)
            pool.wait_ge(r_const_in, R_CONSTS)
            decay_rows(0, 0)
            load_angles(1)
            power(power_no("R", 1), 1)
            decay_queries(0)
            power(power_no("retained", 0), 4)
            store_ro(0)
            with pool.Fori(1, NT) as t:
                decay_rows(t, 0)
                load_angles(t + 1)
                power(power_no("R", t + 1), 1)
                decay_queries(t)
                power(power_no("retained", t), 4)
                store_ro(t)
            wait_drained(pool, ("kv", "R", NT - 1))
            pool.dma_start(ret_p[0, 0].rearrange("h d e -> d h e"), state[:]).then_inc(state_stored, 16)
            decay_rows(SAMPLE, 4)
            power(power_no("O", 0), 1)
            decay_queries(SAMPLE)
            power(power_no("retained", SAMPLE), 4)
            store_ro(SAMPLE)
            wait_drained(pool, ("kv", "R", SAMPLE))
            pool.dma_start(ret_s[0, 0].rearrange("h d e -> d h e"), state_s[:]).then_inc(state_stored, 16)

            def load_mix(t):
                rows = bass.ds(t * P, P)
                pool.dma_start(mixed[:, 0:BW], ret_mem[rows, :]).then_inc(mix_in, 16)
                pool.dma_start(mixed[:, BW:D], att_mem[rows, :]).then_inc(mix_in, 16)

            def load_y(t):
                if isinstance(t, int) and t == SAMPLE:
                    for h in range(2):
                        pool.dma_start(y_row[h * DEC:(h + 1) * DEC, :], xs).then_inc(y_in, 16)
                else:
                    for h in range(2):
                        pool.dma_start(y_row[h * DEC:(h + 1) * DEC, :], xp[bass.ds(t * P + h * DEC, DEC), :])\
                            .then_inc(y_in, 16)

            def finish(t, more=True):
                if more:
                    power(power_no("O", t + 1), 1)
                    wait_filled(pool, ("turn1", "O", t))
                    load_mix(t + 1)
                power(power_no("y", t), 1)
                pool.wait_ge(y_ready, t + 1)
                if isinstance(t, int) and t == SAMPLE:
                    pool.dma_start(y_sample[0], y_row[0:DEC, :]).then_inc(y_stored, 16)
                else:
                    pool.dma_start(y_prompt[0, bass.ds(t * P, P), :], y_row[:]).then_inc(y_stored, 16)
                if more:
                    pool.wait_ge(y_stored, 16 * (t + 1))
                    load_y(t + 1)

            pool.wait_ge(ro_stored, 16 * TILES)
            load_mix(0)
            load_y(0)
            finish(0)
            with pool.Fori(1, NT - 1) as t:
                finish(t)
            finish(NT - 1)
            finish(SAMPLE, more=False)
            pool.wait_ge(y_stored, 16 * TILES)
            pool.wait_ge(state_stored, 32)
            pool.wait_ge(kv_stored, 48 * TILES)


_INS = ["x_prompt", "x_sample", "state_ret", "cache_k", "cache_v", "cache_kidx", "norm_g", "w_in", "ret_gn_g",
        "w_out", "final_g"]
_OUTS = [(1, SEQ, D), (1, DEC, D), (1, 1, RH, RD, RD), (1, 1, SEQ, KVH, HD), (1, 1, SEQ, KVH, HD), (1, 1, SEQ, HD),
         (1, 1, RH, RD, RD), (1, 1, DEC, KVH, HD), (1, 1, DEC, KVH, HD), (1, 1, DEC, HD)]


def kernel(**inputs):
    import concourse.bacc as bacc
    from concourse.bass_utils import run_bass_kernel_spmd

    nc = bacc.Bacc("TRN2", target_bir_lowering=False, num_devices=1)
    arrays, args = {}, []
    given = {n: np.ascontiguousarray(inputs[n]) for n in _INS}
    given["norm_g"] = np.ascontiguousarray(given["norm_g"].reshape(KD, P).T)
    for name, a in {**given, **constants()}.items():
        arrays[f"in_{name}"] = a
        args.append(nc.dram_tensor(f"in_{name}", a.shape, mybir.dt.from_np(a.dtype), kind="ExternalInput").ap())
    for i, shape in enumerate(_OUTS):
        args.append(nc.dram_tensor(f"out_{i}", shape, F32, kind="ExternalOutput").ap())
    hybrid_stream_step(nc, *args)
    r = run_bass_kernel_spmd(nc, [arrays], core_ids=[0])
    return tuple(r.results[0][f"out_{i}"] for i in range(len(_OUTS)))
```

```python
from contextlib import ExitStack
from math import erf, sqrt

import numpy as np

import concourse.bass as bass
from concourse import mybir

F32 = mybir.dt.float32
F32R = mybir.dt.float32r
BF16 = mybir.dt.bfloat16
ALU = mybir.AluOpType
ACT = mybir.ActivationFunctionType
AX_X = mybir.AxisListType.X

P = 128
D = 1024
KD = D // P
SEQ, DEC, PAST = 1024, 64, 1024
CHUNK = 64
NT = SEQ // P
TILES = NT + 1
SAMPLE = NT
RH, RD = 4, 128
AH, HD, KVH = 8, 64, 2
IH = 8
ROT = HD // 4
TOPK = 256
EPS = 1e-6
NB = 8
BW = 512
MASKED = -3.0e38
TAKEN = -3.4e38
BETWEEN = -3.3e38
COUNTS = 5
WINDOW = 16
AIM = TOPK - (WINDOW + 1) / 2
C_RQ, C_RK, C_RV, C_RG = 0, 512, 1024, 1536
C_AQ, C_AK, C_AG, C_IQ, C_IK, C_IW = 2048, 2560, 2816, 3328, 3840, 3904
KVW = 328

LOG_GAMMA = [float(np.log1p(-np.exp2(-5.0 - h))) for h in range(RH)]


def keys_of(t):
    return PAST + DEC if t == SAMPLE else P * (t + 1)


def chunks_of(t):
    n = keys_of(t)
    size = -(-n // (-(-n // BW) * DEC)) * DEC
    return [(c, min(c + size, n)) for c in range(0, n, size)]


def groups_of(t):
    blocks = [(b, min(P, keys_of(t) - b * P)) for b in range(-(-keys_of(t) // P))]
    return [blocks[i:i + 4] for i in range(0, len(blocks), 4)]


BETWEEN_HEADS = {0: "x", 2: "iq", 4: "kv", 6: "turn"}


def attention_order(t):
    scores = lambda h: [("score", h, c) for c in range(len(chunks_of(t)))]
    groups = range(len(groups_of(t)))
    order, last, exps = scores(0) + scores(1) + [("exp", 0, 0), ("exp", 1, 0)], None, 2
    if t != SAMPLE:
        order.append(("between", "aq", t + 1))
    for h in range(AH):
        for g in groups:
            order.append(("turn", h, g))
            if last:
                order.append(("value", *last))
            last = (h, g)
        if exps < min(AH, h + 2):
            order.append(("exp", exps, 0))
            exps += 1
        if h + 2 < AH:
            order += scores(h + 2)
        if t + 2 < TILES and h in BETWEEN_HEADS:
            if exps < min(AH, h + 3):
                order.append(("exp", exps, 0))
                exps += 1
            order.append(("between", BETWEEN_HEADS[h], t + 2))
        elif t + 2 >= TILES:
            order.append(("between", "weights", (t, h)))
            if t == SAMPLE and h == 0:
                order.append(("between", "x_ret", 0))
    return order + [("value", *last)]


def index_order(t):
    return [(h, c) for h in range(IH) for c in range(len(chunks_of(t)))]


SMALL = 28 + 2 * TILES


def searched(t):
    return keys_of(t) > TOPK


def normal_quantile(share):
    low, high = -8.0, 8.0
    for _ in range(60):
        mid = (low + high) / 2
        low, high = (mid, high) if (1 + erf(mid / sqrt(2))) / 2 < share else (low, mid)
    return low


def constants():
    pos = np.concatenate([np.arange(SEQ), PAST + np.arange(DEC), PAST + np.arange(DEC)]).astype(np.float32)

    def angles(half, theta):
        inv = np.power(np.float32(theta), -np.arange(half, dtype=np.float32) / np.float32(half)).astype(np.float32)
        a = (pos[:, None] * inv[None, :]).astype(np.float32)
        return np.cos(a).astype(np.float32), np.sin(a).astype(np.float32)

    c, s = angles(ROT // 2, 500000.0)
    rope_a = np.concatenate([c, c, -s, s], axis=1)
    rope_a = rope_a.reshape(TILES, P, 2 * ROT).transpose(1, 0, 2).reshape(P, -1)
    c, s = angles(RD // 2, 10000.0)
    ks = np.float32(RD ** -0.5)
    rope_r = np.concatenate([c, s, c * ks, s * ks], axis=1)
    lg = np.array(LOG_GAMMA)
    m, n = np.arange(P)[:, None], np.arange(P)[None, :]
    seen = (m // CHUNK) <= (n // CHUNK)
    decay = np.stack([np.where(seen, np.exp(g * np.abs(n - m)), 0.0) for g in lg], 1)
    first = (m < DEC) & (n < 2 * DEC)
    decay_s = np.stack([np.where(first, np.exp(g * np.abs(n % DEC - m)), 0.0) for g in lg], 1)
    from_start = np.stack([np.broadcast_to(np.exp(g * (np.arange(P) + 1)), (P, P)) for g in lg], 1)
    to_end = np.exp(lg[None, :] * (P - 1 - np.arange(P))[:, None])
    to_end_s = np.where(np.arange(P)[:, None] < DEC, np.exp(lg[None, :] * (DEC - 1 - np.arange(P))[:, None]), 0.0)
    small = np.zeros((P, SMALL))
    small[:, 0:4], small[:, 4:8] = to_end, to_end_s
    small[:, 8], small[:, 9], small[:, 10] = -0.5, 0.5, ((WINDOW - 1) / 2) ** 2
    small[:, 12:12 + WINDOW] = np.arange(WINDOW)
    for t in range(TILES):
        if searched(t):
            for rows, n in ((slice(0, CHUNK), keys_of(t) - (CHUNK if t < SAMPLE else 0)), (slice(CHUNK, P), keys_of(t))):
                z = normal_quantile(1 - AIM / n)
                small[rows, 28 + 2 * t] = z
                small[rows, 29 + 2 * t] = np.sqrt(2 * np.pi) * np.exp(z * z / 2) / n
    return {
        "identity": np.eye(P, dtype=np.float32),
        "rope_att": np.ascontiguousarray(rope_a, np.float32),
        "rope_ret": np.ascontiguousarray(rope_r, np.float32),
        "decay": decay.reshape(P, -1).astype(np.float32),
        "decay_sample": decay_s.reshape(P, -1).astype(np.float32),
        "from_start": from_start.reshape(P, -1).astype(np.float32),
        "small": small.astype(np.float32),
    }


def hybrid_stream_step(nc, x_prompt, x_sample, state_ret, cache_k, cache_v, cache_kidx, norm_g, w_in,
                       ret_gn_g, w_out, final_g, identity, rope_att, rope_ret, decay, decay_sample,
                       from_start, small,
                       y_prompt, y_sample, ret_p, k_p, v_p, kidx_p, ret_s, k_s, v_s, kidx_s):
    xp, xs = x_prompt[0], x_sample[0]
    w_rows = w_in[0].rearrange("(k p) n -> p k n", p=P)
    wo_rows = w_out[0].rearrange("(k p) n -> p k n", p=P)
    gn_row = ret_gn_g
    fg_row = final_g.rearrange("(a d) -> a d", a=1)
    kc = cache_k[0, 0].rearrange("(b p) h d -> p b (h d)", p=P)
    vc = cache_v[0, 0].rearrange("(b p) h d -> p b (h d)", p=P)
    ic = cache_kidx[0, 0].rearrange("(b p) d -> p b d", p=P)
    k_out, v_out, i_out = (a[0, 0] for a in (k_p, v_p, kidx_p))
    k_out, v_out = (a.rearrange("t h d -> t (h d)") for a in (k_out, v_out))
    ks_out, vs_out, is_out = (a[0, 0] for a in (k_s, v_s, kidx_s))
    ks_out, vs_out = (a.rearrange("t h d -> t (h d)") for a in (ks_out, vs_out))
    att_mem = nc.dram_tensor("attended", (TILES * P, BW), F32).ap()
    ret_mem = nc.dram_tensor("retained", (TILES * P, BW), F32).ap()

    with ExitStack() as ctx:
        place = [(nc.sbuf_base + 63) // 32 * 32]

        def sb(name, shape, dt=F32, at=None):
            size = int(np.prod(shape[1:])) * (2 if dt == BF16 else 4)
            where = place if at is None else at
            t = nc.alloc_sbuf_tensor_at(name, shape, dt, offset=where[0])
            where[0] += (size + 31) // 32 * 32
            return t

        SLOTS = 4
        where_slots, w_bytes = place[0], KD * BW * 4
        w_hi = [sb(f"w_hi{s}", [P, KD, BW], F32R) for s in range(SLOTS)]
        w_lo = [sb(f"w_lo{s}", [P, KD, BW], F32R) for s in range(SLOTS)]
        EARLY = 4
        at = [where_slots + (SLOTS - 1) * w_bytes]
        early = [sb(f"early{g}", [P, EARLY, BW], at=at) for g in range(2)]
        at = [where_slots + (2 * SLOTS - 1) * w_bytes]
        early += [sb(f"early{g}", [P, EARLY, BW], at=at) for g in range(2, 4)]
        STAGES = 3
        stage = [sb(f"stage{s}", [P, BW]) for s in range(STAGES)]
        ident = sb("ident", [P, P])
        g_in = sb("g_in", [P, KD])
        cst = sb("cst", [P, SMALL])
        ones8 = sb("ones8", [P, KD])
        rope_t = sb("rope_t", [P, TILES, 2 * ROT])
        stats = sb("stats", [P, 2, 6])
        mean2 = sb("mean2", [P, 4])
        mean_sq = sb("mean_sq", [P, 2])
        group_sq = sb("group_sq", [P, 4])
        rstd = sb("rstd", [P, 4])
        xin = sb("xin", [P, D])
        xT_hi = sb("xT_hi", [P, KD, P], F32R)
        xT_lo = sb("xT_lo", [P, KD, P], F32R)
        phase_start = place[0]
        NK = PAST + DEC
        kT_hi, kT_lo = (sb(f"kT_{x}", [P, NK], F32R) for x in ("hi", "lo"))
        kiT_hi, kiT_lo = (sb(f"kiT_{x}", [P, NK], F32R) for x in ("hi", "lo"))
        v_sb = sb("v_sb", [P, TILES, KVH * HD])
        q_row = sb("q_row", [P, BW])
        aq_row = sb("aq_row", [P, BW])
        kv_row = sb("kv_row", [P, 392])
        rope_a, rope_b = (sb(f"rope_{x}", [P, AH, ROT]) for x in "ab")
        iw_s = sb("iw_s", [P, IH])
        iqT_hi, iqT_lo = (sb(f"iqT_{x}", [P, 4, P], F32R) for x in ("hi", "lo"))
        aqT_hi, aqT_lo = (sb(f"aqT_{x}", [P, 4, P], F32R) for x in ("hi", "lo"))
        idx = sb("idx", [P, NK])
        work = sb("work", [P, NK + 8])
        top8 = sb("top8", [P, 8])
        drop8 = sb("drop8", [P, 8])
        found = sb("found", [P, 16])
        total, squares, mean, var, dev, above, slope, seen, over, over_was, far, move, gap, open_, any_far, left = (
            found[:, i:i + 1] for i in range(16))
        bias = sb("bias", [P, NK], BF16)
        probs = [sb(f"probs{i}", [P, NK]) for i in range(2)]
        pT = [sb(f"pT{i}", [P, 4, P]) for i in range(2)]
        low = sb("low", [P, AH, 3])
        den = sb("den", [P, AH])
        rden = sb("rden", [P, AH])
        ao = probs[0][:, 0:BW]
        assert place[0] <= nc.sbuf_usable_end, place[0]
        at = [phase_start]
        rq_row, rk_row, rv_row = (sb(f"{x}_row", [P, RH, RD], at=at) for x in ("rq", "rk", "rv"))
        rtmp = sb("rtmp", [P, RH, RD], at=at)
        kd_row = sb("kd_row", [P, RH, RD], at=at)
        rqT, rkT, rqdT = (sb(f"{x}T", [P, RH, P], at=at) for x in ("rq", "rk", "rqd"))
        rsT = sb("rsT", [P, RH, P], at=at)
        state = sb("state", [P, RH, RD], at=at)
        state_s = sb("state_s", [P, RH, RD], at=at)
        ro = sb("ro", [P, RH, RD], at=at)
        dec_t, dec_s, start_t = (sb(n, [P, RH, P], at=at) for n in ("dec_t", "dec_s", "start_t"))
        gn_t = sb("gn_t", [P, BW], at=at)
        rot_r = sb("rot_r", [P, 4, RD // 2], at=at)
        gate = sb("gate", [P, D], at=at)
        mixed = sb("mixed", [P, D], at=at)
        mT_hi, mT_lo = (sb(f"mT_{x}", [P, KD, P], F32R, at=at) for x in ("hi", "lo"))
        y_row = sb("y_row", [P, D], at=at)
        fg_t = sb("fg_t", [P, D], at=at)
        assert at[0] <= nc.sbuf_usable_end, at[0]

        bank = [ctx.enter_context(nc.psum_tensor(f"bank{b}", [P, BW], F32)) for b in range(NB)]
        filled = [ctx.enter_context(nc.semaphore(f"filled{b}")) for b in range(NB)]
        drained = [ctx.enter_context(nc.semaphore(f"drained{b}")) for b in range(NB)]

        def sem(name):
            return ctx.enter_context(nc.semaphore(name))

        const_in = sem("const_in")
        x_in = sem("x_in")
        stage_in = [sem(f"stage_in{i}") for i in range(STAGES)]
        early_in = [sem(f"early_in{g}") for g in range(4)]
        vcache_in = sem("vcache_in")
        w_rounded = sem("w_rounded")
        w_split = sem("w_split")
        stat_done = sem("stat_done")
        ms_ready = sem("ms_ready")
        rstd_ready = sem("rstd_ready")
        xn_ready = sem("xn_ready")
        hi_ready = sem("hi_ready")
        rowed = sem("rowed")
        rope_step = sem("rope_step")
        q_roped = sem("q_roped")
        kv_roped = sem("kv_roped")
        kv_stored = sem("kv_stored")
        relued = sem("relued")
        index_summed = sem("index_summed")
        guess_step = sem("guess_step")
        guessed = sem("guessed")
        far_ready = sem("far_ready")
        any_ready = sem("any_ready")
        whole_step = sem("whole_step")
        ones_ready = sem("ones_ready")
        value_done = sem("value_done")
        topk_step = sem("topk_step")
        exped = sem("exped")
        ao_step = sem("ao_step")
        ao_stored = sem("ao_stored")
        r_const_in = sem("r_const_in")
        rot_in = sem("rot_in")
        rq_ready, rk_ready = sem("rq_ready"), sem("rk_ready")
        kd_ready = sem("kd_ready")
        rqd_ready = sem("rqd_ready")
        squared = sem("squared")
        ro_stored = sem("ro_stored")
        state_zero = sem("state_zero")
        state_stored = sem("state_stored")
        mix_in = sem("mix_in")
        y_in = sem("y_in")
        gated = sem("gated")
        mixed_ready = sem("mixed_ready")
        summed = sem("summed")
        y_ready = sem("y_ready")
        y_stored = sem("y_stored")
        fg_in = sem("fg_in")

        uses = [0] * NB
        use = {}
        turn = [0]

        def take(key, b=None):
            if b is None:
                b = turn[0] % (NB - 1)
                turn[0] += 1
            use[key] = (b, uses[b])
            uses[b] += 1

        def take_turned(t):
            take(("turn_iq", "A", t))
            take(("turn_kv", "A", t))

        def take_attention(t):
            for step in attention_order(t):
                if step[:2] in (("between", "x"), ("between", "x_ret")):
                    for half in range(2):
                        take((f"x{half}", "A" if step[1] == "x" else "R", step[2]))
                elif step[:2] == ("between", "turn"):
                    take_turned(step[2])
                elif step[0] == "between" and step[1] != "weights":
                    take((step[1], "A", step[2]))
                elif step[0] in ("score", "turn"):
                    take((*step, t))
            take(("attended", t), NB - 1)

        def take_rows(t):
            for s in ("x0", "x1", "iq", "kv"):
                take((s, "A", t))
            take_turned(t)

        take_rows(0)
        for t in range(TILES):
            for h, c in index_order(t):
                take(("index", h, c, t))
            if t:
                take_attention(t - 1)
            else:
                take(("aq", "A", 0))
                take_rows(1)
            take(("turn_aq", "A", t))
            for name in ("turn_ci",) * (t == NT - 1) + ("turn_ck",) * (t == SAMPLE):
                take((name, 0))
                take((name, 1))
        take_attention(SAMPLE)
        base_r = list(uses)
        for b in (3, 4):
            base_r[b] -= 1
        R_BANK = {"q": (0, 0), "k": (1, 0), "v": (2, 0), "x0": (3, 0), "x1": (4, 0), "turn_q": (5, 0),
                  "turn_k": (6, 0), "kv": (6, 1), "scores": (7, 0), "out": (7, 1)}
        R_USES = [1, 1, 1, 1, 1, 1, 2, 2]
        base_o = [b + TILES * u for b, u in zip(base_r, R_USES)]
        O_BANK = {"rg": 0, "ag": 1, "y1": 2, "x0": 3, "x1": 4, "turn0": 5, "turn1": 6, "y0": 7}

        def bank_use(key):
            if isinstance(key[-1], int) and key in use:
                return use[key]
            if key[-2:-1] == ("R",):
                b, k = R_BANK[key[0]]
                return b, base_r[b] + key[-1] * R_USES[b] + k
            if key[-2:-1] == ("O",):
                return O_BANK[key[0]], base_o[O_BANK[key[0]]] + key[-1]
            raise KeyError(key)

        def of(key):
            return bank[bank_use(key)[0]]

        def wait_filled(eng, key):
            b, n = bank_use(key)
            eng.wait_ge(filled[b], n + 1)

        def wait_drained(eng, key):
            b, n = bank_use(key)
            eng.wait_ge(drained[b], n + 1)

        def wait_free(eng, key):
            b, n = bank_use(key)
            if not (isinstance(n, int) and n == 0):
                eng.wait_ge(drained[b], n)

        def fills(key):
            return filled[bank_use(key)[0]], 1

        def drains(key):
            return drained[bank_use(key)[0]], 1

        R_HI, O_HI = 2, 4
        hi_order = [(s, 0) for s in ("x0", "x1", "turn_iq", "turn_kv")]
        for t in range(TILES):
            if t + 1 < TILES:
                hi_order += [(s, t + 1) for s in ("x0", "x1", "turn_iq", "turn_kv")]
            hi_order.append(("turn_aq", t))
            if t >= NT - 1:
                hi_order += [(("ci" if t == NT - 1 else "ck") + half, t) for half in "01"]
        hi_at = {(s, "A", t): i + 1 for i, (s, t) in enumerate(hi_order)}
        n = len(hi_order)
        hi_r = n
        hi_o = hi_r + R_HI * TILES

        def hi_no(s, phase, t):
            if phase == "A":
                return hi_at[s, "A", t]
            if phase == "R":
                return hi_r + t * R_HI + {"x0": 1, "x1": 2}[s]
            half = int(s[-1])
            if s.startswith("x"):
                return hi_o + half + (2 * t + 1 if isinstance(t, int) and t < 2 else O_HI * t - 1)
            return hi_o + half + (O_HI * t + 3 if isinstance(t, int) and t == SAMPLE else O_HI * t + 5)

        index_no, group_no, value_no, n, v = {}, {}, {}, 0, 0
        for t in range(TILES):
            for h, c in index_order(t):
                n += 1
                index_no[t, h, c] = n
        for t in range(TILES):
            for kind, h, g in attention_order(t):
                if kind == "value":
                    group_no[t, h, g] = len(group_no)
                    if (h, g) != (AH - 1, len(groups_of(t)) - 1):
                        v += 1
                        value_no[group_no[t, h, g]] = v
                    else:
                        value_no[group_no[t, h, g]] = ("attended", t)

        def wait_value(eng, no):
            if no >= 0:
                if isinstance(value_no[no], int):
                    eng.wait_ge(value_done, value_no[no])
                else:
                    wait_filled(eng, value_no[no])

        def last_score(t, h):
            return ("score", h, len(chunks_of(t)) - 1, t)

        def stat_no(what, t):
            if what == "y":
                return 35 if isinstance(t, int) and t == SAMPLE else 34 if isinstance(t, int) and t == NT - 1 else 21 + 2 * t
            if what == "O":
                return 18 + t if isinstance(t, int) and t < 2 else 16 + 2 * t
            return NORM[what] + t

        def power_no(what, t):
            if what == "y":
                return 44 if isinstance(t, int) and t == SAMPLE else 43 if isinstance(t, int) and t == NT - 1 else 30 + 2 * t
            if what == "O":
                return 25 + 2 * t
            if what == "retained":
                return 12 + 2 * t
            if what == "R":
                return TILES + t if isinstance(t, int) and t < 2 else 7 + 2 * t
            return t

        R_CONSTS = 16 * 5
        NORM = {"A": 0, "R": TILES, "O": 2 * TILES}

        def slot_items(slot, what):
            return [(slot, what, k) for k in range(KD)]

        items = (slot_items(0, "iq") + slot_items(1, "kv") + slot_items(2, "aq") + slot_items(3, "rq")
                 + [(None, "ci", half) for half in range(2)] + slot_items(0, "rk") + slot_items(1, "rv")[:4]
                 + [(None, "ck", half) for half in range(2)] + slot_items(1, "rv")[4:] + slot_items(2, "rg") + slot_items(3, "ag") + slot_items(0, "wo0")
                 + slot_items(1, "wo1"))
        COLS = {"iq": [(C_IQ, 0, BW)], "kv": [(C_IK, 0, HD), (C_AK, HD, 2 * KVH * HD), (C_IW, HD + 2 * KVH * HD, IH)],
                "aq": [(C_AQ, 0, BW)], "rq": [(C_RQ, 0, BW)], "rk": [(C_RK, 0, BW)], "rv": [(C_RV, 0, BW)],
                "rg": [(C_RG, 0, BW)], "ag": [(C_AG, 0, BW)], "wo0": [(0, 0, BW)], "wo1": [(BW, 0, BW)]}
        item_no = {(w, k): i for i, (_, w, k) in enumerate(items)}
        N_EARLY = item_no["rq", 0]

        def raw(i):
            return early[i // EARLY % 4][:, i % EARLY, :] if i < N_EARLY else stage[i % STAGES]

        count = {}

        def staged_at(i):
            slot, w, _ = items[i]
            s = early_in[i // EARLY % 4] if i < N_EARLY else stage_in[i % STAGES]
            if i >= N_EARLY or i % EARLY == 0:
                count[s.name] = count.get(s.name, 0) + 16 * (len(COLS[w]) if slot is not None else 2 if w == "ci" else 1)
            return s, count[s.name]

        staged = [staged_at(i) for i in range(len(items))]
        split_no, n = {}, 0
        for slot, w, k in items:
            if slot is not None:
                n += 1
                split_no[w, k] = n
        slot_free = {"rk": ("iq", "A", SAMPLE), "rv": ("kv", "A", SAMPLE), "rg": ("aq", "A", SAMPLE),
                     "ag": ("q", "R", SAMPLE), "wo0": ("k", "R", SAMPLE), "wo1": ("v", "R", SAMPLE)}
        SLOT = {w: slot for slot, w, _ in items}
        WIDTH = {w: sum(c[2] for c in COLS[w]) for w in COLS}
        late = [(w, k) for w in ("rk", "rv", "rg") for k in range(KD)]
        cut = late.index(("rv", 4))
        late_at = {(t, h): part[h * n:(h + 1) * n] for t, part, n in ((NT - 1, late[:cut], 2), (SAMPLE, late[cut:], 2))
                   for h in range(AH)}

        block = ctx.enter_context(nc.Block())

        @block.sync
        def _(sp):
            def load(i):
                slot, w, k = items[i]
                buf, (done, _) = raw(i), staged[i]
                if i >= N_EARLY + STAGES:
                    slot2, w2, k2 = items[i - STAGES]
                    if slot2 is None:
                        wait_filled(sp, ("turn_" + w2, k2))
                    else:
                        sp.wait_ge(w_split, split_no[w2, k2])
                if w == "ci":
                    dst = buf[:].rearrange("p (b h d) -> p b h d", h=2, d=HD)
                    for half in range(2):
                        sp.dma_start(dst[:, :, half, :], ic[:, 4 * k:4 * k + 4, :]).then_inc(done, 16)
                elif w == "ck":
                    sp.dma_start(buf[:].rearrange("p (b n) -> p b n", n=P), kc[:, 4 * k:4 * k + 4, :])\
                      .then_inc(done, 16)
                else:
                    rows = wo_rows if w.startswith("wo") else w_rows
                    for src, dst, n in COLS[w]:
                        sp.dma_start(buf[:, dst:dst + n], rows[:, k, src:src + n]).then_inc(done, 16)

            def load_early(w):
                for k in range(0, KD, EARLY):
                    i = item_no[w, k]
                    if i >= 4 * EARLY:
                        _, w2, k2 = items[i - 3 * EARLY - 1]
                        sp.wait_ge(w_split, split_no[w2, k2])
                    for src, dst, n in COLS[w]:
                        sp.dma_start(early[i // EARLY % 4][:, :, dst:dst + n], w_rows[:, k:k + EARLY, src:src + n])\
                          .then_inc(staged[i][0], 16)

            def load_x(phase, t, wait=True):
                if wait:
                    prev = {"A": None, "R": ("x1", "A", SAMPLE), "O": ("x1", "R", SAMPLE)}[phase]
                    if not (isinstance(t, int) and t == 0):
                        prev = ("x1", phase, t - 1)
                    if prev:
                        wait_filled(sp, prev)
                for half in range(2):
                    src = xs if isinstance(t, int) and t == SAMPLE else xp[bass.ds(t * P + half * DEC, DEC), :]
                    sp.dma_start(xin[half * DEC:(half + 1) * DEC, :], src).then_inc(x_in, 16)

            def load_y(t):
                if not (isinstance(t, int) and t == 0):
                    sp.wait_ge(y_stored, 16 * t)
                for half in range(2):
                    src = xs if isinstance(t, int) and t == SAMPLE else xp[bass.ds(t * P + half * DEC, DEC), :]
                    sp.dma_start(y_row[half * DEC:(half + 1) * DEC, :], src).then_inc(y_in, 16)

            load_x("A", 0)
            sp.dma_start(cst[:], small).then_inc(const_in, 16)
            sp.dma_start(g_in[:], norm_g).then_inc(const_in, 16)
            sp.dma_start(ident[:], identity).then_inc(const_in, 16)
            sp.dma_start(rope_t[:], rope_att.rearrange("p (t n) -> p t n", n=2 * ROT)).then_inc(const_in, 16)
            load_early("iq")
            load_early("kv")
            load_x("A", 1)
            load_early("aq")
            for k in range(STAGES):
                load(item_no["rq", k])
            for t in range(2, TILES):
                load_x("A", t)
                for i in {4: (27, 28), 5: (29, 30), 6: (31,), 7: (32, 33, 34)}.get(t, ()):
                    load(i)
            load_x("R", 0)
            for i in range(item_no["rk", 1], item_no["ag", 0]):
                load(i)
            with sp.Fori(1, NT) as t:
                load_x("R", t)
            load_x("R", SAMPLE)
            load_x("O", 0)
            for k in range(KD):
                load(item_no["ag", k])
            load_x("O", 1)
            load_y(0)
            for k in range(KD):
                load(item_no["wo0", k])
            load_x("O", 2)
            for k in range(KD):
                load(item_no["wo1", k])
            with sp.Fori(3, NT) as t:
                load_x("O", t)
                load_y(t - 2)
            load_x("O", SAMPLE)
            for t in (NT - 2, NT - 1, SAMPLE):
                load_y(t)

        @block.tensor
        def _(pe):
            def turn_x(phase, t):
                pe.wait_ge(xn_ready, NORM[phase] + t + 1)
                for half in range(2):
                    key = (f"x{half}", phase, t)
                    wait_free(pe, key)
                    for j in range(4):
                        k = 4 * half + j
                        mm = pe.transpose(of(key)[:, j * P:(j + 1) * P], xin[:, k * P:(k + 1) * P], ident[:])
                    mm.then_inc(*fills(key))

            def x_turned(phase, t):
                for half in range(2):
                    wait_drained(pe, (f"x{half}", phase, t))

            def product(key, slot, width, hi, lo, w=None):
                wait_free(pe, key)
                out = of(key)[:, 0:width]
                for k in range(KD):
                    if w:
                        pe.wait_ge(w_split, split_no[w, k])
                    wh, wl = w_hi[slot][:, k, 0:width], w_lo[slot][:, k, 0:width]
                    pe.matmul(out, hi[:, k, :], wh, start=(k == 0), stop=False)
                    pe.matmul(out, hi[:, k, :], wl, start=False, stop=False)
                    mm = pe.matmul(out, lo[:, k, :], wh, start=False, stop=(k == KD - 1))
                mm.then_inc(*fills(key))

            def project(name, w, phase, t, first):
                product((name, phase, t), SLOT[w], WIDTH[w], xT_hi, xT_lo, w if first else None)

            def turn_rows(key, rows, n):
                wait_free(pe, key)
                for j in range(n):
                    mm = pe.transpose(of(key)[:, j * P:(j + 1) * P], rows[:, j * P:(j + 1) * P], ident[:])
                mm.then_inc(*fills(key))

            def turn_cached(cache):
                for half in range(2):
                    i = item_no[cache, half]
                    pe.wait_ge(*staged[i])
                    turn_rows(("turn_" + cache, half), raw(i), 4)

            def three(out, a_hi, a_lo, b_hi, b_lo):
                pe.matmul(out, a_hi, b_hi, start=True, stop=False)
                pe.matmul(out, a_hi, b_lo, start=False, stop=False)
                return pe.matmul(out, a_lo, b_hi, start=False, stop=True)

            def index(t):
                wait_drained(pe, ("turn_iq", "A", t))
                wait_drained(pe, ("turn_kv", "A", t))
                if t == SAMPLE:
                    for half in range(2):
                        wait_drained(pe, ("turn_ci", half))
                for h, c in index_order(t):
                    a, b = chunks_of(t)[c]
                    r = slice(HD * (h % 2), HD * (h % 2) + HD)
                    key = ("index", h, c, t)
                    wait_free(pe, key)
                    three(of(key)[:, 0:b - a], iqT_hi[r, h // 2, :], iqT_lo[r, h // 2, :],
                          kiT_hi[r, a:b], kiT_lo[r, a:b]).then_inc(*fills(key))

            def turn_a(t):
                pe.wait_ge(q_roped, 2 * t + 1)
                turn_rows(("turn_iq", "A", t), q_row, 4)
                pe.wait_ge(kv_roped, t + 1)
                turn_rows(("turn_kv", "A", t), kv_row, 2)

            def between(name, t):
                if name == "x":
                    turn_x("A", t)
                elif name == "iq":
                    x_turned("A", t)
                    project("iq", "iq", "A", t, t == 0)
                elif name == "kv":
                    project("kv", "kv", "A", t, t == 0)
                elif name == "turn":
                    turn_a(t)
                elif name == "aq":
                    project("aq", "aq", "A", t, t == 0)
                elif name == "x_ret":
                    turn_x("R", 0)

            def attend(t):
                wait_drained(pe, ("turn_aq", "A", t))
                if t == SAMPLE:
                    for half in range(2):
                        wait_drained(pe, ("turn_ck", half))
                for kind, h, n in attention_order(t):
                    if kind == "between":
                        between(h, n)
                    if kind in ("between", "exp"):
                        continue
                    kv = h // (AH // KVH)
                    key = (kind, h, n, t)
                    if kind == "score":
                        a, b = chunks_of(t)[n]
                        r = slice(HD * kv, HD * kv + HD)
                        wait_free(pe, key)
                        three(of(key)[:, 0:b - a], aqT_hi[r, h % 4, :], aqT_lo[r, h % 4, :],
                              kT_hi[r, a:b], kT_lo[r, a:b]).then_inc(*fills(key))
                    elif kind == "turn":
                        pe.wait_ge(exped, AH * t + h + 1)
                        wait_free(pe, key)
                        for j, (blk, rows) in enumerate(groups_of(t)[n]):
                            mm = pe.transpose(of(key)[0:rows, j * P:(j + 1) * P],
                                              probs[h % 2][:, blk * P:blk * P + rows], ident[:])
                        mm.then_inc(*fills(key))
                    else:
                        wait_drained(pe, ("turn", h, n, t))
                        if h == 0 and n == 0:
                            wait_free(pe, ("attended", t))
                            if t == SAMPLE:
                                pe.wait_ge(vcache_in, 16)
                        for j, (blk, rows) in enumerate(groups_of(t)[n]):
                            last = blk == len([1 for g in groups_of(t) for _ in g]) - 1
                            mm = pe.matmul(of(("attended", t))[:, h * HD:(h + 1) * HD],
                                           pT[group_no[t, h, n] % 2][0:rows, j, :],
                                           v_sb[0:rows, blk, kv * HD:(kv + 1) * HD],
                                           start=(blk == 0), stop=last)
                        if last:
                            if h == AH - 1:
                                mm.then_inc(*fills(("attended", t)))
                            else:
                                mm.then_inc(value_done, 1)
                        else:
                            mm.then_inc(value_done, 1)

            pe.wait_ge(const_in, 64)
            for name in BETWEEN_HEADS.values():
                between(name, 0)
            for t in range(TILES):
                index(t)
                if t:
                    attend(t - 1)
                else:
                    between("aq", 0)
                    for name in BETWEEN_HEADS.values():
                        between(name, 1)
                pe.wait_ge(q_roped, 2 * t + 2)
                turn_rows(("turn_aq", "A", t), aq_row, 4)
                if t == NT - 1:
                    turn_cached("ci")
                if t == SAMPLE:
                    turn_cached("ck")
            attend(SAMPLE)

            def retain(t, st, ahead, first=False):
                pe.wait_ge(rq_ready, t + 1)
                turn_rows(("turn_q", "R", t), rq_row[:].rearrange("p h d -> p (h d)"), 4)
                pe.wait_ge(rk_ready, t + 1)
                turn_rows(("turn_k", "R", t), rk_row[:].rearrange("p h d -> p (h d)"), 4)
                ahead[0]()
                wait_drained(pe, ("turn_q", "R", t))
                wait_drained(pe, ("turn_k", "R", t))
                key = ("scores", "R", t)
                wait_free(pe, key)
                for h in range(RH):
                    mm = pe.matmul(of(key)[:, h * P:(h + 1) * P], rkT[:, h, :], rqT[:, h, :], start=True, stop=True)
                mm.then_inc(*fills(key))
                pe.wait_ge(kd_ready, t + 1)
                wait_drained(pe, ("v", "R", t))
                key = ("kv", "R", t)
                wait_free(pe, key)
                for h in range(RH):
                    mm = pe.matmul(of(key)[:, h * RD:(h + 1) * RD], kd_row[:, h, :], rv_row[:, h, :],
                                   start=True, stop=True)
                mm.then_inc(*fills(key))
                ahead[1]()
                pe.wait_ge(rqd_ready, t + 1)
                if isinstance(t, int) and t == SAMPLE:
                    pe.wait_ge(r_const_in, R_CONSTS)
                elif first:
                    pe.wait_ge(state_zero, 1)
                else:
                    wait_drained(pe, ("kv", "R", t - 1))
                wait_drained(pe, ("scores", "R", t))
                key = ("out", "R", t)
                wait_free(pe, key)
                for h in range(RH):
                    out = of(key)[:, h * RD:(h + 1) * RD]
                    pe.matmul(out, rqdT[:, h, :], st[:, h, :], start=True, stop=False)
                    mm = pe.matmul(out, rsT[:, h, :], rv_row[:, h, :], start=False, stop=True)
                mm.then_inc(*fills(key))
                ahead[2]()

            def project_r(name, t, first=False):
                project(name, f"r{name}", "R", t, first)

            def retain_tile(t, first=False):
                def next_q():
                    x_turned("R", t + 1)
                    project_r("q", t + 1)

                retain(t, state, (next_q, lambda: project_r("k", t + 1), lambda: project_r("v", t + 1)), first)

            x_turned("R", 0)
            for name in "qkv":
                project_r(name, 0, True)
            turn_x("R", 1)
            retain_tile(0, True)
            turn_x("R", 2)
            with pe.Fori(1, NT - 1) as t:
                retain_tile(t)
                turn_x("R", t + 2)
            retain_tile(NT - 1)
            turn_x("O", 0)

            def first_gate():
                x_turned("O", 0)
                project("rg", "rg", "O", 0, True)

            retain(SAMPLE, state_s, (first_gate, lambda: None, lambda: project("ag", "ag", "O", 0, True)))
            turn_x("O", 1)

            def turn_mixed(t):
                for half in range(2):
                    pe.wait_ge(mixed_ready, 2 * t + half + 1)
                    turn_rows((f"turn{half}", "O", t), mixed[:, half * BW:(half + 1) * BW], 4)

            def out_tile(t, first=False, gates=True, x=True, t_last=False):
                if gates:
                    x_turned("O", t + 1)
                    project("rg", "rg", "O", t + 1, False)
                    turn_mixed(t)
                    project("ag", "ag", "O", t + 1, False)
                if x:
                    turn_x("O", t + 2)
                for half in range(2):
                    wait_drained(pe, (f"turn{half}", "O", t))
                for half in range(2):
                    product((f"y{half}", "O", t), SLOT[f"wo{half}"], BW, mT_hi, mT_lo,
                            f"wo{half}" if first else None)
                    if t_last and half == 0:
                        turn_mixed(SAMPLE)

            out_tile(0, first=True)
            with pe.Fori(1, NT - 1) as t:
                out_tile(t)
            out_tile(NT - 1, x=False, t_last=True)
            out_tile(SAMPLE, gates=False, x=False)

        @block.scalar
        def _(act):
            def round_w(w, k):
                i = item_no[w, k]
                act.wait_ge(*staged[i])
                if w == "rq":
                    act.wait_ge(w_split, N_EARLY)
                if w in slot_free:
                    wait_filled(act, slot_free[w])
                g = ones8 if w.startswith("wo") else g_in
                act.activation(w_hi[SLOT[w]][:, k, 0:WIDTH[w]], raw(i)[:, 0:WIDTH[w]],
                               ACT.Identity, scale=g[:, k:k + 1]).then_inc(w_rounded, 1)

            def hi(key, dst, src=None):
                wait_filled(act, key)
                act.copy(dst, of(key)[:] if src is None else src).then_inc(hi_ready, 1)

            def hi_x(phase, t):
                for half in range(2):
                    hi((f"x{half}", phase, t), xT_hi[:, 4 * half:4 * half + 4, :].rearrange("p k n -> p (k n)"))

            def between(name, t):
                if name == "x":
                    hi_x("A", t)
                elif name == "iq":
                    key = ("iq", "A", t)
                    wait_filled(act, key)
                    if t:
                        wait_filled(act, ("turn_iq", "A", t - 1))
                    act.copy(q_row[:], of(key)[:]).then_inc(*drains(key))
                elif name == "kv":
                    key = ("kv", "A", t)
                    wait_filled(act, key)
                    if t:
                        wait_filled(act, ("turn_kv", "A", t - 1))
                        act.wait_ge(kv_stored, 48 * t)
                    act.copy(kv_row[:, HD:HD + KVW], of(key)[:, 0:KVW]).then_inc(rowed, 1)
                    n = DEC if t == SAMPLE else P
                    act.copy(v_sb[0:n, t, :], of(key)[0:n, 3 * HD:5 * HD]).then_inc(*drains(key))
                elif name == "turn":
                    hi(("turn_iq", "A", t), iqT_hi[:].rearrange("p k n -> p (k n)"))
                    key = ("turn_kv", "A", t)
                    n = DEC if t == SAMPLE else P
                    wait_filled(act, key)
                    act.copy(kiT_hi[:, t * P:t * P + n], of(key)[:, 0:n])
                    act.copy(kT_hi[:, t * P:t * P + n], of(key)[:, P:P + n]).then_inc(hi_ready, 1)
                elif name == "x_ret":
                    hi_x("R", 0)
                elif name == "aq":
                    key = ("aq", "A", t)
                    wait_filled(act, key)
                    if t:
                        wait_filled(act, ("turn_aq", "A", t - 1))
                    act.copy(aq_row[:].rearrange("p (j a d) -> p a j d", a=2, d=HD),
                             of(key)[:].rearrange("p (a j d) -> p a j d", a=2, d=HD)).then_inc(*drains(key))
                elif name == "weights":
                    for w, k in late_at[t]:
                        round_w(w, k)

            def attend(t):
                for kind, h, g in attention_order(t):
                    if kind == "between":
                        between(h, g)
                    elif kind == "exp":
                        g = len(chunks_of(t)) - 1
                        wait_drained(act, last_score(t, h))
                        act.activation(probs[h % 2][:, 0:keys_of(t)], probs[h % 2][:, 0:keys_of(t)], ACT.Exp,
                                       bias=low[:, h, g:g + 1], scale=-1.0,
                                       accum_out=den[:, h:h + 1]).then_inc(exped, 1)
                    elif kind == "turn":
                        key = ("turn", h, g, t)
                        n = group_no[t, h, g]
                        wait_filled(act, key)
                        wait_value(act, n - 2)
                        grp = groups_of(t)[g]
                        full = [x for x in grp if x[1] == P]
                        if full:
                            ins = act.copy(pT[n % 2][:, 0:len(full), :],
                                           of(key)[:, 0:len(full) * P].rearrange("p (j n) -> p j n", n=P))
                        if len(full) < len(grp):
                            ins = act.copy(pT[n % 2][0:grp[-1][1], len(full), :],
                                           of(key)[0:grp[-1][1], len(full) * P:(len(full) + 1) * P])
                        ins.then_inc(*drains(key))

            act.wait_ge(const_in, 64)
            act.wait_ge(ones_ready, 1)
            for w in ("iq", "kv"):
                for k in range(KD):
                    round_w(w, k)
                    if (w, k) == ("iq", 1):
                        between("x", 0)
            between("iq", 0)
            between("kv", 0)
            for k in range(KD):
                round_w("aq", k)
            between("turn", 0)
            for t in range(TILES):
                for h, c in index_order(t):
                    a, b = chunks_of(t)[c]
                    key = ("index", h, c, t)
                    wait_filled(act, key)
                    act.activation(of(key)[:, 0:b - a], of(key)[:, 0:b - a], ACT.Relu).then_inc(relued, 1)
                if searched(t):
                    n = keys_of(t)
                    wait_drained(act, ("index", IH - 1, len(chunks_of(t)) - 1, t))
                    no = len([x for x in range(t) if searched(x)])
                    act.activation(work[:, 0:n], idx[:, 0:n], ACT.Identity, accum_out=total).then_inc(index_summed, 1)
                    act.wait_ge(index_summed, 2 * no + 1)
                    act.activation(work[:, 0:n], idx[:, 0:n], ACT.Square, accum_out=squares)\
                       .then_inc(index_summed, 1)
                if t:
                    attend(t - 1)
                else:
                    between("aq", 0)
                    for name in BETWEEN_HEADS.values():
                        between(name, 1)
                hi(("turn_aq", "A", t), aqT_hi[:].rearrange("p k n -> p (k n)"))
                for cache, dst in (("ci", kiT_hi),) * (t == NT - 1) + (("ck", kT_hi),) * (t == SAMPLE):
                    for half in range(2):
                        hi(("turn_" + cache, half), dst[:, half * BW:(half + 1) * BW])
                if 2 <= t <= 5:
                    for k in range(2 * t - 4, 2 * t - 2):
                        round_w("rq", k)
            attend(SAMPLE)

            def retained(t):
                key = ("v", "R", t)
                wait_filled(act, key)
                if isinstance(t, int) and t == 0:
                    act.wait_ge(ao_stored, 16 * TILES)
                else:
                    wait_filled(act, ("out", "R", t - 1))
                act.copy(rv_row[:].rearrange("p h d -> p (h d)"), of(key)[:]).then_inc(*drains(key))

            def turned(t):
                key = ("turn_q", "R", t)
                wait_filled(act, key)
                act.copy(rqT[:].rearrange("p h d -> p (h d)"), of(key)[:]).then_inc(*drains(key))
                key = ("turn_k", "R", t)
                wait_filled(act, key)
                act.copy(rkT[:].rearrange("p h d -> p (h d)"), of(key)[:]).then_inc(*drains(key))

            def square(t):
                key = ("out", "R", t)
                wait_filled(act, key)
                if not (isinstance(t, int) and t == 0):
                    act.wait_ge(ro_stored, 16 * t)
                for h in range(RH):
                    ins = act.activation(ro[:, h, :], of(key)[:, h * RD:(h + 1) * RD], ACT.Square,
                                         accum_out=group_sq[:, h:h + 1])
                ins.then_inc(squared, 1)

            retained(0)
            hi_x("R", 1)
            turned(0)
            square(0)
            retained(1)
            hi_x("R", 2)
            with act.Fori(1, NT - 1) as t:
                turned(t)
                square(t)
                retained(t + 1)
                hi_x("R", t + 2)
            turned(NT - 1)
            for k in range(4):
                round_w("ag", k)
            square(NT - 1)
            retained(SAMPLE)
            hi_x("O", 0)
            for k in range(4, KD):
                round_w("ag", k)
            turned(SAMPLE)
            for k in range(4):
                round_w("wo0", k)

            def gates(t):
                for half, name in enumerate(("rg", "ag")):
                    key = (name, "O", t)
                    wait_filled(act, key)
                    if not (isinstance(t, int) and t == 0):
                        act.wait_ge(mixed_ready, 2 * t - 1 + half)
                    act.activation(gate[:, half * BW:(half + 1) * BW], of(key)[:], ACT.Silu)\
                       .then_inc(*drains(key))

            def hi_mixed(t):
                for half in range(2):
                    hi((f"turn{half}", "O", t), mT_hi[:, 4 * half:4 * half + 4, :].rearrange("p k n -> p (k n)"))

            square(SAMPLE)
            gates(0)
            hi_x("O", 1)
            for k in range(4, KD):
                round_w("wo0", k)
            hi_mixed(0)
            for k in range(KD):
                round_w("wo1", k)
            gates(1)
            hi_x("O", 2)
            with act.Fori(1, NT - 1) as t:
                hi_mixed(t)
                gates(t + 1)
                hi_x("O", t + 2)
            hi_mixed(NT - 1)
            gates(SAMPLE)
            wait_filled(act, ("y1", "O", NT - 1))
            hi_mixed(SAMPLE)

        @block.vector
        def _(dve):
            def split_w(w, k):
                i = item_no[w, k]
                dve.wait_ge(w_rounded, split_no[w, k])
                g = ones8 if w.startswith("wo") else g_in
                dve.scalar_tensor_tensor(
                    out=w_lo[SLOT[w]][:, k, 0:WIDTH[w]], in0=raw(i)[:, 0:WIDTH[w]],
                    scalar=g[:, k:k + 1], in1=w_hi[SLOT[w]][:, k, 0:WIDTH[w]].bitcast(F32),
                    op0=ALU.mult, op1=ALU.subtract).then_inc(w_split, 1)

            STAT = 4

            def mean_square(rows, no):
                for half in range(2):
                    ins = dve.bn_stats(stats[:, half, :], rows[:, half * BW:(half + 1) * BW])
                ins.then_inc(stat_done, 1)
                parts = stats[:].rearrange("p a (b c) -> p (a b) c", c=3)
                dve.wait_ge(stat_done, STAT * no + 1)
                dve.tensor_tensor(mean2[:], parts[:, :, 1], parts[:, :, 1], ALU.mult).then_inc(stat_done, 1)
                dve.wait_ge(stat_done, STAT * no + 2)
                dve.scalar_tensor_tensor(out=mean2[:], in0=parts[:, :, 2], scalar=4.0 / D, in1=mean2[:],
                                         op0=ALU.mult, op1=ALU.add).then_inc(stat_done, 1)
                dve.wait_ge(stat_done, STAT * no + 3)
                dve.tensor_reduce(mean_sq[:, 0:1], mean2[:], AX_X, ALU.add).then_inc(stat_done, 1)
                dve.wait_ge(stat_done, STAT * no + 4)
                dve.tensor_scalar(mean_sq[:, 1:2], mean_sq[:, 0:1], 0.25, EPS, ALU.mult, ALU.add)\
                   .then_inc(ms_ready, 1)

            def normalise(phase, t):
                n = NORM[phase] + t
                dve.wait_ge(x_in, 32 * (n + 1))
                mean_square(xin, stat_no(phase, t))
                dve.wait_ge(rstd_ready, power_no(phase, t) + 1)
                dve.tensor_scalar(xin[:], xin[:], rstd[:, 0:1], None, ALU.mult).then_inc(xn_ready, 1)

            def lo(key, hi_index, dst, hi, src=None):
                dve.wait_ge(hi_ready, hi_index)
                dve.tensor_tensor(dst, of(key)[:] if src is None else src, hi.bitcast(F32), ALU.subtract)\
                   .then_inc(*drains(key))

            def lo_x(phase, t):
                for half in range(2):
                    s = slice(4 * half, 4 * half + 4)
                    lo((f"x{half}", phase, t), hi_no(f"x{half}", phase, t),
                       xT_lo[:, s, :].rearrange("p k n -> p (k n)"), xT_hi[:, s, :].rearrange("p k n -> p (k n)"))

            steps = [0]

            def step(ins):
                steps[0] += 1
                ins.then_inc(topk_step, 1)
                dve.wait_ge(topk_step, steps[0])

            def add_index(t):
                dve.wait_ge(kv_roped, t + 1)
                for h, c in index_order(t):
                    a, b = chunks_of(t)[c]
                    key = ("index", h, c, t)
                    dve.wait_ge(relued, index_no[t, h, c])
                    if h == 0:
                        ins = dve.tensor_scalar(idx[:, a:b], of(key)[:, 0:b - a], iw_s[:, 0:1], None, ALU.mult)
                    else:
                        wait_drained(dve, ("index", h - 1, c, t))
                        ins = dve.scalar_tensor_tensor(out=idx[:, a:b], in0=of(key)[:, 0:b - a],
                                                       scalar=iw_s[:, h:h + 1], in1=idx[:, a:b],
                                                       op0=ALU.mult, op1=ALU.add)
                    ins.then_inc(*drains(key))
                wait_drained(dve, ("index", IH - 1, len(chunks_of(t)) - 1, t))

            def counted(t, i):
                return (over, over_was) if i % 2 == 0 else (over_was, over)

            def search(t, i):
                n = keys_of(t)
                no = t - len([x for x in range(TILES) if not searched(x)])
                if i == 0:
                    dve.wait_ge(guessed, no + 1)
                    if t != SAMPLE:
                        step(dve.memset(idx[0:CHUNK, n - CHUNK:n], MASKED))
                now, was = counted(t, i)
                step(dve.tensor_scalar(work[:, 0:n], idx[:, 0:n], above, None, ALU.is_gt, ALU.add, accum_out=seen))
                step(dve.tensor_scalar(now, seen, -AIM, None, ALU.add))
                if i == COUNTS - 1:
                    dve.scalar_tensor_tensor(out=far, in0=now, scalar=now, in1=cst[:, 10:11],
                                             op0=ALU.mult, op1=ALU.is_gt).then_inc(far_ready, 1)
                    return
                step(dve.scalar_tensor_tensor(out=far, in0=now, scalar=now, in1=cst[:, 10:11],
                                              op0=ALU.mult, op1=ALU.is_gt))
                if i:
                    step(dve.tensor_tensor(gap, was, now, ALU.subtract))
                    step(dve.scalar_tensor_tensor(out=gap, in0=gap, scalar=0.0, in1=gap,
                                                  op0=ALU.is_equal, op1=ALU.add))
                    step(dve.reciprocal(gap, gap))
                    step(dve.tensor_tensor(gap, gap, move, ALU.mult))
                    step(dve.scalar_tensor_tensor(out=gap, in0=slope, scalar=0.25, in1=gap,
                                                  op0=ALU.mult, op1=ALU.max))
                    step(dve.scalar_tensor_tensor(out=slope, in0=slope, scalar=4.0, in1=gap,
                                                  op0=ALU.mult, op1=ALU.min))
                step(dve.scalar_tensor_tensor(out=move, in0=now, scalar=slope, in1=far,
                                              op0=ALU.mult, op1=ALU.mult))
                step(dve.tensor_tensor(above, above, move, ALU.add))

            def keep(t):
                n = keys_of(t)
                step(dve.memset(work[:, n:n + 8], TAKEN))
                step(dve.tensor_scalar(work[:, 0:n], idx[:, 0:n], above, TAKEN, ALU.is_gt, ALU.mult))
                step(dve.tensor_tensor(work[:, 0:n], work[:, 0:n], idx[:, 0:n], ALU.add))
                step(dve.tensor_scalar(left, seen, -1.0, float(TOPK), ALU.mult, ALU.add))

            def complete(t, i):
                n = keys_of(t)
                step(dve.tensor_scalar(drop8[:], cst[:, 12 + i:20 + i], left, TAKEN, ALU.is_ge, ALU.mult))
                step(dve.max(top8[:], work[:, 0:n]))
                step(dve.tensor_tensor(top8[:], top8[:], drop8[:], ALU.add))
                step(dve.match_replace(work[:, 0:n + 8], top8[:], work[:, 0:n + 8], TAKEN))

            def choose(t):
                n = keys_of(t)
                if not searched(t):
                    step(dve.memset(bias[:, 0:n], 0.0))
                    step(dve.memset(bias[0:CHUNK, n - CHUNK:n], MASKED))
                    return
                dve.wait_ge(any_ready, t - len([x for x in range(TILES) if not searched(x)]) + 1)
                off = dve.value_load(any_far[0:1, :].bitcast(mybir.dt.int32))
                with dve.If(off > 0):
                    dve.sem_clear(whole_step)
                    dve.tensor_copy(work[:, 0:n], idx[:, 0:n]).then_inc(whole_step, 1)
                    dve.wait_ge(whole_step, 1)
                    with dve.Fori(0, TOPK // 8):
                        dve.sem_clear(whole_step)
                        dve.max(top8[:], work[:, 0:n]).then_inc(whole_step, 1)
                        dve.wait_ge(whole_step, 1)
                        dve.match_replace(work[:, 0:n], top8[:], work[:, 0:n], TAKEN).then_inc(whole_step, 1)
                        dve.wait_ge(whole_step, 2)
                step(dve.tensor_scalar(bias[:, 0:n], work[:, 0:n], BETWEEN, MASKED, ALU.is_gt, ALU.mult))

            def between(name, t):
                if name == "x":
                    lo_x("A", t)
                elif name == "turn":
                    lo(("turn_iq", "A", t), hi_no("turn_iq", "A", t), iqT_lo[:].rearrange("p k n -> p (k n)"),
                       iqT_hi[:].rearrange("p k n -> p (k n)"))
                    key = ("turn_kv", "A", t)
                    n = DEC if t == SAMPLE else P
                    dve.wait_ge(hi_ready, hi_no("turn_kv", "A", t))
                    dve.tensor_tensor(kiT_lo[:, t * P:t * P + n], of(key)[:, 0:n],
                                      kiT_hi[:, t * P:t * P + n].bitcast(F32), ALU.subtract)
                    dve.tensor_tensor(kT_lo[:, t * P:t * P + n], of(key)[:, P:P + n],
                                      kT_hi[:, t * P:t * P + n].bitcast(F32), ALU.subtract).then_inc(*drains(key))
                elif name == "x_ret":
                    lo_x("R", 0)
                elif name == "weights":
                    for w, k in late_at[t]:
                        split_w(w, k)


            def attend(t):
                if t:
                    dve.wait_ge(ao_stored, 16 * t)
                for kind, h, c in attention_order(t):
                    if kind == "between":
                        between(h, c)
                    if kind != "score":
                        continue
                    a, b = chunks_of(t)[c]
                    key = ("score", h, c, t)
                    wait_filled(dve, key)
                    if h >= 2:
                        wait_filled(dve, ("turn", h - 2, len(groups_of(t)) - 1, t))
                    if c:
                        wait_drained(dve, ("score", h, c - 1, t))
                    dve.tensor_tensor_reduce(out=probs[h % 2][:, a:b], in0=of(key)[:, 0:b - a], in1=bias[:, a:b],
                                             scale=-float(HD) ** -0.5, scalar=low[:, h, c - 1:c] if c else 3.0e38,
                                             op0=ALU.add, op1=ALU.min, accum_out=low[:, h, c:c + 1])\
                       .then_inc(*drains(key))
                    if h == 0 and c == len(chunks_of(t)) - 1 and t != SAMPLE:
                        normalise(*(("A", t + 2) if t + 1 != SAMPLE else ("R", 0)))
                    if c == len(chunks_of(t)) - 1 and t != SAMPLE and searched(t + 1):
                        if 1 <= h <= COUNTS:
                            search(t + 1, h - 1)
                        if h == COUNTS + 1:
                            keep(t + 1)
                            complete(t + 1, 0)
                        if h == AH - 1:
                            complete(t + 1, 8)
                if t != SAMPLE:
                    choose(t + 1)
                dve.wait_ge(exped, AH * (t + 1))
                dve.reciprocal(rden[:], den[:]).then_inc(ao_step, 1)
                dve.wait_ge(ao_step, t + 1)
                key = ("attended", t)
                wait_filled(dve, key)
                dve.tensor_tensor(ao.rearrange("p (h d) -> p h d", d=HD),
                                  of(key)[:].rearrange("p (h d) -> p h d", d=HD),
                                  rden[:].unsqueeze(2).broadcast_to([P, AH, HD]), ALU.mult)\
                   .then_inc(*drains(key))

            dve.memset(ones8[:], 1.0).then_inc(ones_ready, 1)
            normalise("A", 0)
            dve.wait_ge(const_in, 64)
            dve.wait_ge(ones_ready, 1)
            for w in ("iq", "kv", "aq"):
                for k in range(KD):
                    split_w(w, k)
                    if (w, k) == ("iq", 1):
                        between("x", 0)
            between("turn", 0)
            for t in range(TILES):
                add_index(t)
                if t:
                    attend(t - 1)
                else:
                    normalise("A", 1)
                    for name in BETWEEN_HEADS.values():
                        between(name, 1)
                    choose(0)
                lo(("turn_aq", "A", t), hi_no("turn_aq", "A", t), aqT_lo[:].rearrange("p k n -> p (k n)"),
                   aqT_hi[:].rearrange("p k n -> p (k n)"))
                for cache, hi_, lo_ in (("ci", kiT_hi, kiT_lo),) * (t == NT - 1) + (("ck", kT_hi, kT_lo),) * (t == SAMPLE):
                    for half in range(2):
                        s = slice(half * BW, (half + 1) * BW)
                        lo(("turn_" + cache, half), hi_no(f"{cache}{half}", "A", t), lo_[:, s], hi_[:, s])
                if 2 <= t <= 5:
                    for k in range(2 * t - 4, 2 * t - 2):
                        split_w("rq", k)
            attend(SAMPLE)

            half = RD // 2

            def rotate(t, name, row, table, ready):
                key = (name, "R", t)
                wait_filled(dve, key)
                sin = rot_r[:, table + 1, :].unsqueeze(1)
                x = of(key)[:].rearrange("p (h a d) -> p h a d", a=2, d=half)
                both = rot_r[:, table, :].unsqueeze(1).broadcast_to([P, 2 * RH, half])
                dve.tensor_tensor(row[:].rearrange("p h (a d) -> p (h a) d", a=2),
                                  of(key)[:].rearrange("p (g d) -> p g d", d=half), both, ALU.mult)
                tm = rtmp[:].rearrange("p h (a d) -> p h a d", a=2)
                ro_ = row[:].rearrange("p h (a d) -> p h a d", a=2)
                for a in range(2):
                    ins = dve.tensor_tensor(tm[:, :, a, :], x[:, :, 1 - a, :], sin.broadcast_to([P, RH, half]), ALU.mult)
                ins.then_inc(*drains(key))
                wait_drained(dve, key)
                dve.tensor_tensor(ro_[:, :, 0, :], ro_[:, :, 0, :], tm[:, :, 0, :], ALU.subtract)
                dve.tensor_tensor(ro_[:, :, 1, :], ro_[:, :, 1, :], tm[:, :, 1, :], ALU.add).then_inc(ready, 1)

            def rotate_q(t):
                dve.wait_ge(rot_in, 16 * (t + 1))
                if not (isinstance(t, int) and t == 0):
                    wait_filled(dve, ("turn_q", "R", t - 1))
                    dve.wait_ge(rk_ready, t)
                rotate(t, "q", rq_row, 0, rq_ready)

            def rotate_k(t):
                if not (isinstance(t, int) and t == 0):
                    wait_filled(dve, ("turn_k", "R", t - 1))
                    dve.wait_ge(kd_ready, t)
                dve.wait_ge(rq_ready, t + 1)
                rotate(t, "k", rk_row, 2, rk_ready)

            def decay_scores(t, table):
                key = ("scores", "R", t)
                wait_filled(dve, key)
                if not (isinstance(t, int) and t == 0):
                    wait_filled(dve, ("out", "R", t - 1))
                dve.tensor_tensor(rsT[:].rearrange("p h d -> p (h d)"), of(key)[:],
                                  table[:].rearrange("p h d -> p (h d)"), ALU.mult).then_inc(*drains(key))

            def retain(t, st, length):
                key = ("kv", "R", t)
                wait_filled(dve, key)
                wait_filled(dve, ("out", "R", t))
                for h in range(RH):
                    ins = dve.scalar_tensor_tensor(out=st[:, h, :], in0=st[:, h, :],
                                                   scalar=float(np.exp(LOG_GAMMA[h] * length)),
                                                   in1=of(key)[:, h * RD:(h + 1) * RD], op0=ALU.mult, op1=ALU.add)
                ins.then_inc(*drains(key))
                key = ("out", "R", t)
                dve.wait_ge(squared, t + 1)
                dve.tensor_scalar(group_sq[:], group_sq[:], 1.0 / RD, EPS, ALU.mult, ALU.add).then_inc(ms_ready, 1)
                dve.wait_ge(rstd_ready, power_no("retained", t) + 1)
                for h in range(RH):
                    ins = dve.scalar_tensor_tensor(out=ro[:, h, :], in0=of(key)[:, h * RD:(h + 1) * RD],
                                                   scalar=rstd[:, h:h + 1], in1=gn_t[:, h * RD:(h + 1) * RD],
                                                   op0=ALU.mult, op1=ALU.mult)
                ins.then_inc(*drains(key))

            def retain_tile(t):
                rotate_q(t + 1)
                decay_scores(t, dec_t)
                normalise("R", t + 2)
                rotate_k(t + 1)
                retain(t, state, P)
                lo_x("R", t + 2)

            normalise("R", 1)
            dve.wait_ge(ao_stored, 16 * TILES)
            dve.memset(state[:], 0.0).then_inc(state_zero, 1)
            dve.wait_ge(state_zero, 1)
            rotate_q(0)
            rotate_k(0)
            lo_x("R", 1)
            dve.wait_ge(r_const_in, R_CONSTS)
            retain_tile(0)
            with dve.Fori(1, NT - 1) as t:
                retain_tile(t)
            rotate_q(SAMPLE)
            decay_scores(NT - 1, dec_t)
            normalise("O", 0)
            rotate_k(SAMPLE)
            for k in range(4):
                split_w("ag", k)
            retain(NT - 1, state, P)
            lo_x("O", 0)
            for k in range(4, KD):
                split_w("ag", k)
            decay_scores(SAMPLE, dec_s)
            for k in range(4):
                split_w("wo0", k)
            normalise("O", 1)
            retain(SAMPLE, state_s, DEC)
            lo_x("O", 1)

            def mix(t):
                dve.wait_ge(mix_in, 32 * (t + 1))
                for half_, name in enumerate(("rg", "ag")):
                    s = slice(half_ * BW, (half_ + 1) * BW)
                    wait_drained(dve, (name, "O", t))
                    dve.tensor_tensor(mixed[:, s], mixed[:, s], gate[:, s], ALU.mult).then_inc(mixed_ready, 1)

            def lo_mixed(t):
                for half_ in range(2):
                    s = slice(4 * half_, 4 * half_ + 4)
                    lo((f"turn{half_}", "O", t), hi_no(f"turn{half_}", "O", t),
                       mT_lo[:, s, :].rearrange("p k n -> p (k n)"), mT_hi[:, s, :].rearrange("p k n -> p (k n)"))

            def output(t):
                dve.wait_ge(y_in, 32 * (t + 1))
                for half_ in range(2):
                    s = slice(half_ * BW, (half_ + 1) * BW)
                    key = (f"y{half_}", "O", t)
                    wait_filled(dve, key)
                    dve.tensor_tensor(y_row[:, s], of(key)[:], y_row[:, s], ALU.add).then_inc(*drains(key))
                for half_ in range(2):
                    wait_drained(dve, (f"y{half_}", "O", t))
                mean_square(y_row, stat_no("y", t))
                dve.wait_ge(rstd_ready, power_no("y", t) + 1)
                dve.scalar_tensor_tensor(out=y_row[:], in0=y_row[:], scalar=rstd[:, 0:1], in1=fg_t[:],
                                         op0=ALU.mult, op1=ALU.mult).then_inc(y_ready, 1)

            def out_tile(t):
                lo_mixed(t)
                normalise("O", t + 2)
                mix(t + 1)
                lo_x("O", t + 2)
                output(t)

            dve.wait_ge(fg_in, 16)
            mix(0)
            for k in range(4, KD):
                split_w("wo0", k)
            lo_mixed(0)
            normalise("O", 2)
            for k in range(KD):
                split_w("wo1", k)
            mix(1)
            lo_x("O", 2)
            output(0)
            with dve.Fori(1, NT - 1) as t:
                out_tile(t)
            lo_mixed(NT - 1)
            mix(SAMPLE)
            output(NT - 1)
            lo_mixed(SAMPLE)
            output(SAMPLE)

        @block.gpsimd
        def _(pool):
            def power(no, width):
                pool.wait_ge(ms_ready, no + 1)
                src = mean_sq[:, 1:2] if width == 1 else group_sq[:]
                pool.tensor_tensor(rstd[:, 0:width], src, cst[:, 8:9].broadcast_to([P, width]), ALU.pow)\
                    .then_inc(rstd_ready, 1)

            steps = [0]
            guesses = [0]

            def step(ins):
                steps[0] += 1
                ins.then_inc(rope_step, 1)
                pool.wait_ge(rope_step, steps[0])

            def rotate(rows, heads, t):
                x = rows.rearrange("p (h d) -> p h d", d=HD)
                cos = rope_t[:, t, 0:ROT].unsqueeze(1).broadcast_to([P, heads, ROT])
                a, b = rope_a[:, 0:heads, :], rope_b[:, 0:heads, :]
                h2 = ROT // 2
                pool.tensor_tensor(a, x[:, :, 0:ROT], cos, ALU.mult)
                for s in range(2):
                    sin = rope_t[:, t, ROT + s * h2:ROT + (s + 1) * h2].unsqueeze(1).broadcast_to([P, heads, h2])
                    ins = pool.tensor_tensor(b[:, :, s * h2:(s + 1) * h2], x[:, :, (1 - s) * h2:(2 - s) * h2], sin,
                                             ALU.mult)
                step(ins)
                return pool.tensor_tensor(x[:, :, 0:ROT], a, b, ALU.add)

            pool.wait_ge(const_in, 64)
            def rotate_iq(t):
                wait_drained(pool, ("iq", "A", t))
                rotate(q_row[:], AH, t).then_inc(q_roped, 1)
                pool.wait_ge(q_roped, 2 * t + 1)

            def rotate_kv(t):
                pool.wait_ge(rowed, t + 1)
                step(rotate(kv_row[:, HD:4 * HD], 3, t))
                if t:
                    wait_drained(pool, ("index", IH - 1, len(chunks_of(t - 1)) - 1, t - 1))
                pool.tensor_scalar(iw_s[:], kv_row[:, 6 * HD:6 * HD + IH], IH ** -0.5 * HD ** -0.5, None, ALU.mult)
                pool.tensor_copy(kv_row[:, 0:HD], kv_row[:, HD:2 * HD]).then_inc(kv_roped, 1)
                pool.wait_ge(kv_roped, t + 1)
                outs = (k_out, v_out, i_out) if t != SAMPLE else (ks_out, vs_out, is_out)
                n = P if t != SAMPLE else DEC
                rows = slice(t * P, t * P + n) if t != SAMPLE else slice(0, DEC)
                for dst, a, b in ((outs[0], 2, 4), (outs[1], 4, 6), (outs[2], 1, 2)):
                    pool.dma_start(dst[rows, :], kv_row[0:n, a * HD:b * HD]).then_inc(kv_stored, 16)

            def guess(ins):
                guesses[0] += 1
                ins.then_inc(guess_step, 1)
                pool.wait_ge(guess_step, guesses[0])

            def guess_threshold(t, no):
                pool.wait_ge(index_summed, 2 * (no + 1))
                n = keys_of(t)
                guess(pool.tensor_scalar(mean, total, 1.0 / n, None, ALU.mult))
                guess(pool.tensor_scalar(var, squares, 1.0 / n, None, ALU.mult))
                guess(pool.tensor_tensor(dev, mean, mean, ALU.mult))
                guess(pool.tensor_tensor(var, var, dev, ALU.subtract))
                guess(pool.tensor_scalar(var, var, 1e-30, None, ALU.max))
                guess(pool.tensor_tensor(dev, var, cst[:, 9:10], ALU.pow))
                guess(pool.tensor_tensor(slope, dev, cst[:, 29 + 2 * t:30 + 2 * t], ALU.mult))
                guess(pool.tensor_tensor(above, dev, cst[:, 28 + 2 * t:29 + 2 * t], ALU.mult))
                pool.tensor_tensor(above, above, mean, ALU.add).then_inc(guessed, 1)

            def store_attended(t):
                wait_drained(pool, ("attended", t))
                pool.dma_start(att_mem[t * P:(t + 1) * P, :], ao).then_inc(ao_stored, 16)

            power(power_no("A", 0), 1)
            rotate_iq(0)
            rotate_kv(0)
            for t in range(TILES):
                no = len([x for x in range(t) if searched(x)])
                power(power_no(*(("A", t + 1) if t != SAMPLE else ("R", 0))), 1)
                if searched(t):
                    guess_threshold(t, no)
                wait_drained(pool, ("aq", "A", t))
                rotate(aq_row[:], AH, t).then_inc(q_roped, 1)
                pool.wait_ge(q_roped, 2 * t + 2)
                if t + 1 < TILES:
                    rotate_iq(t + 1)
                    rotate_kv(t + 1)
                if searched(t):
                    pool.wait_ge(far_ready, no + 1)
                    pool.partition_all_reduce(any_far, far, P, bass.bass_isa.ReduceOp.max).then_inc(any_ready, 1)
                if t:
                    store_attended(t - 1)
                if t == SAMPLE:
                    pool.dma_start(v_sb[:, 0:NT, :], vc).then_inc(vcache_in, 16)
            store_attended(SAMPLE)

            pool.wait_ge(ao_stored, 16 * TILES)
            for dst, src in ((dec_t, decay), (dec_s, decay_sample), (start_t, from_start)):
                pool.dma_start(dst[:].rearrange("p h n -> p (h n)"), src).then_inc(r_const_in, 16)
            pool.dma_start(gn_t[:], gn_row.broadcast_to([P, BW]))\
                .then_inc(r_const_in, 16)
            pool.dma_start(state_s[:], state_ret[0, 0].rearrange("h d e -> d h e")).then_inc(r_const_in, 16)
            pool.dma_start(fg_t[:], fg_row.broadcast_to([P, D])).then_inc(fg_in, 16)

            def load_angles(t):
                pool.dma_start(rot_r[:].rearrange("p a d -> p (a d)"), rope_ret[bass.ds(t * P, P), :])\
                    .then_inc(rot_in, 16)

            def decay_rows(t, col):
                pool.wait_ge(rk_ready, t + 1)
                if not (isinstance(t, int) and t == 0):
                    wait_filled(pool, ("kv", "R", t - 1))
                pool.tensor_tensor(kd_row[:], rk_row[:], cst[:, col:col + RH].unsqueeze(2).broadcast_to([P, RH, RD]),
                                   ALU.mult).then_inc(kd_ready, 1)

            def decay_queries(t):
                wait_drained(pool, ("turn_q", "R", t))
                if not (isinstance(t, int) and t == 0):
                    wait_filled(pool, ("out", "R", t - 1))
                pool.tensor_tensor(rqdT[:], rqT[:], start_t[:], ALU.mult).then_inc(rqd_ready, 1)

            def store_ro(t):
                wait_drained(pool, ("out", "R", t))
                pool.dma_start(ret_mem[bass.ds(t * P, P), :], ro[:].rearrange("p h d -> p (h d)"))\
                    .then_inc(ro_stored, 16)

            def retain_tile(t):
                decay_queries(t)
                power(power_no("R", t + 2), 1)
                decay_rows(t + 1, 0)
                load_angles(t + 2)
                power(power_no("retained", t), 4)
                store_ro(t)

            load_angles(0)
            power(power_no("R", 1), 1)
            pool.wait_ge(r_const_in, R_CONSTS)
            decay_rows(0, 0)
            load_angles(1)
            retain_tile(0)
            with pool.Fori(1, NT - 1) as t:
                retain_tile(t)
            decay_queries(NT - 1)
            power(power_no("O", 0), 1)
            decay_rows(SAMPLE, 4)
            power(power_no("retained", NT - 1), 4)
            store_ro(NT - 1)
            wait_drained(pool, ("kv", "R", NT - 1))
            pool.dma_start(ret_p[0, 0].rearrange("h d e -> d h e"), state[:]).then_inc(state_stored, 16)
            decay_queries(SAMPLE)

            def load_mix(t):
                rows = bass.ds(t * P, P)
                pool.dma_start(mixed[:, 0:BW], ret_mem[rows, :]).then_inc(mix_in, 16)
                pool.dma_start(mixed[:, BW:D], att_mem[rows, :]).then_inc(mix_in, 16)

            def finish(t, x=True, more=True):
                if more:
                    wait_filled(pool, ("turn1", "O", t))
                    load_mix(t + 1)
                if x:
                    power(power_no("O", t + 2), 1)
                power(power_no("y", t), 1)
                pool.wait_ge(y_ready, t + 1)
                if isinstance(t, int) and t == SAMPLE:
                    pool.dma_start(y_sample[0], y_row[0:DEC, :]).then_inc(y_stored, 16)
                else:
                    pool.dma_start(y_prompt[0, bass.ds(t * P, P), :], y_row[:]).then_inc(y_stored, 16)

            pool.wait_ge(ro_stored, 16 * NT)
            load_mix(0)
            power(power_no("O", 1), 1)
            power(power_no("retained", SAMPLE), 4)
            store_ro(SAMPLE)
            wait_drained(pool, ("kv", "R", SAMPLE))
            pool.dma_start(ret_s[0, 0].rearrange("h d e -> d h e"), state_s[:]).then_inc(state_stored, 16)
            finish(0)
            with pool.Fori(1, NT - 1) as t:
                finish(t)
            pool.wait_ge(ro_stored, 16 * TILES)
            finish(NT - 1, x=False)
            finish(SAMPLE, x=False, more=False)
            pool.wait_ge(y_stored, 16 * TILES)
            pool.wait_ge(state_stored, 32)
            pool.wait_ge(kv_stored, 48 * TILES)


_INS = ["x_prompt", "x_sample", "state_ret", "cache_k", "cache_v", "cache_kidx", "norm_g", "w_in", "ret_gn_g",
        "w_out", "final_g"]
_OUTS = [(1, SEQ, D), (1, DEC, D), (1, 1, RH, RD, RD), (1, 1, SEQ, KVH, HD), (1, 1, SEQ, KVH, HD), (1, 1, SEQ, HD),
         (1, 1, RH, RD, RD), (1, 1, DEC, KVH, HD), (1, 1, DEC, KVH, HD), (1, 1, DEC, HD)]


def kernel(**inputs):
    import concourse.bacc as bacc
    from concourse.bass_utils import run_bass_kernel_spmd

    nc = bacc.Bacc("TRN2", target_bir_lowering=False, num_devices=1)
    arrays, args = {}, []
    given = {n: np.ascontiguousarray(inputs[n]) for n in _INS}
    given["norm_g"] = np.ascontiguousarray(given["norm_g"].reshape(KD, P).T)
    for name, a in {**given, **constants()}.items():
        arrays[f"in_{name}"] = a
        args.append(nc.dram_tensor(f"in_{name}", a.shape, mybir.dt.from_np(a.dtype), kind="ExternalInput").ap())
    for i, shape in enumerate(_OUTS):
        args.append(nc.dram_tensor(f"out_{i}", shape, F32, kind="ExternalOutput").ap())
    hybrid_stream_step(nc, *args)
    r = run_bass_kernel_spmd(nc, [arrays], core_ids=[0])
    return tuple(r.results[0][f"out_{i}"] for i in range(len(_OUTS)))
```

```python
from contextlib import ExitStack
from math import erf, sqrt

import numpy as np

import concourse.bass as bass
from concourse import mybir

F32 = mybir.dt.float32
F32R = mybir.dt.float32r
BF16 = mybir.dt.bfloat16
ALU = mybir.AluOpType
ACT = mybir.ActivationFunctionType
AX_X = mybir.AxisListType.X

P = 128
D = 1024
KD = D // P
SEQ, DEC, PAST = 1024, 64, 1024
CHUNK = 64
NT = SEQ // P
TILES = NT + 1
SAMPLE = NT
RH, RD = 4, 128
AH, HD, KVH = 8, 64, 2
IH = 8
ROT = HD // 4
TOPK = 256
EPS = 1e-6
NB = 8
BW = 512
MASKED = -3.0e38
TAKEN = -3.4e38
BETWEEN = -3.3e38
COUNTS = 5
WINDOW = 16
AIM = TOPK - (WINDOW + 1) / 2
C_RQ, C_RK, C_RV, C_RG = 0, 512, 1024, 1536
C_AQ, C_AK, C_AG, C_IQ, C_IK, C_IW = 2048, 2560, 2816, 3328, 3840, 3904
KVW = 328

LOG_GAMMA = [float(np.log1p(-np.exp2(-5.0 - h))) for h in range(RH)]


def heads_of(t):
    return AH // 2 if t == SAMPLE else AH


def keys_of(t):
    return PAST + DEC if t == SAMPLE else P * (t + 1)


def chunks_of(t):
    n = keys_of(t)
    size = -(-n // (-(-n // BW) * DEC)) * DEC
    return [(c, min(c + size, n)) for c in range(0, n, size)]


def groups_of(t):
    blocks = [(b, min(P, keys_of(t) - b * P)) for b in range(-(-keys_of(t) // P))]
    return [blocks[i:i + 4] for i in range(0, len(blocks), 4)]


BETWEEN_HEADS = {2: "kv", 5: "turn"}


def attention_order(t):
    scores = lambda h: [("score", h, c) for c in range(len(chunks_of(t)))]
    groups = range(len(groups_of(t)))
    order, last, exps = scores(0) + scores(1) + [("exp", 0, 0)], None, 1
    if t + 2 < TILES:
        order += [("exp", 1, 0), ("between", "iq", t + 2)]
        exps = 2
    heads = heads_of(t)
    for h in range(heads):
        for g in groups:
            order.append(("turn", h, g))
            if last:
                order.append(("value", *last))
            last = (h, g)
        if exps < min(heads, h + 2):
            order.append(("exp", exps, 0))
            exps += 1
        if h + 2 < heads:
            order += scores(h + 2)
        if t + 2 < TILES and h in BETWEEN_HEADS:
            if exps < min(heads, h + 3):
                order.append(("exp", exps, 0))
                exps += 1
            order.append(("between", BETWEEN_HEADS[h], t + 2))
        elif t + 2 >= TILES:
            order.append(("between", "weights", (t, h)))
    return order + [("value", *last)]


PRODUCTS = 3 * KD


def index_order(t):
    order, steps, done = [], [("index", h, c) for h in range(heads_of(t)) for c in range(len(chunks_of(t)))], 0
    spread = -(-len(steps) * 3 // 4)
    for i, step in enumerate(steps):
        order.append(step)
        if i < spread:
            upto = PRODUCTS * (i + 1) // spread
            order.append(("aq", done, upto))
            done = upto
        if i == spread // 2:
            order.append(("scale", t + 1, 0))
        if i == spread:
            order.append(("x", t + 1, 0))
    if t == SAMPLE:
        order += [("fold", 0, c) for c in range(len(chunks_of(t)))]
    return order


def index_steps(t):
    return [step[1:] for step in index_order(t) if step[0] == "index"]


def x_of(t):
    return ("A", t) if t < TILES else ("R", 0)


SMALL = 28 + 2 * TILES


def searched(t):
    return keys_of(t) > TOPK


def normal_quantile(share):
    low, high = -8.0, 8.0
    for _ in range(60):
        mid = (low + high) / 2
        low, high = (mid, high) if (1 + erf(mid / sqrt(2))) / 2 < share else (low, mid)
    return low


def constants():
    pos = np.concatenate([np.arange(SEQ), PAST + np.arange(DEC), PAST + np.arange(DEC)]).astype(np.float32)

    def angles(half, theta):
        inv = np.power(np.float32(theta), -np.arange(half, dtype=np.float32) / np.float32(half)).astype(np.float32)
        a = (pos[:, None] * inv[None, :]).astype(np.float32)
        return np.cos(a).astype(np.float32), np.sin(a).astype(np.float32)

    c, s = angles(ROT // 2, 500000.0)
    rope_a = np.concatenate([c, c, -s, s], axis=1)
    rope_a = rope_a.reshape(TILES, P, 2 * ROT).transpose(1, 0, 2).reshape(P, -1)
    c, s = angles(RD // 2, 10000.0)
    ks = np.float32(RD ** -0.5)
    rope_r = np.concatenate([c, s, c * ks, s * ks], axis=1)
    lg = np.array(LOG_GAMMA)
    m, n = np.arange(P)[:, None], np.arange(P)[None, :]
    seen = (m // CHUNK) <= (n // CHUNK)
    decay = np.stack([np.where(seen, np.exp(g * np.abs(n - m)), 0.0) for g in lg], 1)
    first = (m < DEC) & (n < 2 * DEC)
    decay_s = np.stack([np.where(first, np.exp(g * np.abs(n % DEC - m)), 0.0) for g in lg], 1)
    from_start = np.stack([np.broadcast_to(np.exp(g * (np.arange(P) + 1)), (P, P)) for g in lg], 1)
    to_end = np.exp(lg[None, :] * (P - 1 - np.arange(P))[:, None])
    to_end_s = np.where(np.arange(P)[:, None] < DEC, np.exp(lg[None, :] * (DEC - 1 - np.arange(P))[:, None]), 0.0)
    small = np.zeros((P, SMALL))
    small[:, 0:4], small[:, 4:8] = to_end, to_end_s
    small[:, 8], small[:, 9], small[:, 10] = -0.5, 0.5, ((WINDOW - 1) / 2) ** 2
    small[:, 12:12 + WINDOW] = np.arange(WINDOW)
    for t in range(TILES):
        if searched(t):
            for rows, n in ((slice(0, CHUNK), keys_of(t) - (CHUNK if t < SAMPLE else 0)), (slice(CHUNK, P), keys_of(t))):
                z = normal_quantile(1 - AIM / n)
                small[rows, 28 + 2 * t] = z
                small[rows, 29 + 2 * t] = np.sqrt(2 * np.pi) * np.exp(z * z / 2) / n
    return {
        "identity": np.eye(P, dtype=np.float32),
        "fold": np.tile(np.eye(DEC, dtype=np.float32), (2, 2)),
        "rope_att": np.ascontiguousarray(rope_a, np.float32),
        "rope_ret": np.ascontiguousarray(rope_r, np.float32),
        "decay": decay.reshape(P, -1).astype(np.float32),
        "decay_sample": decay_s.reshape(P, -1).astype(np.float32),
        "from_start": from_start.reshape(P, -1).astype(np.float32),
        "small": small.astype(np.float32),
    }


def hybrid_stream_step(nc, x_prompt, x_sample, state_ret, cache_k, cache_v, cache_kidx, norm_g, w_in,
                       ret_gn_g, w_out, final_g, identity, fold, rope_att, rope_ret, decay, decay_sample,
                       from_start, small,
                       y_prompt, y_sample, ret_p, k_p, v_p, kidx_p, ret_s, k_s, v_s, kidx_s):
    xp, xs = x_prompt[0], x_sample[0]
    w_rows = w_in[0].rearrange("(k p) n -> p k n", p=P)
    wo_rows = w_out[0].rearrange("(k p) n -> p k n", p=P)
    gn_row = ret_gn_g
    fg_row = final_g.rearrange("(a d) -> a d", a=1)
    kc = cache_k[0, 0].rearrange("(b p) h d -> p b (h d)", p=P)
    vc = cache_v[0, 0].rearrange("(b p) h d -> p b (h d)", p=P)
    ic = cache_kidx[0, 0].rearrange("(b p) d -> p b d", p=P)
    k_out, v_out, i_out = (a[0, 0] for a in (k_p, v_p, kidx_p))
    k_out, v_out = (a.rearrange("t h d -> t (h d)") for a in (k_out, v_out))
    ks_out, vs_out, is_out = (a[0, 0] for a in (k_s, v_s, kidx_s))
    ks_out, vs_out = (a.rearrange("t h d -> t (h d)") for a in (ks_out, vs_out))
    att_mem = nc.dram_tensor("attended", (TILES * P, BW), F32).ap()
    ret_mem = nc.dram_tensor("retained", (TILES * P, BW), F32).ap()

    with ExitStack() as ctx:
        place = [(nc.sbuf_base + 63) // 32 * 32]

        def sb(name, shape, dt=F32, at=None):
            size = int(np.prod(shape[1:])) * (2 if dt == BF16 else 4)
            where = place if at is None else at
            t = nc.alloc_sbuf_tensor_at(name, shape, dt, offset=where[0])
            where[0] += (size + 31) // 32 * 32
            return t

        SLOTS = 4
        where_slots, w_bytes = place[0], KD * BW * 4
        w_hi = [sb(f"w_hi{s}", [P, KD, BW], F32R) for s in range(SLOTS)]
        w_lo = [sb(f"w_lo{s}", [P, KD, BW], F32R) for s in range(SLOTS)]
        EARLY = 4
        at = [where_slots + (SLOTS - 1) * w_bytes]
        early = [sb(f"early{g}", [P, EARLY, BW], at=at) for g in range(2)]
        at = [where_slots + (2 * SLOTS - 1) * w_bytes]
        early += [sb(f"early{g}", [P, EARLY, BW], at=at) for g in range(2, 4)]
        STAGES = 3
        stage = [sb(f"stage{s}", [P, BW]) for s in range(STAGES)]
        ident = sb("ident", [P, P])
        fold_t = sb("fold_t", [P, P])
        g_in = sb("g_in", [P, KD])
        cst = sb("cst", [P, SMALL])
        ones8 = sb("ones8", [P, KD])
        rope_t = sb("rope_t", [P, TILES, 2 * ROT])
        stats = sb("stats", [P, 2, 6])
        mean2 = sb("mean2", [P, 4])
        mean_sq = sb("mean_sq", [P, 2])
        group_sq = sb("group_sq", [P, 4])
        rstd = sb("rstd", [P, 4])
        x_sq = sb("x_sq", [P, 2])
        x_rstd = sb("x_rstd", [P, 1])
        xin = sb("xin", [P, D])
        x_heads = xin[:].rearrange("p (h a d) -> p h a d", a=2, d=HD)
        xT_hi = sb("xT_hi", [P, KD, P], F32R)
        xT_lo = sb("xT_lo", [P, KD, P], F32R)
        phase_start = place[0]
        NK = PAST + DEC
        kT = sb("kT", [P, KVH, NK], F32R)
        kiT_hi, kiT_lo = (sb(f"kiT_{x}", [P, NK], F32R) for x in ("hi", "lo"))
        v_sb = sb("v_sb", [P, TILES, KVH * HD])
        q_row = sb("q_row", [P, AH, 2, HD])
        aq_row = sb("aq_row", [P, AH, 2, HD])
        kv_row = sb("kv_row", [P, 1 + KVH, 2, HD])
        vw_row = sb("vw_row", [P, KVH * HD + IH])
        rope_a, rope_b = (sb(f"rope_{x}", [P, 2 * AH, ROT]) for x in "ab")
        iw_s = sb("iw_s", [P, IH])
        iqT, aqT_hi = w_lo[1][:, :, BW - P:BW], w_hi[1][:, :, BW - P:BW]
        aqT_lo = sb("aqT_lo", [P, AH // KVH, P], F32R)
        idx = sb("idx", [P, NK])
        work = sb("work", [P, NK + 8])
        top8 = sb("top8", [P, 8])
        drop8 = sb("drop8", [P, 8])
        found = sb("found", [P, 16])
        total, squares, mean, var, dev, above, slope, seen, over, over_was, far, move, gap, open_, any_far, left = (
            found[:, i:i + 1] for i in range(16))
        bias = sb("bias", [P, NK], BF16)
        probs = [sb(f"probs{i}", [P, NK]) for i in range(2)]
        pT = [sb(f"pT{i}", [P, 4, P]) for i in range(2)]
        low = sb("low", [P, AH, 3])
        den = sb("den", [P, AH])
        rden = sb("rden", [P, AH])
        ao = probs[0][:, 0:BW]
        assert place[0] <= nc.sbuf_usable_end, place[0]
        at = [phase_start]
        rq_row, rk_row, rv_row = (sb(f"{x}_row", [P, RH, RD], at=at) for x in ("rq", "rk", "rv"))
        rtmp = sb("rtmp", [P, RH, RD], at=at)
        kd_row = sb("kd_row", [P, RH, RD], at=at)
        rqT, rkT, rqdT = (sb(f"{x}T", [P, RH, P], at=at) for x in ("rq", "rk", "rqd"))
        rsT = sb("rsT", [P, RH, P], at=at)
        state = sb("state", [P, RH, RD], at=at)
        state_s = sb("state_s", [P, RH, RD], at=at)
        ro = sb("ro", [P, RH, RD], at=at)
        dec_t, dec_s, start_t = (sb(n, [P, RH, P], at=at) for n in ("dec_t", "dec_s", "start_t"))
        gn_t = sb("gn_t", [P, BW], at=at)
        rot_r = sb("rot_r", [P, 4, RD // 2], at=at)
        gate = sb("gate", [P, D], at=at)
        mixed = sb("mixed", [P, D], at=at)
        mT_hi, mT_lo = (sb(f"mT_{x}", [P, KD, P], F32R, at=at) for x in ("hi", "lo"))
        y_row = sb("y_row", [P, D], at=at)
        fg_t = sb("fg_t", [P, D], at=at)
        assert at[0] <= nc.sbuf_usable_end, at[0]

        bank = [ctx.enter_context(nc.psum_tensor(f"bank{b}", [P, BW], F32)) for b in range(NB)]
        filled = [ctx.enter_context(nc.semaphore(f"filled{b}")) for b in range(NB)]
        drained = [ctx.enter_context(nc.semaphore(f"drained{b}")) for b in range(NB)]

        def sem(name):
            return ctx.enter_context(nc.semaphore(name))

        const_in = sem("const_in")
        x_in = sem("x_in")
        stage_in = [sem(f"stage_in{i}") for i in range(STAGES)]
        early_in = [sem(f"early_in{g}") for g in range(4)]
        vcache_in = sem("vcache_in")
        w_rounded = sem("w_rounded")
        w_split = sem("w_split")
        x_squared = sem("x_squared")
        x_rstd_ready = sem("x_rstd_ready")
        stat_done = sem("stat_done")
        ms_ready = sem("ms_ready")
        rstd_ready = sem("rstd_ready")
        xn_ready = sem("xn_ready")
        hi_ready = sem("hi_ready")
        rowed = sem("rowed")
        rope_step = sem("rope_step")
        q_roped = sem("q_roped")
        kv_roped = sem("kv_roped")
        kv_stored = sem("kv_stored")
        doubled = sem("doubled")
        relued = sem("relued")
        index_summed = sem("index_summed")
        guess_step = sem("guess_step")
        guessed = sem("guessed")
        far_ready = sem("far_ready")
        any_ready = sem("any_ready")
        whole_step = sem("whole_step")
        ones_ready = sem("ones_ready")
        value_done = sem("value_done")
        topk_step = sem("topk_step")
        exped = sem("exped")
        ao_step = sem("ao_step")
        ao_stored = sem("ao_stored")
        r_const_in = sem("r_const_in")
        rot_in = sem("rot_in")
        rq_ready, rk_ready = sem("rq_ready"), sem("rk_ready")
        kd_ready = sem("kd_ready")
        rqd_ready = sem("rqd_ready")
        squared = sem("squared")
        ro_stored = sem("ro_stored")
        state_zero = sem("state_zero")
        state_stored = sem("state_stored")
        mix_in = sem("mix_in")
        y_in = sem("y_in")
        gated = sem("gated")
        mixed_ready = sem("mixed_ready")
        summed = sem("summed")
        y_ready = sem("y_ready")
        y_stored = sem("y_stored")
        fg_in = sem("fg_in")

        uses = [0] * NB
        use = {}
        turn = [0]

        def take(key, b=None):
            if b is None:
                b = turn[0] % (NB - 1)
                turn[0] += 1
            use[key] = (b, uses[b])
            uses[b] += 1

        def take_turned(t):
            take(("turn_iq0", "A", t))
            take(("turn_iq1", "A", t))
            take(("turn_kv", "A", t))

        def take_attention(t):
            for step in attention_order(t):
                if step[:2] == ("between", "turn"):
                    take_turned(step[2])
                elif step[0] == "between" and step[1] != "weights":
                    take((step[1], "A", step[2]))
                elif step[0] in ("score", "turn"):
                    take((*step, t))
            take(("attended", t), NB - 1)

        def take_rows(t):
            for s in ("iq", "kv"):
                take((s, "A", t))
            take_turned(t)

        def take_x(t):
            for half in range(2):
                take((f"x{half}", *x_of(t)))

        take_x(0)
        take_rows(0)
        for t in range(TILES):
            take(("aq", "A", t), NB - 1)
            for kind, *step in index_order(t):
                if kind == "index":
                    take(("index", *step, t))
                elif kind == "x":
                    take_x(step[0])
                elif kind == "fold":
                    take(("fold", step[1]))
            if t:
                take_attention(t - 1)
            else:
                take_rows(1)
            take(("turn_aq0", "A", t))
            take(("turn_aq1", "A", t))
            for name, banks in (("turn_ci", 2 * (t == NT - 1)), ("turn_ck", 4 * (t == SAMPLE))):
                for b in range(banks):
                    take((name, b))
        take_attention(SAMPLE)
        base_r = list(uses)
        for b in (3, 4):
            base_r[b] -= 1
        R_BANK = {"q": (0, 0), "k": (1, 0), "v": (2, 0), "x0": (3, 0), "x1": (4, 0), "turn_q": (5, 0),
                  "turn_k": (6, 0), "kv": (6, 1), "scores": (7, 0), "out": (7, 1)}
        R_USES = [1, 1, 1, 1, 1, 1, 2, 2]
        base_o = [b + TILES * u for b, u in zip(base_r, R_USES)]
        O_BANK = {"rg": 0, "ag": 1, "y1": 2, "x0": 3, "x1": 4, "turn0": 5, "turn1": 6, "y0": 7}

        def bank_use(key):
            if isinstance(key[-1], int) and key in use:
                return use[key]
            if key[-2:-1] == ("R",):
                b, k = R_BANK[key[0]]
                return b, base_r[b] + key[-1] * R_USES[b] + k
            if key[-2:-1] == ("O",):
                return O_BANK[key[0]], base_o[O_BANK[key[0]]] + key[-1]
            raise KeyError(key)

        def of(key):
            return bank[bank_use(key)[0]]

        def wait_filled(eng, key):
            b, n = bank_use(key)
            eng.wait_ge(filled[b], n + 1)

        def wait_drained(eng, key):
            b, n = bank_use(key)
            eng.wait_ge(drained[b], n + 1)

        def wait_free(eng, key):
            b, n = bank_use(key)
            if not (isinstance(n, int) and n == 0):
                eng.wait_ge(drained[b], n)

        def fills(key):
            return filled[bank_use(key)[0]], 1

        def drains(key):
            return drained[bank_use(key)[0]], 1

        R_HI, O_HI = 2, 4
        hi_a = ("turn_iq0", "turn_iq1", "turn_kv")
        hi_order = [(s, 0) for s in ("x0", "x1", *hi_a)]
        for t in range(TILES):
            hi_order += [(s, t + 1) for s in ("x0", "x1") + hi_a * (t + 1 < TILES)]
            hi_order += [("turn_aq0", t), ("turn_aq1", t)]
            if t == NT - 1:
                hi_order += [("ci0", t), ("ci1", t)]
            if t == SAMPLE:
                hi_order += [(f"ck{b}", t) for b in range(4)]
        hi_at = {(s, *x_of(t)): i + 1 for i, (s, t) in enumerate(hi_order)}
        n = len(hi_order) - 2
        hi_r = n
        hi_o = hi_r + R_HI * TILES

        def hi_no(s, phase, t):
            if isinstance(t, int) and (s, phase, t) in hi_at:
                return hi_at[s, phase, t]
            if phase == "R":
                return hi_r + t * R_HI + {"x0": 1, "x1": 2}[s]
            half = int(s[-1])
            if s.startswith("x"):
                return hi_o + half + (2 * t + 1 if isinstance(t, int) and t < 2 else O_HI * t - 1)
            return hi_o + half + (O_HI * t + 3 if isinstance(t, int) and t == SAMPLE else O_HI * t + 5)

        index_no, group_no, value_no, n, v = {}, {}, {}, 0, 0
        for t in range(TILES):
            for h, c in index_steps(t):
                n += 1
                index_no[t, h, c] = n
        for t in range(TILES):
            for kind, h, g in attention_order(t):
                if kind == "value":
                    group_no[t, h, g] = len(group_no)
                    if (h, g) != (heads_of(t) - 1, len(groups_of(t)) - 1):
                        v += 1
                        value_no[group_no[t, h, g]] = v
                    else:
                        value_no[group_no[t, h, g]] = ("attended", t)

        def wait_value(eng, no):
            if no >= 0:
                if isinstance(value_no[no], int):
                    eng.wait_ge(value_done, value_no[no])
                else:
                    wait_filled(eng, value_no[no])

        def last_index(t):
            return ("index", heads_of(t) - 1, len(chunks_of(t)) - 1, t)

        def last_score(t, h):
            return ("score", h, len(chunks_of(t)) - 1, t)

        def turned_heads(t, key, r=slice(0, P)):
            if t != SAMPLE:
                return of(key)[r, :].rearrange("p (h n) -> p h n", n=P)
            return of(key)[r, :].rearrange("p (j a n) -> p j a n", a=2, n=P)[:, :, :, 0:DEC]

        def packed(t, dst, half, r=slice(0, P)):
            if t != SAMPLE:
                return dst[r, 4 * half:4 * half + 4, :]
            return dst[r, 2 * half:2 * half + 2, :].rearrange("p j (a n) -> p j a n", a=2)

        def iq_roped(t):
            return 2 * t + 1

        def aq_roped(t):
            return 2 * t + 2

        BY_ACT = TILES

        def stat_no(what, t):
            if what == "y":
                return 26 if isinstance(t, int) and t == SAMPLE else 25 if isinstance(t, int) and t == NT - 1 else 12 + 2 * t
            if what == "O":
                return 9 + t if isinstance(t, int) and t < 2 else 7 + 2 * t
            return t

        def power_no(what, t):
            if what == "y":
                return 35 if isinstance(t, int) and t == SAMPLE else 34 if isinstance(t, int) and t == NT - 1 else 21 + 2 * t
            if what == "O":
                return 16 + 2 * t
            if what == "retained":
                return 3 + 2 * t
            if what == "R":
                return t if isinstance(t, int) and t < 2 else 2 * t - 2
            return t

        R_CONSTS = 16 * 5
        AO_STORES = 16 * (NT + 4)
        NORM = {"A": 0, "R": TILES, "O": 2 * TILES}

        def slot_items(slot, what):
            return [(slot, what, k) for k in range(KD)]

        items = (slot_items(0, "iq") + slot_items(1, "kv") + slot_items(2, "aq") + slot_items(3, "rq")
                 + [(None, "ci", 0), (None, "ck", 0), (None, "ck", 1)] + slot_items(0, "rk") + slot_items(2, "rv") + slot_items(1, "rg") + slot_items(3, "ag") + slot_items(0, "wo0")
                 + slot_items(2, "wo1"))
        COLS = {"iq": [(C_IQ, 0, BW)], "kv": [(C_IK, 0, HD), (C_AK, HD, 2 * KVH * HD), (C_IW, HD + 2 * KVH * HD, IH)],
                "aq": [(C_AQ, 0, BW)], "rq": [(C_RQ, 0, BW)], "rk": [(C_RK, 0, BW)], "rv": [(C_RV, 0, BW)],
                "rg": [(C_RG, 0, BW)], "ag": [(C_AG, 0, BW)], "wo0": [(0, 0, BW)], "wo1": [(BW, 0, BW)]}
        item_no = {(w, k): i for i, (_, w, k) in enumerate(items)}
        N_EARLY = item_no["rq", 0]

        def raw(i):
            return early[i // EARLY % 4][:, i % EARLY, :] if i < N_EARLY else stage[i % STAGES]

        count = {}

        def staged_at(i):
            slot, w, _ = items[i]
            s = early_in[i // EARLY % 4] if i < N_EARLY else stage_in[i % STAGES]
            if i >= N_EARLY or i % EARLY == 0:
                count[s.name] = count.get(s.name, 0) + 16 * (len(COLS[w]) if slot is not None else 1)
            return s, count[s.name]

        staged = [staged_at(i) for i in range(len(items))]
        split_no, n = {}, 0
        for slot, w, k in items:
            if slot is not None:
                n += 1
                split_no[w, k] = n
        DOUBLED = {("ci", 0): 1, ("ck", 0): 2, ("ck", 1): 3}
        slot_free = {"rk": ("iq", "A", SAMPLE), "rv": ("aq", "A", SAMPLE), "rg": ("attended", SAMPLE),
                     "ag": ("q", "R", SAMPLE), "wo0": ("k", "R", SAMPLE), "wo1": ("v", "R", SAMPLE)}
        SLOT = {w: slot for slot, w, _ in items}
        WIDTH = {w: sum(c[2] for c in COLS[w]) for w in COLS}
        late_at = {(t, h): [(w, k) for k in range(h * KD // heads_of(t), (h + 1) * KD // heads_of(t))]
                   for t, w in ((NT - 1, "rk"), (SAMPLE, "rv")) for h in range(heads_of(t))}

        block = ctx.enter_context(nc.Block())

        @block.sync
        def _(sp):
            def load(i):
                slot, w, k = items[i]
                buf, (done, _) = raw(i), staged[i]
                if i >= N_EARLY + STAGES:
                    slot2, w2, k2 = items[i - STAGES]
                    if slot2 is None:
                        sp.wait_ge(doubled, DOUBLED[w2, k2])
                    else:
                        sp.wait_ge(w_split, split_no[w2, k2])
                if w == "ci":
                    sp.dma_start(buf[:].rearrange("p (b d) -> p b d", d=HD), ic).then_inc(done, 16)
                elif w == "ck":
                    sp.dma_start(buf[:].rearrange("p (b n) -> p b n", n=P), kc[:, 4 * k:4 * k + 4, :])\
                      .then_inc(done, 16)
                else:
                    rows = wo_rows if w.startswith("wo") else w_rows
                    for src, dst, n in COLS[w]:
                        sp.dma_start(buf[:, dst:dst + n], rows[:, k, src:src + n]).then_inc(done, 16)

            def load_early(w):
                for k in range(0, KD, EARLY):
                    i = item_no[w, k]
                    if i >= 4 * EARLY:
                        _, w2, k2 = items[i - 3 * EARLY - 1]
                        sp.wait_ge(w_split, split_no[w2, k2])
                    for src, dst, n in COLS[w]:
                        sp.dma_start(early[i // EARLY % 4][:, :, dst:dst + n], w_rows[:, k:k + EARLY, src:src + n])\
                          .then_inc(staged[i][0], 16)

            def load_x(phase, t, wait=True):
                if wait:
                    prev = {"A": None, "R": ("x1", "A", SAMPLE), "O": ("x1", "R", SAMPLE)}[phase]
                    if not (isinstance(t, int) and t == 0):
                        prev = ("x1", phase, t - 1)
                    if prev:
                        wait_filled(sp, prev)
                for half in range(2):
                    src = xs if isinstance(t, int) and t == SAMPLE else xp[bass.ds(t * P + half * DEC, DEC), :]
                    sp.dma_start(xin[half * DEC:(half + 1) * DEC, :], src).then_inc(x_in, 16)

            def load_y(t):
                if not (isinstance(t, int) and t == 0):
                    sp.wait_ge(y_stored, 16 * t)
                for half in range(2):
                    src = xs if isinstance(t, int) and t == SAMPLE else xp[bass.ds(t * P + half * DEC, DEC), :]
                    sp.dma_start(y_row[half * DEC:(half + 1) * DEC, :], src).then_inc(y_in, 16)

            load_x("A", 0)
            sp.dma_start(cst[:], small).then_inc(const_in, 16)
            sp.dma_start(g_in[:], norm_g).then_inc(const_in, 16)
            sp.dma_start(ident[:], identity).then_inc(const_in, 16)
            sp.dma_start(fold_t[:], fold).then_inc(const_in, 16)
            sp.dma_start(rope_t[:], rope_att.rearrange("p (t n) -> p t n", n=2 * ROT)).then_inc(const_in, 16)
            load_early("iq")
            load_early("kv")
            load_x("A", 1)
            load_early("aq")
            for k in range(STAGES):
                load(item_no["rq", k])
            for t in range(2, TILES):
                load_x("A", t)
                for i in {4: (27, 28), 5: (29, 30), 6: (31,), 7: (32, 33, 34)}.get(t, ()):
                    load(i)
            load_x("R", 0)
            for i in range(item_no["rk", 0], item_no["rg", STAGES]):
                load(i)
            wait_filled(sp, ("turn_ck", 3))
            load_x("R", 1)
            load_x("R", 2)
            for k in range(STAGES, KD):
                load(item_no["rg", k])
            with sp.Fori(3, NT) as t:
                load_x("R", t)
            load_x("R", SAMPLE)
            load_x("O", 0)
            for k in range(KD):
                load(item_no["ag", k])
            load_x("O", 1)
            load_y(0)
            for k in range(KD):
                load(item_no["wo0", k])
            load_x("O", 2)
            for k in range(KD):
                load(item_no["wo1", k])
            with sp.Fori(3, NT) as t:
                load_x("O", t)
                load_y(t - 2)
            load_x("O", SAMPLE)
            for t in (NT - 2, NT - 1, SAMPLE):
                load_y(t)

        @block.tensor
        def _(pe):
            def turn_x(phase, t):
                pe.wait_ge(xn_ready, NORM[phase] + t + 1)
                for half in range(2):
                    key = (f"x{half}", phase, t)
                    wait_free(pe, key)
                    for j in range(4):
                        k = 4 * half + j
                        mm = pe.transpose(of(key)[:, j * P:(j + 1) * P], xin[:, k * P:(k + 1) * P], ident[:])
                    mm.then_inc(*fills(key))

            def x_turned(phase, t):
                for half in range(2):
                    wait_drained(pe, (f"x{half}", phase, t))

            def product(key, slot, width, hi, lo, w=None, part=(0, PRODUCTS)):
                if part[0] == 0:
                    wait_free(pe, key)
                out = of(key)[:, 0:width]
                for i in range(*part):
                    k, which = i // 3, i % 3
                    if w and which == 0:
                        pe.wait_ge(w_split, split_no[w, k])
                    mm = pe.matmul(out, (lo if which == 2 else hi)[:, k, :],
                                   (w_lo if which == 1 else w_hi)[slot][:, k, 0:width],
                                   start=(i == 0), stop=(i == PRODUCTS - 1))
                if part[1] == PRODUCTS:
                    mm.then_inc(*fills(key))

            def project(name, w, phase, t, first, part=(0, PRODUCTS)):
                product((name, phase, t), SLOT[w], WIDTH[w], xT_hi, xT_lo, w if first else None, part)

            def turn_rows(key, rows, n):
                wait_free(pe, key)
                for j in range(n):
                    mm = pe.transpose(of(key)[:, j * P:(j + 1) * P], rows[:, j * P:(j + 1) * P], ident[:])
                mm.then_inc(*fills(key))

            def turn_heads(key, row, heads):
                wait_free(pe, key)
                for j, h in enumerate(heads):
                    mm = pe.transpose(of(key)[:, j * P:(j + 1) * P], row[:, h].rearrange("p a d -> p (a d)"), ident[:])
                mm.then_inc(*fills(key))

            def turn_queries(name, t, row):
                for half in range(2):
                    turn_heads((f"{name}{half}", "A", t), row, range(4 * half, 4 * half + 4))

            def turn_cached_indexer():
                pe.wait_ge(doubled, DOUBLED["ci", 0])
                for half in range(2):
                    turn_heads(("turn_ci", half), q_row, range(4 * half, 4 * half + 4))

            def turn_cached_keys():
                for half, row in enumerate((q_row, x_heads)):
                    pe.wait_ge(doubled, DOUBLED["ck", half])
                    for g in range(KVH):
                        turn_heads(("turn_ck", KVH * half + g), row, range(g, 4 * KVH, KVH))

            def index(t):
                for half in range(2):
                    wait_drained(pe, (f"turn_iq{half}", "A", t))
                wait_drained(pe, ("turn_kv", "A", t))
                if t == SAMPLE:
                    for half in range(2):
                        wait_drained(pe, ("turn_ci", half))
                for kind, h, c in index_order(t):
                    if kind == "aq":
                        project("aq", "aq", "A", t, t == 0, (h, c))
                        continue
                    if kind == "x":
                        turn_x(*x_of(t + 1))
                    if kind == "fold":
                        a, b = chunks_of(t)[c]
                        wait_drained(pe, ("index", heads_of(t) - 1, c, t))
                        wait_free(pe, ("fold", c))
                        pe.matmul(of(("fold", c))[:, 0:b - a], fold_t[:], idx[:, a:b], start=True, stop=True)\
                          .then_inc(*fills(("fold", c)))
                    if kind != "index":
                        continue
                    a, b = chunks_of(t)[c]
                    key = ("index", h, c, t)
                    wait_free(pe, key)
                    out = of(key)[:, 0:b - a]
                    pe.matmul(out, iqT[:, h, :], kiT_hi[:, a:b], start=True, stop=False)
                    pe.matmul(out, iqT[:, h, :], kiT_lo[:, a:b], start=False, stop=True).then_inc(*fills(key))

            def turn_a(t):
                pe.wait_ge(q_roped, iq_roped(t))
                turn_queries("turn_iq", t, q_row)
                pe.wait_ge(kv_roped, t + 1)
                turn_heads(("turn_kv", "A", t), kv_row, range(1 + KVH))

            def between(name, t):
                if name == "iq":
                    x_turned("A", t)
                    project("iq", "iq", "A", t, t == 0)
                elif name == "kv":
                    project("kv", "kv", "A", t, t == 0)
                elif name == "turn":
                    turn_a(t)

            def attend(t):
                for half in range(2):
                    wait_drained(pe, (f"turn_aq{half}", "A", t))
                if t == SAMPLE:
                    for b in range(4):
                        wait_drained(pe, ("turn_ck", b))
                for kind, h, n in attention_order(t):
                    if kind == "between":
                        between(h, n)
                    if kind in ("between", "exp"):
                        continue
                    kv = h // (heads_of(t) // KVH)
                    key = (kind, h, n, t)
                    if kind == "score":
                        a, b = chunks_of(t)[n]
                        r = slice(HD * kv, HD * kv + HD)
                        wait_free(pe, key)
                        out = of(key)[:, 0:b - a]
                        pe.matmul(out, aqT_hi[:, h, :], kT[:, kv, a:b], start=True, stop=False)
                        pe.matmul(out, aqT_lo[r, h % (heads_of(t) // KVH), :], kT[r, kv, a:b], start=False, stop=True)\
                          .then_inc(*fills(key))
                    elif kind == "turn":
                        pe.wait_ge(exped, AH * t + h + 1)
                        wait_free(pe, key)
                        for j, (blk, rows) in enumerate(groups_of(t)[n]):
                            mm = pe.transpose(of(key)[0:rows, j * P:(j + 1) * P],
                                              probs[h % 2][:, blk * P:blk * P + rows], ident[:])
                        mm.then_inc(*fills(key))
                    else:
                        wait_drained(pe, ("turn", h, n, t))
                        if h == 0 and n == 0:
                            wait_free(pe, ("attended", t))
                            if t == SAMPLE:
                                pe.wait_ge(vcache_in, 16)
                        for j, (blk, rows) in enumerate(groups_of(t)[n]):
                            last = blk == len([1 for g in groups_of(t) for _ in g]) - 1
                            mm = pe.matmul(of(("attended", t))[:, h * HD:(h + 1) * HD],
                                           pT[group_no[t, h, n] % 2][0:rows, j, :],
                                           v_sb[0:rows, blk, kv * HD:(kv + 1) * HD],
                                           start=(blk == 0), stop=last)
                        if last:
                            if h == heads_of(t) - 1:
                                mm.then_inc(*fills(("attended", t)))
                            else:
                                mm.then_inc(value_done, 1)
                        else:
                            mm.then_inc(value_done, 1)

            pe.wait_ge(const_in, 80)
            turn_x("A", 0)
            for name in ("iq", "kv", "turn"):
                between(name, 0)
            for t in range(TILES):
                index(t)
                if t:
                    attend(t - 1)
                else:
                    for name in ("iq", "kv", "turn"):
                        between(name, 1)
                pe.wait_ge(q_roped, aq_roped(t))
                turn_queries("turn_aq", t, aq_row)
                if t == NT - 1:
                    turn_cached_indexer()
                if t == SAMPLE:
                    turn_cached_keys()
            attend(SAMPLE)

            def retain(t, st, ahead, first=False):
                pe.wait_ge(rq_ready, t + 1)
                turn_rows(("turn_q", "R", t), rq_row[:].rearrange("p h d -> p (h d)"), 4)
                pe.wait_ge(rk_ready, t + 1)
                turn_rows(("turn_k", "R", t), rk_row[:].rearrange("p h d -> p (h d)"), 4)
                ahead[0]()
                wait_drained(pe, ("turn_q", "R", t))
                wait_drained(pe, ("turn_k", "R", t))
                key = ("scores", "R", t)
                wait_free(pe, key)
                for h in range(RH):
                    mm = pe.matmul(of(key)[:, h * P:(h + 1) * P], rkT[:, h, :], rqT[:, h, :], start=True, stop=True)
                mm.then_inc(*fills(key))
                pe.wait_ge(kd_ready, t + 1)
                wait_drained(pe, ("v", "R", t))
                key = ("kv", "R", t)
                wait_free(pe, key)
                for h in range(RH):
                    mm = pe.matmul(of(key)[:, h * RD:(h + 1) * RD], kd_row[:, h, :], rv_row[:, h, :],
                                   start=True, stop=True)
                mm.then_inc(*fills(key))
                ahead[1]()
                pe.wait_ge(rqd_ready, t + 1)
                if isinstance(t, int) and t == SAMPLE:
                    pe.wait_ge(r_const_in, R_CONSTS)
                elif first:
                    pe.wait_ge(state_zero, 1)
                else:
                    wait_drained(pe, ("kv", "R", t - 1))
                wait_drained(pe, ("scores", "R", t))
                key = ("out", "R", t)
                wait_free(pe, key)
                for h in range(RH):
                    out = of(key)[:, h * RD:(h + 1) * RD]
                    pe.matmul(out, rqdT[:, h, :], st[:, h, :], start=True, stop=False)
                    mm = pe.matmul(out, rsT[:, h, :], rv_row[:, h, :], start=False, stop=True)
                mm.then_inc(*fills(key))
                ahead[2]()

            def project_r(name, t, first=False):
                project(name, f"r{name}", "R", t, first)

            def retain_tile(t, first=False):
                def next_q():
                    x_turned("R", t + 1)
                    project_r("q", t + 1)

                retain(t, state, (next_q, lambda: project_r("k", t + 1), lambda: project_r("v", t + 1)), first)

            x_turned("R", 0)
            for name in "qkv":
                project_r(name, 0, True)
            turn_x("R", 1)
            retain_tile(0, True)
            turn_x("R", 2)
            with pe.Fori(1, NT - 1) as t:
                retain_tile(t)
                turn_x("R", t + 2)
            retain_tile(NT - 1)
            turn_x("O", 0)

            def first_gate():
                x_turned("O", 0)
                project("rg", "rg", "O", 0, True)

            retain(SAMPLE, state_s, (first_gate, lambda: None, lambda: project("ag", "ag", "O", 0, True)))
            turn_x("O", 1)

            def turn_mixed(t):
                for half in range(2):
                    pe.wait_ge(mixed_ready, 2 * t + half + 1)
                    turn_rows((f"turn{half}", "O", t), mixed[:, half * BW:(half + 1) * BW], 4)

            def out_tile(t, first=False, gates=True, x=True, t_last=False):
                if gates:
                    x_turned("O", t + 1)
                    project("rg", "rg", "O", t + 1, False)
                    turn_mixed(t)
                    project("ag", "ag", "O", t + 1, False)
                if x:
                    turn_x("O", t + 2)
                for half in range(2):
                    wait_drained(pe, (f"turn{half}", "O", t))
                for half in range(2):
                    product((f"y{half}", "O", t), SLOT[f"wo{half}"], BW, mT_hi, mT_lo,
                            f"wo{half}" if first else None)
                    if t_last and half == 0:
                        turn_mixed(SAMPLE)

            out_tile(0, first=True)
            with pe.Fori(1, NT - 1) as t:
                out_tile(t)
            out_tile(NT - 1, x=False, t_last=True)
            out_tile(SAMPLE, gates=False, x=False)

        @block.scalar
        def _(act):
            def round_w(w, k):
                i = item_no[w, k]
                act.wait_ge(*staged[i])
                if w == "rq":
                    act.wait_ge(w_split, N_EARLY)
                if w in slot_free:
                    wait_filled(act, slot_free[w])
                g = ones8 if w.startswith("wo") else g_in
                act.activation(w_hi[SLOT[w]][:, k, 0:WIDTH[w]], raw(i)[:, 0:WIDTH[w]],
                               ACT.Identity, scale=g[:, k:k + 1]).then_inc(w_rounded, 1)

            def hi(key, dst, src=None):
                wait_filled(act, key)
                act.copy(dst, of(key)[:] if src is None else src).then_inc(hi_ready, 1)

            def twice(dst, src, heads):
                return act.copy(dst, src.rearrange("p (h d) -> p h d", d=HD).unsqueeze(2)
                                .broadcast_to([P, heads, 2, HD]))

            def square_x(t):
                act.wait_ge(x_in, 32 * (t + 1))
                if t >= 2:
                    wait_filled(act, ("turn_aq1", "A", t - 2))
                act.activation(aq_row[:].rearrange("p h a d -> p (h a d)"), xin[:], ACT.Square,
                               accum_out=x_sq[:, 0:1]).then_inc(x_squared, 1)

            def hi_queries(name, t, dst):
                for half in range(2):
                    key = (f"{name}{half}", "A", t)
                    hi(key, packed(t, dst, half), turned_heads(t, key))

            def hi_x(phase, t):
                for half in range(2):
                    hi((f"x{half}", phase, t), xT_hi[:, 4 * half:4 * half + 4, :].rearrange("p k n -> p (k n)"))

            def between(name, t):
                if name == "iq":
                    key = ("iq", "A", t)
                    wait_filled(act, key)
                    if t:
                        wait_filled(act, ("turn_iq1", "A", t - 1))
                    twice(q_row[:], of(key)[:], AH).then_inc(*drains(key))
                elif name == "kv":
                    key = ("kv", "A", t)
                    wait_filled(act, key)
                    if t:
                        wait_filled(act, ("turn_kv", "A", t - 1))
                        act.wait_ge(kv_stored, 48 * t)
                    twice(kv_row[:], of(key)[:, 0:3 * HD], 1 + KVH)
                    act.copy(vw_row[:], of(key)[:, 3 * HD:KVW]).then_inc(rowed, 1)
                    n = DEC if t == SAMPLE else P
                    act.copy(v_sb[0:n, t, :], of(key)[0:n, 3 * HD:5 * HD]).then_inc(*drains(key))
                elif name == "turn":
                    hi_queries("turn_iq", t, iqT)
                    key = ("turn_kv", "A", t)
                    n = DEC if t == SAMPLE else P
                    wait_filled(act, key)
                    act.copy(kiT_hi[:, t * P:t * P + n], of(key)[:, 0:n])
                    act.copy(kT[:, :, t * P:t * P + n],
                             of(key)[:, P:3 * P].rearrange("p (g n) -> p g n", n=P)[:, :, 0:n]).then_inc(hi_ready, 1)
                elif name == "weights":
                    for w, k in late_at[t]:
                        round_w(w, k)

            def attend(t):
                for kind, h, g in attention_order(t):
                    if kind == "between":
                        between(h, g)
                    elif kind == "exp":
                        g = len(chunks_of(t)) - 1
                        wait_drained(act, last_score(t, h))
                        act.activation(probs[h % 2][:, 0:keys_of(t)], probs[h % 2][:, 0:keys_of(t)], ACT.Exp,
                                       bias=low[:, h, g:g + 1], scale=-1.0,
                                       accum_out=den[:, h:h + 1]).then_inc(exped, 1)
                    elif kind == "turn":
                        key = ("turn", h, g, t)
                        n = group_no[t, h, g]
                        wait_filled(act, key)
                        wait_value(act, n - 2)
                        grp = groups_of(t)[g]
                        full = [x for x in grp if x[1] == P]
                        if full:
                            ins = act.copy(pT[n % 2][:, 0:len(full), :],
                                           of(key)[:, 0:len(full) * P].rearrange("p (j n) -> p j n", n=P))
                        if len(full) < len(grp):
                            ins = act.copy(pT[n % 2][0:grp[-1][1], len(full), :],
                                           of(key)[0:grp[-1][1], len(full) * P:(len(full) + 1) * P])
                        ins.then_inc(*drains(key))

            act.wait_ge(const_in, 80)
            act.wait_ge(ones_ready, 1)
            for w in ("iq", "kv"):
                for k in range(KD):
                    round_w(w, k)
                    if (w, k) == ("iq", 1):
                        hi_x("A", 0)
            between("iq", 0)
            square_x(1)
            between("kv", 0)
            for k in range(KD):
                round_w("aq", k)
            between("turn", 0)
            for t in range(TILES):
                for kind, h, c in index_order(t):
                    if kind == "scale":
                        act.wait_ge(x_rstd_ready, t + 1)
                        act.activation(xin[:], xin[:], ACT.Identity, scale=x_rstd[:, 0:1]).then_inc(xn_ready, 1)
                    if kind == "x":
                        hi_x(*x_of(t + 1))
                        key = ("aq", "A", t)
                        wait_filled(act, key)
                        if t:
                            wait_filled(act, ("turn_aq1", "A", t - 1))
                        twice(aq_row[:], of(key)[:], AH).then_inc(*drains(key))
                    if kind != "index":
                        continue
                    a, b = chunks_of(t)[c]
                    key = ("index", h, c, t)
                    wait_filled(act, key)
                    act.activation(of(key)[:, 0:b - a], of(key)[:, 0:b - a], ACT.Relu).then_inc(relued, 1)
                if searched(t):
                    n = keys_of(t)
                    if t == SAMPLE:
                        for c, (a, b) in enumerate(chunks_of(t)):
                            wait_filled(act, ("fold", c))
                            act.copy(idx[:, a:b], of(("fold", c))[:, 0:b - a]).then_inc(*drains(("fold", c)))
                            wait_drained(act, ("fold", c))
                    else:
                        wait_drained(act, last_index(t))
                    no = len([x for x in range(t) if searched(x)])
                    act.activation(work[:, 0:n], idx[:, 0:n], ACT.Identity, accum_out=total).then_inc(index_summed, 1)
                    act.wait_ge(index_summed, 2 * no + 1)
                    act.activation(work[:, 0:n], idx[:, 0:n], ACT.Square, accum_out=squares)\
                       .then_inc(index_summed, 1)
                if t:
                    attend(t - 1)
                else:
                    for name in ("iq", "kv", "turn"):
                        between(name, 1)
                hi_queries("turn_aq", t, aqT_hi)
                if t + 2 <= TILES:
                    square_x(t + 2)
                if t == NT - 1:
                    for half in range(2):
                        hi(("turn_ci", half), kiT_hi[:, half * BW:(half + 1) * BW])
                if t == SAMPLE:
                    for b in range(4):
                        hi(("turn_ck", b), kT[:, b % KVH, b // KVH * BW:(b // KVH + 1) * BW])
                if 2 <= t <= 5:
                    for k in range(2 * t - 4, 2 * t - 2):
                        round_w("rq", k)
            attend(SAMPLE)

            def retained(t):
                key = ("v", "R", t)
                wait_filled(act, key)
                if isinstance(t, int) and t == 0:
                    act.wait_ge(ao_stored, AO_STORES)
                else:
                    wait_filled(act, ("out", "R", t - 1))
                act.copy(rv_row[:].rearrange("p h d -> p (h d)"), of(key)[:]).then_inc(*drains(key))

            def turned(t):
                key = ("turn_q", "R", t)
                wait_filled(act, key)
                act.copy(rqT[:].rearrange("p h d -> p (h d)"), of(key)[:]).then_inc(*drains(key))
                key = ("turn_k", "R", t)
                wait_filled(act, key)
                act.copy(rkT[:].rearrange("p h d -> p (h d)"), of(key)[:]).then_inc(*drains(key))

            def square(t):
                key = ("out", "R", t)
                wait_filled(act, key)
                if not (isinstance(t, int) and t == 0):
                    act.wait_ge(ro_stored, 16 * t)
                for h in range(RH):
                    ins = act.activation(ro[:, h, :], of(key)[:, h * RD:(h + 1) * RD], ACT.Square,
                                         accum_out=group_sq[:, h:h + 1])
                ins.then_inc(squared, 1)

            retained(0)
            hi_x("R", 1)
            turned(0)
            for k in range(4):
                round_w("rg", k)
            square(0)
            retained(1)
            hi_x("R", 2)
            for k in range(4, KD):
                round_w("rg", k)
            with act.Fori(1, NT - 1) as t:
                turned(t)
                square(t)
                retained(t + 1)
                hi_x("R", t + 2)
            turned(NT - 1)
            for k in range(4):
                round_w("ag", k)
            square(NT - 1)
            retained(SAMPLE)
            hi_x("O", 0)
            for k in range(4, KD):
                round_w("ag", k)
            turned(SAMPLE)
            for k in range(4):
                round_w("wo0", k)

            def gates(t):
                for half, name in enumerate(("rg", "ag")):
                    key = (name, "O", t)
                    wait_filled(act, key)
                    if not (isinstance(t, int) and t == 0):
                        act.wait_ge(mixed_ready, 2 * t - 1 + half)
                    act.activation(gate[:, half * BW:(half + 1) * BW], of(key)[:], ACT.Silu)\
                       .then_inc(*drains(key))

            def hi_mixed(t):
                for half in range(2):
                    hi((f"turn{half}", "O", t), mT_hi[:, 4 * half:4 * half + 4, :].rearrange("p k n -> p (k n)"))

            square(SAMPLE)
            gates(0)
            hi_x("O", 1)
            for k in range(4, KD):
                round_w("wo0", k)
            hi_mixed(0)
            for k in range(KD):
                round_w("wo1", k)
            gates(1)
            hi_x("O", 2)
            with act.Fori(1, NT - 1) as t:
                hi_mixed(t)
                gates(t + 1)
                hi_x("O", t + 2)
            hi_mixed(NT - 1)
            gates(SAMPLE)
            wait_filled(act, ("y1", "O", NT - 1))
            hi_mixed(SAMPLE)

        @block.vector
        def _(dve):
            def split_w(w, k):
                i = item_no[w, k]
                dve.wait_ge(w_rounded, split_no[w, k])
                g = ones8 if w.startswith("wo") else g_in
                dve.scalar_tensor_tensor(
                    out=w_lo[SLOT[w]][:, k, 0:WIDTH[w]], in0=raw(i)[:, 0:WIDTH[w]],
                    scalar=g[:, k:k + 1], in1=w_hi[SLOT[w]][:, k, 0:WIDTH[w]].bitcast(F32),
                    op0=ALU.mult, op1=ALU.subtract).then_inc(w_split, 1)

            STAT = 4

            def mean_square(rows, no):
                for half in range(2):
                    ins = dve.bn_stats(stats[:, half, :], rows[:, half * BW:(half + 1) * BW])
                ins.then_inc(stat_done, 1)
                parts = stats[:].rearrange("p a (b c) -> p (a b) c", c=3)
                dve.wait_ge(stat_done, STAT * no + 1)
                dve.tensor_tensor(mean2[:], parts[:, :, 1], parts[:, :, 1], ALU.mult).then_inc(stat_done, 1)
                dve.wait_ge(stat_done, STAT * no + 2)
                dve.scalar_tensor_tensor(out=mean2[:], in0=parts[:, :, 2], scalar=4.0 / D, in1=mean2[:],
                                         op0=ALU.mult, op1=ALU.add).then_inc(stat_done, 1)
                dve.wait_ge(stat_done, STAT * no + 3)
                dve.tensor_reduce(mean_sq[:, 0:1], mean2[:], AX_X, ALU.add).then_inc(stat_done, 1)
                dve.wait_ge(stat_done, STAT * no + 4)
                dve.tensor_scalar(mean_sq[:, 1:2], mean_sq[:, 0:1], 0.25, EPS, ALU.mult, ALU.add)\
                   .then_inc(ms_ready, 1)

            def normalise(phase, t):
                n = NORM[phase] + t
                dve.wait_ge(x_in, 32 * (n + 1))
                mean_square(xin, stat_no(phase, t))
                dve.wait_ge(rstd_ready, power_no(phase, t) + 1)
                dve.tensor_scalar(xin[:], xin[:], rstd[:, 0:1], None, ALU.mult).then_inc(xn_ready, 1)

            def lo(key, hi_index, dst, hi, src=None):
                dve.wait_ge(hi_ready, hi_index)
                dve.tensor_tensor(dst, of(key)[:] if src is None else src, hi.bitcast(F32), ALU.subtract)\
                   .then_inc(*drains(key))

            def lo_below(t, key, half):
                r = slice(HD, P)
                lo(key, hi_no(*key), packed(t, iqT, half, r), packed(t, iqT, half, r), turned_heads(t, key, r))

            def lo_key(g, s, src):
                r = slice(HD * (1 - g), HD * (1 - g) + HD)
                return dve.tensor_tensor(kT[r, g, s], src[r, :], kT[r, g, s].bitcast(F32), ALU.subtract)

            def lo_x(phase, t):
                for half in range(2):
                    s = slice(4 * half, 4 * half + 4)
                    lo((f"x{half}", phase, t), hi_no(f"x{half}", phase, t),
                       xT_lo[:, s, :].rearrange("p k n -> p (k n)"), xT_hi[:, s, :].rearrange("p k n -> p (k n)"))

            steps = [0]

            def step(ins):
                steps[0] += 1
                ins.then_inc(topk_step, 1)
                dve.wait_ge(topk_step, steps[0])

            def add_index(t):
                dve.wait_ge(kv_roped, t + 1)
                for kind, h, c in index_order(t):
                    if kind == "x":
                        lo_x(*x_of(t + 1))
                    if kind != "index":
                        continue
                    a, b = chunks_of(t)[c]
                    key = ("index", h, c, t)
                    dve.wait_ge(relued, index_no[t, h, c])
                    if h == 0:
                        ins = dve.tensor_scalar(idx[:, a:b], of(key)[:, 0:b - a], iw_s[:, 0:1], None, ALU.mult)
                    else:
                        wait_drained(dve, ("index", h - 1, c, t))
                        ins = dve.scalar_tensor_tensor(out=idx[:, a:b], in0=of(key)[:, 0:b - a],
                                                       scalar=iw_s[:, h:h + 1], in1=idx[:, a:b],
                                                       op0=ALU.mult, op1=ALU.add)
                    ins.then_inc(*drains(key))
                wait_drained(dve, last_index(t))

            def counted(t, i):
                return (over, over_was) if i % 2 == 0 else (over_was, over)

            def search(t, i):
                n = keys_of(t)
                no = t - len([x for x in range(TILES) if not searched(x)])
                if i == 0:
                    dve.wait_ge(guessed, no + 1)
                    if t != SAMPLE:
                        step(dve.memset(idx[0:CHUNK, n - CHUNK:n], MASKED))
                now, was = counted(t, i)
                step(dve.tensor_scalar(work[:, 0:n], idx[:, 0:n], above, None, ALU.is_gt, ALU.add, accum_out=seen))
                step(dve.tensor_scalar(now, seen, -AIM, None, ALU.add))
                if i == COUNTS - 1:
                    dve.scalar_tensor_tensor(out=far, in0=now, scalar=now, in1=cst[:, 10:11],
                                             op0=ALU.mult, op1=ALU.is_gt).then_inc(far_ready, 1)
                    return
                step(dve.scalar_tensor_tensor(out=far, in0=now, scalar=now, in1=cst[:, 10:11],
                                              op0=ALU.mult, op1=ALU.is_gt))
                if i:
                    step(dve.tensor_tensor(gap, was, now, ALU.subtract))
                    step(dve.scalar_tensor_tensor(out=gap, in0=gap, scalar=0.0, in1=gap,
                                                  op0=ALU.is_equal, op1=ALU.add))
                    step(dve.reciprocal(gap, gap))
                    step(dve.tensor_tensor(gap, gap, move, ALU.mult))
                    step(dve.scalar_tensor_tensor(out=gap, in0=slope, scalar=0.25, in1=gap,
                                                  op0=ALU.mult, op1=ALU.max))
                    step(dve.scalar_tensor_tensor(out=slope, in0=slope, scalar=4.0, in1=gap,
                                                  op0=ALU.mult, op1=ALU.min))
                step(dve.scalar_tensor_tensor(out=move, in0=now, scalar=slope, in1=far,
                                              op0=ALU.mult, op1=ALU.mult))
                step(dve.tensor_tensor(above, above, move, ALU.add))

            def keep(t):
                n = keys_of(t)
                step(dve.memset(work[:, n:n + 8], TAKEN))
                step(dve.scalar_tensor_tensor(out=work[:, 0:n], in0=work[:, 0:n], scalar=TAKEN, in1=idx[:, 0:n],
                                              op0=ALU.mult, op1=ALU.add))
                step(dve.tensor_scalar(left, seen, -1.0, float(TOPK), ALU.mult, ALU.add))

            def complete(t, i):
                n = keys_of(t)
                step(dve.tensor_scalar(drop8[:], cst[:, 12 + i:20 + i], left, TAKEN, ALU.is_ge, ALU.mult))
                step(dve.max(top8[:], work[:, 0:n]))
                step(dve.tensor_tensor(top8[:], top8[:], drop8[:], ALU.add))
                step(dve.match_replace(work[:, 0:n + 8], top8[:], work[:, 0:n + 8], TAKEN))

            def choose(t):
                n = keys_of(t)
                if not searched(t):
                    step(dve.memset(bias[:, 0:n], 0.0))
                    step(dve.memset(bias[0:CHUNK, n - CHUNK:n], MASKED))
                    return
                dve.wait_ge(any_ready, t - len([x for x in range(TILES) if not searched(x)]) + 1)
                off = dve.value_load(any_far[0:1, :].bitcast(mybir.dt.int32))
                with dve.If(off > 0):
                    dve.sem_clear(whole_step)
                    dve.tensor_copy(work[:, 0:n], idx[:, 0:n]).then_inc(whole_step, 1)
                    dve.wait_ge(whole_step, 1)
                    with dve.Fori(0, TOPK // 8):
                        dve.sem_clear(whole_step)
                        dve.max(top8[:], work[:, 0:n]).then_inc(whole_step, 1)
                        dve.wait_ge(whole_step, 1)
                        dve.match_replace(work[:, 0:n], top8[:], work[:, 0:n], TAKEN).then_inc(whole_step, 1)
                        dve.wait_ge(whole_step, 2)
                step(dve.tensor_scalar(bias[:, 0:n], work[:, 0:n], BETWEEN, MASKED, ALU.is_gt, ALU.mult))

            def between(name, t):
                if name == "turn":
                    for half in range(2):
                        lo_below(t, (f"turn_iq{half}", "A", t), half)
                    key = ("turn_kv", "A", t)
                    s = slice(t * P, t * P + (DEC if t == SAMPLE else P))
                    n = s.stop - s.start
                    dve.wait_ge(hi_ready, hi_no("turn_kv", "A", t))
                    dve.tensor_tensor(kiT_lo[:, s], of(key)[:, 0:n], kiT_hi[:, s].bitcast(F32), ALU.subtract)
                    for g in range(KVH):
                        ins = lo_key(g, s, of(key)[:, (1 + g) * P:(1 + g) * P + n])
                    ins.then_inc(*drains(key))
                elif name == "weights":
                    for w, k in late_at[t]:
                        split_w(w, k)


            def attend(t):
                if t:
                    dve.wait_ge(ao_stored, 16 * t)
                for kind, h, c in attention_order(t):
                    if kind == "between":
                        between(h, c)
                    if kind != "score":
                        continue
                    a, b = chunks_of(t)[c]
                    key = ("score", h, c, t)
                    wait_filled(dve, key)
                    if h >= 2:
                        wait_filled(dve, ("turn", h - 2, len(groups_of(t)) - 1, t))
                    if c:
                        wait_drained(dve, ("score", h, c - 1, t))
                    dve.tensor_tensor_reduce(out=probs[h % 2][:, a:b], in0=of(key)[:, 0:b - a], in1=bias[:, a:b],
                                             scale=-float(HD) ** -0.5, scalar=low[:, h, c - 1:c] if c else 3.0e38,
                                             op0=ALU.add, op1=ALU.min, accum_out=low[:, h, c:c + 1])\
                       .then_inc(*drains(key))
                    if c == len(chunks_of(t)) - 1 and t != SAMPLE and searched(t + 1):
                        if 1 <= h <= COUNTS:
                            search(t + 1, h - 1)
                        if h == COUNTS + 1:
                            keep(t + 1)
                            complete(t + 1, 0)
                        if h == AH - 1:
                            complete(t + 1, 8)
                if t != SAMPLE:
                    choose(t + 1)
                heads = heads_of(t)
                dve.wait_ge(exped, AH * t + heads)
                dve.reciprocal(rden[:, 0:heads], den[:, 0:heads]).then_inc(ao_step, 1)
                dve.wait_ge(ao_step, t + 1)
                key = ("attended", t)
                wait_filled(dve, key)
                dve.tensor_tensor(ao[:, 0:heads * HD].rearrange("p (h d) -> p h d", d=HD),
                                  of(key)[:, 0:heads * HD].rearrange("p (h d) -> p h d", d=HD),
                                  rden[:, 0:heads].unsqueeze(2).broadcast_to([P, heads, HD]), ALU.mult)\
                   .then_inc(*drains(key))

            dve.memset(ones8[:], 1.0).then_inc(ones_ready, 1)
            normalise("A", 0)
            dve.wait_ge(const_in, 80)
            dve.wait_ge(ones_ready, 1)
            for w in ("iq", "kv", "aq"):
                for k in range(KD):
                    split_w(w, k)
                    if (w, k) == ("iq", 1):
                        lo_x("A", 0)
            between("turn", 0)
            for t in range(TILES):
                add_index(t)
                if t:
                    attend(t - 1)
                else:
                    between("turn", 1)
                    choose(0)
                for g in range(KVH):
                    r = slice(HD * g, HD * g + HD)
                    key = (f"turn_aq{g}", "A", t)
                    lo(key, hi_no(*key), packed(t, aqT_lo, 0, r), packed(t, aqT_hi, g, r), turned_heads(t, key, r))
                if t == NT - 1:
                    for half in range(2):
                        s = slice(half * BW, (half + 1) * BW)
                        lo(("turn_ci", half), hi_no(f"ci{half}", "A", t), kiT_lo[:, s], kiT_hi[:, s])
                if t == SAMPLE:
                    for b in range(4):
                        key = ("turn_ck", b)
                        dve.wait_ge(hi_ready, hi_no(f"ck{b}", "A", t))
                        lo_key(b % KVH, slice(b // KVH * BW, (b // KVH + 1) * BW), of(key)).then_inc(*drains(key))
                if 2 <= t <= 5:
                    for k in range(2 * t - 4, 2 * t - 2):
                        split_w("rq", k)
            attend(SAMPLE)

            half = RD // 2

            def rotate(t, name, row, table, ready):
                key = (name, "R", t)
                wait_filled(dve, key)
                sin = rot_r[:, table + 1, :].unsqueeze(1)
                x = of(key)[:].rearrange("p (h a d) -> p h a d", a=2, d=half)
                both = rot_r[:, table, :].unsqueeze(1).broadcast_to([P, 2 * RH, half])
                dve.tensor_tensor(row[:].rearrange("p h (a d) -> p (h a) d", a=2),
                                  of(key)[:].rearrange("p (g d) -> p g d", d=half), both, ALU.mult)
                tm = rtmp[:].rearrange("p h (a d) -> p h a d", a=2)
                ro_ = row[:].rearrange("p h (a d) -> p h a d", a=2)
                for a in range(2):
                    ins = dve.tensor_tensor(tm[:, :, a, :], x[:, :, 1 - a, :], sin.broadcast_to([P, RH, half]), ALU.mult)
                ins.then_inc(*drains(key))
                wait_drained(dve, key)
                dve.tensor_tensor(ro_[:, :, 0, :], ro_[:, :, 0, :], tm[:, :, 0, :], ALU.subtract)
                dve.tensor_tensor(ro_[:, :, 1, :], ro_[:, :, 1, :], tm[:, :, 1, :], ALU.add).then_inc(ready, 1)

            def rotate_q(t):
                dve.wait_ge(rot_in, 16 * (t + 1))
                if not (isinstance(t, int) and t == 0):
                    wait_filled(dve, ("turn_q", "R", t - 1))
                    dve.wait_ge(rk_ready, t)
                rotate(t, "q", rq_row, 0, rq_ready)

            def rotate_k(t):
                if not (isinstance(t, int) and t == 0):
                    wait_filled(dve, ("turn_k", "R", t - 1))
                    dve.wait_ge(kd_ready, t)
                dve.wait_ge(rq_ready, t + 1)
                rotate(t, "k", rk_row, 2, rk_ready)

            def decay_scores(t, table):
                key = ("scores", "R", t)
                wait_filled(dve, key)
                if not (isinstance(t, int) and t == 0):
                    wait_filled(dve, ("out", "R", t - 1))
                dve.tensor_tensor(rsT[:].rearrange("p h d -> p (h d)"), of(key)[:],
                                  table[:].rearrange("p h d -> p (h d)"), ALU.mult).then_inc(*drains(key))

            def retain(t, st, length):
                key = ("kv", "R", t)
                wait_filled(dve, key)
                wait_filled(dve, ("out", "R", t))
                for h in range(RH):
                    ins = dve.scalar_tensor_tensor(out=st[:, h, :], in0=st[:, h, :],
                                                   scalar=float(np.exp(LOG_GAMMA[h] * length)),
                                                   in1=of(key)[:, h * RD:(h + 1) * RD], op0=ALU.mult, op1=ALU.add)
                ins.then_inc(*drains(key))
                key = ("out", "R", t)
                dve.wait_ge(squared, t + 1)
                dve.tensor_scalar(group_sq[:], group_sq[:], 1.0 / RD, EPS, ALU.mult, ALU.add).then_inc(ms_ready, 1)
                dve.wait_ge(rstd_ready, power_no("retained", t) + 1)
                for h in range(RH):
                    ins = dve.scalar_tensor_tensor(out=ro[:, h, :], in0=of(key)[:, h * RD:(h + 1) * RD],
                                                   scalar=rstd[:, h:h + 1], in1=gn_t[:, h * RD:(h + 1) * RD],
                                                   op0=ALU.mult, op1=ALU.mult)
                ins.then_inc(*drains(key))

            def retain_tile(t):
                rotate_q(t + 1)
                decay_scores(t, dec_t)
                normalise("R", t + 2)
                rotate_k(t + 1)
                retain(t, state, P)
                lo_x("R", t + 2)

            normalise("R", 1)
            dve.wait_ge(ao_stored, AO_STORES)
            dve.memset(state[:], 0.0).then_inc(state_zero, 1)
            dve.wait_ge(state_zero, 1)
            rotate_q(0)
            rotate_k(0)
            lo_x("R", 1)
            dve.wait_ge(r_const_in, R_CONSTS)
            rotate_q(1)
            decay_scores(0, dec_t)
            normalise("R", 2)
            for k in range(4):
                split_w("rg", k)
            rotate_k(1)
            retain(0, state, P)
            lo_x("R", 2)
            for k in range(4, KD):
                split_w("rg", k)
            with dve.Fori(1, NT - 1) as t:
                retain_tile(t)
            rotate_q(SAMPLE)
            decay_scores(NT - 1, dec_t)
            normalise("O", 0)
            rotate_k(SAMPLE)
            for k in range(4):
                split_w("ag", k)
            retain(NT - 1, state, P)
            lo_x("O", 0)
            for k in range(4, KD):
                split_w("ag", k)
            decay_scores(SAMPLE, dec_s)
            for k in range(4):
                split_w("wo0", k)
            normalise("O", 1)
            retain(SAMPLE, state_s, DEC)
            lo_x("O", 1)

            def mix(t):
                dve.wait_ge(mix_in, 32 * (t + 1))
                for half_, name in enumerate(("rg", "ag")):
                    s = slice(half_ * BW, (half_ + 1) * BW)
                    wait_drained(dve, (name, "O", t))
                    dve.tensor_tensor(mixed[:, s], mixed[:, s], gate[:, s], ALU.mult).then_inc(mixed_ready, 1)

            def lo_mixed(t):
                for half_ in range(2):
                    s = slice(4 * half_, 4 * half_ + 4)
                    lo((f"turn{half_}", "O", t), hi_no(f"turn{half_}", "O", t),
                       mT_lo[:, s, :].rearrange("p k n -> p (k n)"), mT_hi[:, s, :].rearrange("p k n -> p (k n)"))

            def output(t):
                dve.wait_ge(y_in, 32 * (t + 1))
                for half_ in range(2):
                    s = slice(half_ * BW, (half_ + 1) * BW)
                    key = (f"y{half_}", "O", t)
                    wait_filled(dve, key)
                    dve.tensor_tensor(y_row[:, s], of(key)[:], y_row[:, s], ALU.add).then_inc(*drains(key))
                for half_ in range(2):
                    wait_drained(dve, (f"y{half_}", "O", t))
                mean_square(y_row, stat_no("y", t))
                dve.wait_ge(rstd_ready, power_no("y", t) + 1)
                dve.scalar_tensor_tensor(out=y_row[:], in0=y_row[:], scalar=rstd[:, 0:1], in1=fg_t[:],
                                         op0=ALU.mult, op1=ALU.mult).then_inc(y_ready, 1)

            def out_tile(t):
                lo_mixed(t)
                normalise("O", t + 2)
                mix(t + 1)
                lo_x("O", t + 2)
                output(t)

            dve.wait_ge(fg_in, 16)
            mix(0)
            for k in range(4, KD):
                split_w("wo0", k)
            lo_mixed(0)
            normalise("O", 2)
            for k in range(KD):
                split_w("wo1", k)
            mix(1)
            lo_x("O", 2)
            output(0)
            with dve.Fori(1, NT - 1) as t:
                out_tile(t)
            lo_mixed(NT - 1)
            mix(SAMPLE)
            output(NT - 1)
            lo_mixed(SAMPLE)
            output(SAMPLE)

        @block.gpsimd
        def _(pool):
            def power(no, width):
                pool.wait_ge(ms_ready, no + 1)
                src = mean_sq[:, 1:2] if width == 1 else group_sq[:]
                pool.tensor_tensor(rstd[:, 0:width], src, cst[:, 8:9].broadcast_to([P, width]), ALU.pow)\
                    .then_inc(rstd_ready, 1)

            steps = [0]
            guesses = [0]

            def step(ins):
                steps[0] += 1
                ins.then_inc(rope_step, 1)
                pool.wait_ge(rope_step, steps[0])

            def rotate(rows, heads, t):
                x = rows.rearrange("p h a d -> p (h a) d")
                cos = rope_t[:, t, 0:ROT].unsqueeze(1).broadcast_to([P, heads, ROT])
                a, b = rope_a[:, 0:heads, :], rope_b[:, 0:heads, :]
                h2 = ROT // 2
                pool.tensor_tensor(a, x[:, :, 0:ROT], cos, ALU.mult)
                for s in range(2):
                    sin = rope_t[:, t, ROT + s * h2:ROT + (s + 1) * h2].unsqueeze(1).broadcast_to([P, heads, h2])
                    ins = pool.tensor_tensor(b[:, :, s * h2:(s + 1) * h2], x[:, :, (1 - s) * h2:(2 - s) * h2], sin,
                                             ALU.mult)
                step(ins)
                return pool.tensor_tensor(x[:, :, 0:ROT], a, b, ALU.add)

            pool.wait_ge(const_in, 80)
            def power_x(t):
                pool.wait_ge(x_squared, t)
                step(pool.tensor_scalar(x_sq[:, 1:2], x_sq[:, 0:1], 1.0 / D, EPS, ALU.mult, ALU.add))
                pool.tensor_tensor(x_rstd[:], x_sq[:, 1:2], cst[:, 8:9], ALU.pow).then_inc(x_rstd_ready, 1)

            def rotate_iq(t):
                wait_drained(pool, ("iq", "A", t))
                rotate(q_row[:], 2 * AH, t).then_inc(q_roped, 1)
                pool.wait_ge(q_roped, iq_roped(t))

            def rotate_kv(t):
                pool.wait_ge(rowed, t + 1)
                ins = rotate(kv_row[:], 2 * (1 + KVH), t)
                if t:
                    wait_drained(pool, last_index(t - 1))
                step(ins)
                scale = IH ** -0.5 * HD ** -0.5
                if t == SAMPLE:
                    w = vw_row[:, KVH * HD:].rearrange("p (j a) -> p a j", a=2)
                    for a in range(2):
                        r = slice(a * DEC, (a + 1) * DEC)
                        ins = pool.tensor_scalar(iw_s[r, 0:IH // 2], w[r, a, :], scale, None, ALU.mult)
                else:
                    ins = pool.tensor_scalar(iw_s[:], vw_row[:, KVH * HD:], scale, None, ALU.mult)
                ins.then_inc(kv_roped, 1)
                pool.wait_ge(kv_roped, t + 1)
                outs = (k_out, v_out, i_out) if t != SAMPLE else (ks_out, vs_out, is_out)
                n = P if t != SAMPLE else DEC
                rows = slice(t * P, t * P + n) if t != SAMPLE else slice(0, DEC)
                for dst, src in ((outs[0].rearrange("t (h d) -> t h d", d=HD), kv_row[0:n, 1:, 0, :]),
                                 (outs[1], vw_row[0:n, 0:KVH * HD]), (outs[2], kv_row[0:n, 0, 0, :])):
                    pool.dma_start(dst[rows], src).then_inc(kv_stored, 16)

            def guess(ins):
                guesses[0] += 1
                ins.then_inc(guess_step, 1)
                pool.wait_ge(guess_step, guesses[0])

            def guess_threshold(t, no):
                pool.wait_ge(index_summed, 2 * (no + 1))
                n = keys_of(t)
                guess(pool.tensor_scalar(mean, total, 1.0 / n, None, ALU.mult))
                guess(pool.tensor_scalar(var, squares, 1.0 / n, None, ALU.mult))
                guess(pool.tensor_tensor(dev, mean, mean, ALU.mult))
                guess(pool.tensor_tensor(var, var, dev, ALU.subtract))
                guess(pool.tensor_scalar(var, var, 1e-30, None, ALU.max))
                guess(pool.tensor_tensor(dev, var, cst[:, 9:10], ALU.pow))
                guess(pool.tensor_tensor(slope, dev, cst[:, 29 + 2 * t:30 + 2 * t], ALU.mult))
                guess(pool.tensor_tensor(above, dev, cst[:, 28 + 2 * t:29 + 2 * t], ALU.mult))
                pool.tensor_tensor(above, above, mean, ALU.add).then_inc(guessed, 1)

            def double(what, half, row, free):
                i = item_no[what, half]
                pool.wait_ge(*staged[i])
                wait_filled(pool, free)
                pool.tensor_copy(row[:], raw(i)[:].rearrange("p (b d) -> p b d", d=HD).unsqueeze(2)
                                 .broadcast_to([P, AH, 2, HD])).then_inc(doubled, 1)

            def store_attended(t):
                wait_drained(pool, ("attended", t))
                if t != SAMPLE:
                    pool.dma_start(att_mem[t * P:(t + 1) * P, :], ao).then_inc(ao_stored, 16)
                    return
                for copy in range(2):
                    rows = att_mem[t * P + copy * DEC:t * P + (copy + 1) * DEC, :]
                    for a in range(2):
                        pool.dma_start(rows.rearrange("t (j a d) -> t j a d", a=2, d=HD)[:, :, a, :],
                                       ao[a * DEC:(a + 1) * DEC, 0:AH // 2 * HD].rearrange("p (j d) -> p j d", d=HD))\
                            .then_inc(ao_stored, 16)

            power(power_no("A", 0), 1)
            rotate_iq(0)
            rotate_kv(0)
            power_x(1)
            for t in range(TILES):
                no = len([x for x in range(t) if searched(x)])
                if t == SAMPLE:
                    double("ck", 0, q_row, ("turn_ci", 1))
                wait_drained(pool, ("aq", "A", t))
                rotate(aq_row[:], 2 * AH, t).then_inc(q_roped, 1)
                pool.wait_ge(q_roped, aq_roped(t))
                if searched(t):
                    guess_threshold(t, no)
                if t + 1 < TILES:
                    rotate_iq(t + 1)
                    rotate_kv(t + 1)
                if t == SAMPLE:
                    double("ck", 1, x_heads, ("x1", "R", 0))
                if searched(t):
                    pool.wait_ge(far_ready, no + 1)
                    pool.partition_all_reduce(any_far, far, P, bass.bass_isa.ReduceOp.max).then_inc(any_ready, 1)
                if t == NT - 1:
                    double("ci", 0, q_row, ("turn_iq1", "A", SAMPLE))
                if t:
                    store_attended(t - 1)
                if t + 2 <= TILES:
                    power_x(t + 2)
                if t == SAMPLE:
                    pool.dma_start(v_sb[:, 0:NT, :], vc).then_inc(vcache_in, 16)
            store_attended(SAMPLE)

            pool.wait_ge(ao_stored, AO_STORES)
            for dst, src in ((dec_t, decay), (dec_s, decay_sample), (start_t, from_start)):
                pool.dma_start(dst[:].rearrange("p h n -> p (h n)"), src).then_inc(r_const_in, 16)
            pool.dma_start(gn_t[:], gn_row.broadcast_to([P, BW]))\
                .then_inc(r_const_in, 16)
            pool.dma_start(state_s[:], state_ret[0, 0].rearrange("h d e -> d h e")).then_inc(r_const_in, 16)
            pool.dma_start(fg_t[:], fg_row.broadcast_to([P, D])).then_inc(fg_in, 16)

            def load_angles(t):
                pool.dma_start(rot_r[:].rearrange("p a d -> p (a d)"), rope_ret[bass.ds(t * P, P), :])\
                    .then_inc(rot_in, 16)

            def decay_rows(t, col):
                pool.wait_ge(rk_ready, t + 1)
                if not (isinstance(t, int) and t == 0):
                    wait_filled(pool, ("kv", "R", t - 1))
                pool.tensor_tensor(kd_row[:], rk_row[:], cst[:, col:col + RH].unsqueeze(2).broadcast_to([P, RH, RD]),
                                   ALU.mult).then_inc(kd_ready, 1)

            def decay_queries(t):
                wait_drained(pool, ("turn_q", "R", t))
                if not (isinstance(t, int) and t == 0):
                    wait_filled(pool, ("out", "R", t - 1))
                pool.tensor_tensor(rqdT[:], rqT[:], start_t[:], ALU.mult).then_inc(rqd_ready, 1)

            def store_ro(t):
                wait_drained(pool, ("out", "R", t))
                pool.dma_start(ret_mem[bass.ds(t * P, P), :], ro[:].rearrange("p h d -> p (h d)"))\
                    .then_inc(ro_stored, 16)

            def retain_tile(t):
                decay_queries(t)
                power(power_no("R", t + 2), 1)
                decay_rows(t + 1, 0)
                load_angles(t + 2)
                power(power_no("retained", t), 4)
                store_ro(t)

            load_angles(0)
            power(power_no("R", 1), 1)
            pool.wait_ge(r_const_in, R_CONSTS)
            decay_rows(0, 0)
            load_angles(1)
            retain_tile(0)
            with pool.Fori(1, NT - 1) as t:
                retain_tile(t)
            decay_queries(NT - 1)
            power(power_no("O", 0), 1)
            decay_rows(SAMPLE, 4)
            power(power_no("retained", NT - 1), 4)
            store_ro(NT - 1)
            wait_drained(pool, ("kv", "R", NT - 1))
            pool.dma_start(ret_p[0, 0].rearrange("h d e -> d h e"), state[:]).then_inc(state_stored, 16)
            decay_queries(SAMPLE)

            def load_mix(t):
                rows = bass.ds(t * P, P)
                pool.dma_start(mixed[:, 0:BW], ret_mem[rows, :]).then_inc(mix_in, 16)
                pool.dma_start(mixed[:, BW:D], att_mem[rows, :]).then_inc(mix_in, 16)

            def finish(t, x=True, more=True):
                if more:
                    wait_filled(pool, ("turn1", "O", t))
                    load_mix(t + 1)
                if x:
                    power(power_no("O", t + 2), 1)
                power(power_no("y", t), 1)
                pool.wait_ge(y_ready, t + 1)
                if isinstance(t, int) and t == SAMPLE:
                    pool.dma_start(y_sample[0], y_row[0:DEC, :]).then_inc(y_stored, 16)
                else:
                    pool.dma_start(y_prompt[0, bass.ds(t * P, P), :], y_row[:]).then_inc(y_stored, 16)

            pool.wait_ge(ro_stored, 16 * NT)
            load_mix(0)
            power(power_no("O", 1), 1)
            power(power_no("retained", SAMPLE), 4)
            store_ro(SAMPLE)
            wait_drained(pool, ("kv", "R", SAMPLE))
            pool.dma_start(ret_s[0, 0].rearrange("h d e -> d h e"), state_s[:]).then_inc(state_stored, 16)
            finish(0)
            with pool.Fori(1, NT - 1) as t:
                finish(t)
            pool.wait_ge(ro_stored, 16 * TILES)
            finish(NT - 1, x=False)
            finish(SAMPLE, x=False, more=False)
            pool.wait_ge(y_stored, 16 * TILES)
            pool.wait_ge(state_stored, 32)
            pool.wait_ge(kv_stored, 48 * TILES)


_INS = ["x_prompt", "x_sample", "state_ret", "cache_k", "cache_v", "cache_kidx", "norm_g", "w_in", "ret_gn_g",
        "w_out", "final_g"]
_OUTS = [(1, SEQ, D), (1, DEC, D), (1, 1, RH, RD, RD), (1, 1, SEQ, KVH, HD), (1, 1, SEQ, KVH, HD), (1, 1, SEQ, HD),
         (1, 1, RH, RD, RD), (1, 1, DEC, KVH, HD), (1, 1, DEC, KVH, HD), (1, 1, DEC, HD)]


def kernel(**inputs):
    import concourse.bacc as bacc
    from concourse.bass_utils import run_bass_kernel_spmd

    nc = bacc.Bacc("TRN2", target_bir_lowering=False, num_devices=1)
    arrays, args = {}, []
    given = {n: np.ascontiguousarray(inputs[n]) for n in _INS}
    given["norm_g"] = np.ascontiguousarray(given["norm_g"].reshape(KD, P).T)
    for name, a in {**given, **constants()}.items():
        arrays[f"in_{name}"] = a
        args.append(nc.dram_tensor(f"in_{name}", a.shape, mybir.dt.from_np(a.dtype), kind="ExternalInput").ap())
    for i, shape in enumerate(_OUTS):
        args.append(nc.dram_tensor(f"out_{i}", shape, F32, kind="ExternalOutput").ap())
    hybrid_stream_step(nc, *args)
    r = run_bass_kernel_spmd(nc, [arrays], core_ids=[0])
    return tuple(r.results[0][f"out_{i}"] for i in range(len(_OUTS)))
```
